# Optimizing a Trainium2 kernel written in Bass

```python
import math
import jax, jax.numpy as jnp
from jax import lax
import numpy as np

D_MODEL = 1024
BATCH = 1
SEQ = 512
DEPTH = 1

N_META = 16
BLOCK_Q = 128
RMS_EPS = 1e-6

MLA_HEADS = 16
MLA_Q_RANK = 256
MLA_KV_RANK = 128
MLA_NOPE_DIM = 64
MLA_ROPE_DIM = 32
MLA_V_DIM = 64
MLA_WIDTH = MLA_HEADS * MLA_V_DIM
MLA_SCALE = 1.0 / math.sqrt(MLA_NOPE_DIM + MLA_ROPE_DIM)
ROPE_THETA = 10000.0

FOX_HEADS = 16
FOX_HEAD_DIM = 64
FOX_WIDTH = FOX_HEADS * FOX_HEAD_DIM
FOX_SCALE = 1.0 / math.sqrt(FOX_HEAD_DIM)

IN_SPLITS = (MLA_Q_RANK, MLA_KV_RANK, MLA_ROPE_DIM, MLA_WIDTH,
             FOX_WIDTH, FOX_WIDTH, FOX_WIDTH, FOX_HEADS, FOX_WIDTH,
             D_MODEL, D_MODEL)
IN_WIDTH = sum(IN_SPLITS)


def rmsnorm(x, g):
    xf = x.astype(jnp.float32)
    y = xf * lax.rsqrt(jnp.mean(xf * xf, axis=-1, keepdims=True) + RMS_EPS)
    return (y * g.astype(jnp.float32)).astype(x.dtype)

def rope(x, pos):
    half = x.shape[-1] // 2
    inv_freq = ROPE_THETA ** (-jnp.arange(half, dtype=jnp.float32) / half)
    ang = pos.astype(jnp.float32)[:, None] * inv_freq[None, :]
    cos, sin = jnp.cos(ang), jnp.sin(ang)
    x1 = x[..., :half].astype(jnp.float32)
    x2 = x[..., half:].astype(jnp.float32)
    return jnp.concatenate([x1 * cos - x2 * sin, x1 * sin + x2 * cos], axis=-1).astype(x.dtype)

def causal_block_attention(q, k, v, scale, cum=None):
    B, H, L, _ = q.shape
    n_real = L - N_META
    nb = n_real // BLOCK_Q
    key_pos = jnp.arange(L)

    def attend(qb, qpos, cq=None):
        s = jnp.einsum('bhqd,bhkd->bhqk', qb, k, preferred_element_type=jnp.float32) * scale
        if cq is not None:
            s = s + (cq[..., :, None] - cum[:, :, None, :])
        s = jnp.where(key_pos[None, :] <= qpos[:, None], s, -jnp.inf)
        p = jax.nn.softmax(s, axis=-1)
        return jnp.einsum('bhqk,bhkd->bhqd', p.astype(v.dtype), v)

    out_meta = attend(q[:, :, :N_META], key_pos[:N_META],
                      None if cum is None else cum[:, :, :N_META])

    def to_blocks(a):
        a = a[:, :, N_META:]
        a = a.reshape((B, H, nb, BLOCK_Q) + a.shape[3:])
        return jnp.moveaxis(a, 2, 0)

    xs = (to_blocks(q), key_pos[N_META:].reshape(nb, BLOCK_Q))
    if cum is not None:
        xs = xs + (to_blocks(cum),)
    out_real = lax.map(lambda args: attend(*args), xs)
    out_real = jnp.moveaxis(out_real, 0, 2).reshape(B, H, n_real, v.shape[-1])
    return jnp.concatenate([out_meta, out_real], axis=2)

def first_inputs(seed: int = 0) -> dict:
    key = jax.random.key(seed)
    ks = jax.random.split(key, 13)
    f32 = jnp.float32

    def gain(k, n):
        return 1.0 + 0.1 * jax.random.normal(k, (DEPTH, n), f32)

    def dense(k, fan_in, fan_out):
        return jax.random.normal(k, (DEPTH, fan_in, fan_out), f32) * fan_in ** -0.5

    return {
        'x': jax.random.normal(ks[0], (BATCH, SEQ, D_MODEL), f32),
        'meta_tokens': jax.random.normal(ks[1], (N_META, D_MODEL), f32),
        'pre_norm_g': gain(ks[2], D_MODEL),
        'w_in': dense(ks[3], D_MODEL, IN_WIDTH),
        'fox_forget_b': jax.random.uniform(ks[4], (DEPTH, FOX_HEADS), f32, 1.0, 4.0),
        'mla_q_norm_g': gain(ks[5], MLA_Q_RANK),
        'mla_kv_norm_g': gain(ks[6], MLA_KV_RANK),
        'w_uq': dense(ks[7], MLA_Q_RANK, MLA_HEADS * (MLA_NOPE_DIM + MLA_ROPE_DIM)),
        'w_ukv': dense(ks[8], MLA_KV_RANK, MLA_HEADS * (MLA_NOPE_DIM + MLA_V_DIM)),
        'w_br_mla': dense(ks[9], MLA_WIDTH, D_MODEL),
        'w_br_fox': dense(ks[10], FOX_WIDTH, D_MODEL),
        'w_out': dense(ks[11], D_MODEL, D_MODEL),
        'post_norm_g': gain(ks[12], D_MODEL),
    }

def first_block(x, meta_tokens, pre_norm_g, w_in, fox_forget_b, mla_q_norm_g, mla_kv_norm_g,
              w_uq, w_ukv, w_br_mla, w_br_fox, w_out, post_norm_g):
    B, S, D = x.shape
    L = S + N_META
    pos = jnp.arange(L)
    h = jnp.concatenate([jnp.broadcast_to(meta_tokens[None].astype(x.dtype), (B, N_META, D)), x], axis=1)
    split_idx = np.cumsum(IN_SPLITS)[:-1].tolist()

    def fox_heads(t):
        return t.reshape(B, L, FOX_HEADS, FOX_HEAD_DIM).transpose(0, 2, 1, 3)

    for l in range(DEPTH):
        u = rmsnorm(h, pre_norm_g[l])
        proj = u @ w_in[l]
        (cq, ckv, k_pe_raw, z_mla, fq, fk, fv, f_logit, z_fox, gate_a, gate_b) = jnp.split(proj, split_idx, axis=-1)

        q = (rmsnorm(cq, mla_q_norm_g[l]) @ w_uq[l]).reshape(B, L, MLA_HEADS, MLA_NOPE_DIM + MLA_ROPE_DIM).transpose(0, 2, 1, 3)
        kv = (rmsnorm(ckv, mla_kv_norm_g[l]) @ w_ukv[l]).reshape(B, L, MLA_HEADS, MLA_NOPE_DIM + MLA_V_DIM).transpose(0, 2, 1, 3)
        q_nope, q_pe = q[..., :MLA_NOPE_DIM], q[..., MLA_NOPE_DIM:]
        k_nope, v_mla = kv[..., :MLA_NOPE_DIM], kv[..., MLA_NOPE_DIM:]
        k_pe = rope(k_pe_raw, pos)[:, None]
        q_m = jnp.concatenate([q_nope, rope(q_pe, pos)], axis=-1)
        k_m = jnp.concatenate([k_nope, jnp.broadcast_to(k_pe, (B, MLA_HEADS, L, MLA_ROPE_DIM))], axis=-1)
        o_mla = causal_block_attention(q_m, k_m, v_mla, MLA_SCALE)
        o_mla = o_mla.transpose(0, 2, 1, 3).reshape(B, L, MLA_WIDTH)
        y_mla = (o_mla * jax.nn.silu(z_mla)) @ w_br_mla[l]

        log_f = jax.nn.log_sigmoid((f_logit + fox_forget_b[l]).astype(jnp.float32)).transpose(0, 2, 1)
        cum = jnp.cumsum(log_f, axis=-1)
        o_fox = causal_block_attention(fox_heads(fq), fox_heads(fk), fox_heads(fv), FOX_SCALE, cum)
        o_fox = o_fox.transpose(0, 2, 1, 3).reshape(B, L, FOX_WIDTH)
        y_fox = (o_fox * jax.nn.silu(z_fox)) @ w_br_fox[l]

        mixed = (jax.nn.sigmoid(gate_a) * y_mla + jax.nn.sigmoid(gate_b) * y_fox) @ w_out[l]
        h = h + rmsnorm(mixed, post_norm_g[l])

    return h[:, N_META:]


DEPTH_2 = 2

EPS = 1e-6
CONV_WIDTH = 3
A_HEADS = 8
A_HEAD_DIM = 64
A_WIDTH = A_HEADS * A_HEAD_DIM
POOL_WINDOWS = (2, 4, 8, 16)
B_GROUPS = len(POOL_WINDOWS)
B_GROUP_DIM = 128
B_WIDTH = B_GROUPS * B_GROUP_DIM
EVEN_IN = 3 * A_WIDTH + B_WIDTH
EVEN_MIX = A_WIDTH + B_WIDTH
CHUNK = 128
C_HEADS = 8
C_HEAD_DIM = 128
C_WIDTH = C_HEADS * C_HEAD_DIM
D_FF = 2816

N_EVEN = (DEPTH_2 + 1) // 2
N_ODD = DEPTH_2 // 2


def rms_norm(x, g):
    x32 = x.astype(jnp.float32)
    y = x32 * lax.rsqrt(jnp.mean(x32 * x32, axis=-1, keepdims=True) + EPS)
    return y.astype(x.dtype) * g

def causal_dwconv3(x, w):
    s = x.shape[1]
    xp = jnp.pad(x, ((0, 0), (CONV_WIDTH - 1, 0), (0, 0)))
    y = xp[:, 0:s] * w[0]
    for k in range(1, CONV_WIDTH):
        y = y + xp[:, k:k + s] * w[k]
    return y

def short_gated_conv(gate_b, gate_c, val, conv_w):
    return gate_b * causal_dwconv3(gate_c * val, conv_w)

def multiscale_pool(z, w_pool, pool_scale):
    b, s, _ = z.shape
    z32 = z.astype(jnp.float32).reshape(b, s, B_GROUPS, B_GROUP_DIM)
    cs = jnp.cumsum(z32, axis=1)
    pos = jnp.arange(1, s + 1, dtype=jnp.float32)[None, :, None]
    outs = []
    for g, w in enumerate(POOL_WINDOWS):
        csg = cs[:, :, g]
        shifted = jnp.pad(csg, ((0, 0), (w, 0), (0, 0)))[:, :s]
        count = jnp.minimum(pos, jnp.float32(w))
        outs.append((csg - shifted) / count - z32[:, :, g])
    pooled = jnp.stack(outs, axis=2).astype(z.dtype)
    mixed = jnp.einsum('bsgc,gcd->bsgd', pooled, w_pool)
    return mixed.reshape(b, s, B_WIDTH) * pool_scale

def chunked_spatial_gating(u, v, sgu_norm, w_spatial, b_spatial):
    b, s, _ = u.shape
    n = s // CHUNK
    vn = rms_norm(v, sgu_norm).reshape(b, n, CHUNK, C_HEADS, C_HEAD_DIM)
    mask = jnp.tril(jnp.ones((CHUNK, CHUNK), dtype=w_spatial.dtype))
    ws = w_spatial * mask
    gate = jnp.einsum('hts,bnshc->bnthc', ws, vn) + b_spatial.T[None, None, :, :, None]
    return u * gate.reshape(b, s, C_WIDTH)

def gated_conv_ffn(x, w_gate, w_up, conv_w, conv_b, w_down):
    g = jnp.einsum('bsd,df->bsf', x, w_gate)
    g = causal_dwconv3(g, conv_w) + conv_b
    up = jnp.einsum('bsd,df->bsf', x, w_up)
    return jnp.einsum('bsf,fd->bsd', jax.nn.silu(g) * up, w_down)

def second_inputs(seed: int = 0) -> dict:
    key = jax.random.key(seed)
    ks = jax.random.split(key, 20)
    f32 = jnp.float32
    nrm = lambda k, shape, s: jax.random.normal(k, shape, f32) * s
    return {
        "x": nrm(ks[0], (BATCH, SEQ, D_MODEL), 1.0),
        "norm_mix": 1.0 + nrm(ks[1], (DEPTH_2, D_MODEL), 0.05),
        "norm_ffn": 1.0 + nrm(ks[2], (DEPTH_2, D_MODEL), 0.05),
        "final_norm": 1.0 + nrm(ks[3], (D_MODEL,), 0.05),
        "w_in_even": nrm(ks[4], (N_EVEN, D_MODEL, EVEN_IN), D_MODEL ** -0.5),
        "conv_a": nrm(ks[5], (N_EVEN, CONV_WIDTH, A_WIDTH), CONV_WIDTH ** -0.5),
        "w_pool": nrm(ks[6], (N_EVEN, B_GROUPS, B_GROUP_DIM, B_GROUP_DIM), B_GROUP_DIM ** -0.5),
        "pool_scale": 1.0 + nrm(ks[7], (N_EVEN, B_WIDTH), 0.1),
        "w_out_even": nrm(ks[8], (N_EVEN, EVEN_MIX, D_MODEL), EVEN_MIX ** -0.5),
        "w_in_odd": nrm(ks[9], (N_ODD, D_MODEL, 2 * C_WIDTH), D_MODEL ** -0.5),
        "sgu_norm": 1.0 + nrm(ks[10], (N_ODD, C_WIDTH), 0.05),
        "w_spatial": nrm(ks[11], (N_ODD, C_HEADS, CHUNK, CHUNK), CHUNK ** -0.5),
        "b_spatial": 1.0 + nrm(ks[12], (N_ODD, C_HEADS, CHUNK), 0.05),
        "w_out_odd": nrm(ks[13], (N_ODD, C_WIDTH, D_MODEL), C_WIDTH ** -0.5),
        "w_ffn_gate": nrm(ks[14], (DEPTH_2, D_MODEL, D_FF), D_MODEL ** -0.5),
        "w_ffn_up": nrm(ks[15], (DEPTH_2, D_MODEL, D_FF), D_MODEL ** -0.5),
        "conv_ffn": nrm(ks[16], (DEPTH_2, CONV_WIDTH, D_FF), CONV_WIDTH ** -0.5),
        "b_conv_ffn": nrm(ks[17], (DEPTH_2, D_FF), 0.02),
        "w_ffn_down": nrm(ks[18], (DEPTH_2, D_FF, D_MODEL), D_FF ** -0.5),
    }

def second_block(x, norm_mix, norm_ffn, final_norm, w_in_even, conv_a, w_pool, pool_scale,
              w_out_even, w_in_odd, sgu_norm, w_spatial, b_spatial, w_out_odd,
              w_ffn_gate, w_ffn_up, conv_ffn, b_conv_ffn, w_ffn_down):
    h = x
    for layer in range(DEPTH_2):
        xn = rms_norm(h, norm_mix[layer])
        if layer % 2 == 0:
            i = layer // 2
            proj = jnp.einsum('bsd,de->bse', xn, w_in_even[i])
            a_b = proj[..., 0:A_WIDTH]
            a_c = proj[..., A_WIDTH:2 * A_WIDTH]
            a_v = proj[..., 2 * A_WIDTH:3 * A_WIDTH]
            z_b = proj[..., 3 * A_WIDTH:]
            y_a = short_gated_conv(a_b, a_c, a_v, conv_a[i])
            y_b = multiscale_pool(z_b, w_pool[i], pool_scale[i])
            mix = jnp.concatenate([y_a, y_b], axis=-1)
            h = h + jnp.einsum('bse,ed->bsd', mix, w_out_even[i])
        else:
            i = layer // 2
            proj = jax.nn.gelu(jnp.einsum('bsd,de->bse', xn, w_in_odd[i]), approximate=False)
            u = proj[..., :C_WIDTH]
            v = proj[..., C_WIDTH:]
            mix = chunked_spatial_gating(u, v, sgu_norm[i], w_spatial[i], b_spatial[i])
            h = h + jnp.einsum('bse,ed->bsd', mix, w_out_odd[i])
        hn = rms_norm(h, norm_ffn[layer])
        h = h + gated_conv_ffn(hn, w_ffn_gate[layer], w_ffn_up[layer], conv_ffn[layer],
                               b_conv_ffn[layer], w_ffn_down[layer])
    return rms_norm(h, final_norm)


def setup_inputs(seed=0):
    out = dict(first_inputs(seed))
    for name, value in second_inputs(seed + 1).items():
        if name != "x":
            out[name + "_2"] = value
    return out


def reference(
    x, meta_tokens, pre_norm_g, w_in, fox_forget_b, mla_q_norm_g, mla_kv_norm_g, w_uq, w_ukv,
    w_br_mla, w_br_fox, w_out, post_norm_g, norm_mix_2, norm_ffn_2, final_norm_2, w_in_even_2,
    conv_a_2, w_pool_2, pool_scale_2, w_out_even_2, w_in_odd_2, sgu_norm_2, w_spatial_2,
    b_spatial_2, w_out_odd_2, w_ffn_gate_2, w_ffn_up_2, conv_ffn_2, b_conv_ffn_2, w_ffn_down_2,
):
    x = first_block(
        x, meta_tokens, pre_norm_g, w_in, fox_forget_b, mla_q_norm_g, mla_kv_norm_g, w_uq,
        w_ukv, w_br_mla, w_br_fox, w_out, post_norm_g,
    )
    return second_block(
        x, norm_mix_2, norm_ffn_2, final_norm_2, w_in_even_2, conv_a_2, w_pool_2, pool_scale_2,
        w_out_even_2, w_in_odd_2, sgu_norm_2, w_spatial_2, b_spatial_2, w_out_odd_2,
        w_ffn_gate_2, w_ffn_up_2, conv_ffn_2, b_conv_ffn_2, w_ffn_down_2,
    )


_drawn_inputs = setup_inputs


def setup_inputs(seed=0):
    import zlib

    import numpy as np

    out = dict(_drawn_inputs(seed))
    spreads = {}
    factors = {'sgu_norm_2': 4.754, 'b_spatial_2': 3.314, 'b_conv_ffn_2': 6.063}
    for name, (base, spread) in spreads.items():
        noise = np.random.default_rng([zlib.crc32(name.encode()), seed]).standard_normal(out[name].shape)
        drawn = base * np.exp(spread * noise) if base else spread * noise
        out[name] = __import__('jax').numpy.asarray(drawn.astype(out[name].dtype))
    for name, factor in factors.items():
        out[name] = (out[name] * factor).astype(out[name].dtype)
    return out
```

```python
from contextlib import ExitStack
import math

import numpy as np

import concourse.bass as bass
from concourse import mybir

F32 = mybir.dt.float32
F32R = mybir.dt.float32r
ACT = mybir.ActivationFunctionType
ALU = mybir.AluOpType
AX = mybir.AxisListType

P = 128
D = 1024
KT = D // P
SEQ = 512
META = 16
LEN = SEQ + META
NQ = SEQ // P
EPS = 1e-6
HEADS = 16
PAIRS = HEADS // 2
STEPS = 2 * PAIRS
NOPE, ROPE = 64, 32
HD = 64
Q_RANK, KV_RANK = 256, 128
MLA_SCALE = 1.0 / math.sqrt(NOPE + ROPE)
FOX_SCALE = 1.0 / math.sqrt(HD)
ROPE_THETA = 10000.0
MASKED = -1e30
W_CQ = 0
W_CKV = W_CQ + Q_RANK
W_KPE = W_CKV + KV_RANK
W_ZM = W_KPE + ROPE
W_FQ = W_ZM + D
W_FK = W_FQ + D
W_FV = W_FK + D
W_F = W_FV + D
W_ZF = W_F + HEADS
W_GA = W_ZF + D
W_GB = W_GA + D
GROUPS = 4
DFF = 2816
FT = DFF // P
DOWN = (8, 8, 6)
C_HEADS = 8
UNIT = KT * P
VEC_ROWS = (("pre_g", 8), ("q_g", 2), ("kv_g", 1), ("post_g", 8), ("mix_g", 16), ("ffn_g", 16),
            ("pool_scale", 4), ("sgu_g", 8), ("conv_a", 12))
FFN_ROWS = 4 * FT

B_S, B_T, B_O, B_META = 4, 6, 7, 3


def vec_column(name, k=0):
    at = 0
    for n, rows in VEC_ROWS:
        if n == name:
            return at + k
        at += rows
    raise KeyError(name)


N_VEC = sum(r for _, r in VEC_ROWS)


def plan_units():
    kinds, first = [], {}

    def phase(name, *ks):
        first[name] = len(kinds)
        kinds.extend(ks)

    phase("pro", "full", "kpe", "full", "full", "full")
    for s in range(STEPS):
        phase(("attn", s), *(("full", "qkv") if s < PAIRS else ("full",) * 4))
    phase("mix", *("full",) * (4 * KT))
    phase("out", *("full",) * KT)
    phase("even", *("full",) * (4 * GROUPS))
    phase("pool", "pool")
    phase("even_out", *("full",) * KT)
    phase(("ffn", 0), *("full",) * (2 * FT))
    phase(("down", 0), *("full", "full", "six") * KT)
    phase("odd_v", *("full",) * KT)
    phase("odd_u", *("full",) * KT)
    phase("odd_out", *("full",) * KT)
    phase(("ffn", 1), *("full",) * (2 * FT))
    phase(("down", 1), *("full", "full", "six") * KT)
    return kinds, first


KINDS, FIRST = plan_units()


def hybrid_blocks_kernel(nc, a, rope_t, consts, out):
    forget_dram = nc.dram_tensor("forget_rows", [2, HEADS, 2, LEN], F32, kind="Internal").ap()

    with ExitStack() as ctx:
        def sb(name, shape, dt=F32):
            return ctx.enter_context(nc.sbuf_tensor(name, shape, dt))

        sems = {}

        def sem(name):
            if name not in sems:
                sems[name] = ctx.enter_context(nc.semaphore(name))
            return sems[name]

        ps = ctx.enter_context(nc.psum_tensor("ps", [P, 8 * 512], F32))

        def bank(b, lo=0, hi=512, rows=slice(0, P)):
            return ps[rows, b * 512 + lo:b * 512 + hi]

        raw = sb("w_raw", [P, 2, UNIT])
        wsp = sb("w_split", [P, 2, 2, UNIT], F32R)
        u = sb("u", [P, KT, 2, LEN], F32R)
        ra = sb("arena_r", [P, FT * 2 * SEQ], F32R)
        big = sb("big", [P, 16, SEQ])
        tmp = sb("tmp", [P, 5120])
        cst = sb("cst", [P, 400])
        ident_r = sb("ident_r", [P, P], F32R)
        mask_r = sb("mask_r", [P, P], F32R)
        ones = sb("ones", [P, P])
        vec = sb("vec", [P, N_VEC + 2 * FFN_ROWS])
        st = sb("stats", [P, 64])
        ident = cst[:, 0:128]
        triu = cst[:, 256:384]
        inv_count = cst[:, 384:400]

        def view(t, at, *dims):
            n = math.prod(dims)
            v = t[:, at:at + n]
            if len(dims) == 2:
                v = v.rearrange("p (a b) -> p a b", a=dims[0])
            elif len(dims) == 3:
                v = v.rearrange("p (a b c) -> p a b c", a=dims[0], b=dims[1])
            elif len(dims) == 4:
                v = v.rearrange("p (a b c d) -> p a b c d", a=dims[0], b=dims[1], c=dims[2])
            return v, at + n

        q_t, at = view(ra, 0, 2, 2, SEQ)
        k_t, at = view(ra, at, 2, 2, LEN)
        v_t, at = view(ra, at, 2, NQ, 2, P)
        v_m, at = view(ra, at, 2, P)
        p_t, at = view(ra, at, 2, 2 * NQ, SEQ)
        p_m, at = view(ra, at, 2, SEQ)
        cq_r, at = view(ra, at, 2, 2, SEQ)
        ckv_r, at = view(ra, at, 2, LEN)
        o_r, _ = view(ra, 0, 16, 2, SEQ)
        mix_r, at = view(ra, 0, KT, 2, SEQ)
        pool_r, _ = view(ra, at, GROUPS, 2, SEQ)
        vs_r, at = view(ra, at, NQ, 2, D)
        ws_r, _ = view(ra, at, 2, 2, D)
        a_r, _ = view(ra, 0, FT, 2, SEQ)

        prob, at = view(tmp, 0, 2, LEN)
        rot, at = view(tmp, at, 2, SEQ)
        rt1, at = view(tmp, at, 1, SEQ)
        rt2, at = view(tmp, at, 1, SEQ)
        prob_m, at = view(tmp, at, NQ, P)
        rope_s, at = view(tmp, at, 2, LEN)
        rbc, at = view(tmp, 0, 1, SEQ)
        acc, at = view(tmp, at, 1, SEQ)
        sq, at = view(tmp, at, 2, SEQ)
        rest = at
        xin, _ = view(tmp, rest, 2, D)
        res_t, _ = view(tmp, rest + 2048, 2, SEQ)
        gfin, _ = view(tmp, rest + 2048, 1, D)
        sig, _ = view(tmp, rest, 4, SEQ)
        gpad, at = view(tmp, rest - 0, 2, 516)
        cnv, at = view(tmp, at, 2, SEQ)
        hid, at = view(tmp, at, 1, SEQ)
        cpad, at = view(tmp, rest, 1, 516)
        ecv, at = view(tmp, at, 1, SEQ)
        zpad, at = view(tmp, at, 2, 8 + SEQ)
        zf, at = view(tmp, at, 1, SEQ)
        wst, at = view(tmp, rest, 1, D)
        bbc, at = view(tmp, at, 1, D)
        odt, at = view(tmp, at, 2, SEQ)
        h = big[:, 0:KT, :]
        m2 = big[:, KT:16, :]

        ssx, rsx = st[:, 0:5], st[:, 5:10]
        mx, neg, rs, ri = (st[:, 10 + 8 * j:18 + 8 * j] for j in range(4))
        rtok, sstok = st[:, 42:46], st[:, 46:50]
        ssv, rsv = st[:, 50:54], st[:, 54:58]
        sd = st[:, 58:63]

        HI, LO = 0, 1
        PASSES = ((HI, HI), (HI, LO), (LO, HI))

        def vcol(name, k=0):
            c = vec_column(name) + k
            return vec[:, c:c + 1] if isinstance(k, int) else vec[:, bass.ds(c, 1)]

        def ffn_vec(layer, row, f):
            c = N_VEC + layer * FFN_ROWS + row * FT + f
            return vec[:, c:c + 1] if isinstance(f, int) else vec[:, bass.ds(c, 1)]

        def idx(i):
            return i if isinstance(i, int) else bass.ds(i, 1)

        def flat(ap, i):
            if isinstance(i, int):
                return ap
            return ap

        def loop(eng, n, body):
            body(0, True, n == 1)
            if n > 3:
                with eng.Fori(1, n - 1) as i:
                    body(i, False, False)
            elif n == 3:
                body(1, False, False)
            if n > 1:
                body(n - 1, False, True)

        def num(c, i=0, k=0):
            return c + i * k if k else c

        def w_load(sp, c, parts, i=0, k=0):
            if c >= 2 or k:
                sp.wait_ge(sem("w_lo"), num(c, i, k) - 1)
            for dst, src in parts:
                sp.dma_start(dst(raw[:, c % 2, :]), src).then_inc(sem(f"w_load{c % 2}"), 16)

        def split_pairs(kind, r, s):
            if kind == "full":
                return [(r[:, 0:UNIT], s[:, 0:UNIT])]
            if kind == "six":
                return [(r[:, 0:6 * P], s[:, 0:6 * P])]
            if kind == "pool":
                return [(r[:, 0:4 * P], s[:, 0:4 * P])]
            if kind == "kpe":
                r3, s3 = (x[:, 0:UNIT].rearrange("p (k n) -> p k n", k=KT) for x in (r, s))
                return [(r3[:, :, 0:32], s3[:, :, 0:32]), (r3[:, :, 16:32], s3[:, :, 32:48]),
                        (r3[:, :, 0:16], s3[:, :, 48:64]), (r3[:, :, 64:128], s3[:, :, 64:128])]
            rq = r[:, 0:384].rearrange("p (g n) -> p g n", g=4)
            sq_ = s[:, 0:512].rearrange("p (g n) -> p g n", g=4)
            rk = r[:, 384:640].rearrange("p (h t d) -> p t h d", h=2, t=2)
            sk = s[:, 512:768].rearrange("p (t h d) -> p t h d", h=2, t=2)
            return [(rq[:, :, 0:96], sq_[:, :, 0:96]), (rq[:, :, 80:96], sq_[:, :, 96:112]),
                    (rq[:, :, 64:80], sq_[:, :, 112:128]),
                    (rk[:, 0], sk[:, 0]), (rk[:, 1], sk[:, 1])]

        def w_hi(act, c, i=0, k=0, kind=None):
            if c >= len(KINDS):
                return
            kind = kind or KINDS[c]
            half = k // 2
            act.wait_ge(sem(f"w_load{c % 2}"), 32 * (c // 2 + 1) + (i * (32 * half) if k else 0))
            if c >= 2:
                act.wait_ge(sem("w_used"), num(c, i, k) - 1)
            pieces = split_pairs(kind, raw[:, c % 2, :], wsp[:, c % 2, HI, :])
            for n, (src, dst) in enumerate(pieces):
                ins = act.copy(dst, src)
            ins.then_inc(sem("w_hi"), 1)

        def w_lo(dve, c, i=0, k=0, kind=None):
            if c >= len(KINDS):
                return
            kind = kind or KINDS[c]
            dve.wait_ge(sem("w_hi"), num(c, i, k) + 1)
            src = split_pairs(kind, raw[:, c % 2, :], wsp[:, c % 2, HI, :])
            dst = split_pairs(kind, raw[:, c % 2, :], wsp[:, c % 2, LO, :])
            for (r, hi), (_, lo) in zip(src, dst):
                ins = dve.tensor_tensor(lo, r, hi, ALU.subtract)
            ins.then_inc(sem("w_lo"), 1)

        def w_ready(pe, c, i=0, k=0):
            pe.wait_ge(sem("w_lo"), num(c, i, k) + 1)

        def w_tile(c, part, k, width=P):
            return wsp[:, c % 2, part, k * P:k * P + width]

        def panel(dram, col, rows=KT, row0=0):
            halves = [(rows // 2, rows), (0, rows // 2)]
            out_ = []
            for lo, hi in halves:
                src = dram[(row0 + lo) * P:(row0 + hi) * P, bass.ds(col, P)] if not isinstance(col, int) \
                    else dram[(row0 + lo) * P:(row0 + hi) * P, col:col + P]
                out_.append((lambda r, lo=lo, hi=hi: r[:, lo * P:hi * P].rearrange("p (k n) -> p k n", k=hi - lo),
                             src.rearrange("(k p) n -> p k n", p=P)))
            return out_

        def product(pe, out_ap, c, moving, ks=range(KT), start=True, stop=True, n0=0):
            last = None
            total = [(k, ws, ms) for k in ks for ws, ms in PASSES]
            for n, (k, ws, ms) in enumerate(total):
                last = pe.matmul(out_ap, w_tile(c, ws, k - n0), moving(k, ms),
                                 start=start and n == 0, stop=stop and n == len(total) - 1,
                                 skip_group_check=True)
            return last

        def u_real(k, part):
            return u[:, k, part, META:LEN]

        def u_meta(k, part):
            return u[:, k, part, 0:META]

        PRO = FIRST["pro"]
        nat = big.rearrange("p a b -> p (a b)")[:, 0:5 * D].rearrange("p (t d) -> p t d", t=5)
        junk = big.rearrange("p a b -> p (a b)")[:, 5 * D:6 * D]
        stage = tmp[:, 0:3 * P].rearrange("p (s n) -> p s n", s=3)
        w_in = a["w_in"][0]
        lf = big[0:16, 12, :].rearrange("p n -> p n")
        bigf = big.rearrange("p a b -> p (a b)")
        pf = [bigf[:, 6 * D + j * 528:6 * D + (j + 1) * 528] for j in range(3)]
        fx, fe, fm = (t[0:HEADS, :] for t in pf)
        forget_r = ra[0:HEADS, 0:4 * LEN].rearrange("p (s j n) -> p s j n", s=2, j=2)
        kp1 = rt1[64:96, 0, :]
        ksq = bigf[:, 0:3 * LEN].rearrange("p (t n) -> p t n", t=3)
        krs = bigf[:, 3 * LEN:5 * LEN].rearrange("p (t n) -> p t n", t=2)
        kn = bigf[:, 5 * LEN:6 * LEN]
        kro = bigf[:, 6 * LEN:9 * LEN].rearrange("p (t n) -> p t n", t=3)
        fbias = st[0:HEADS, 63:64]

        def dma_prologue(sp):
            for t in range(NQ):
                sp.dma_start(nat[:, t, :], a["x"][0, t * P:(t + 1) * P, :]).then_inc(sem("x_in"), 16)
                if t == 0:
                    sp.dma_start(nat[0:META, 4, :], a["meta_tokens"]).then_inc(sem("x_in"), 16)
                    sp.dma_start(cst[:], consts).then_inc(sem("cst_in"), 16)
            rows = 0
            for name, n in VEC_ROWS:
                src = {"pre_g": a["pre_norm_g"], "q_g": a["mla_q_norm_g"], "kv_g": a["mla_kv_norm_g"],
                       "post_g": a["post_norm_g"], "mix_g": a["norm_mix_2"], "ffn_g": a["norm_ffn_2"],
                       "pool_scale": a["pool_scale_2"], "sgu_g": a["sgu_norm_2"],
                       "conv_a": a["conv_a_2"][0]}[name]
                sp.dma_start(stage[rows:rows + n, 0, :], src.rearrange("a (k p) -> (a k) p", p=P)) \
                    .then_inc(sem("vec_in"), 16)
                rows += n
            for layer in range(2):
                sp.dma_start(stage[0:3 * FT, 1 + layer, :],
                             a["conv_ffn_2"][layer].rearrange("a (k p) -> (a k) p", p=P)).then_inc(sem("vec_in"), 16)
                sp.dma_start(stage[3 * FT:4 * FT, 1 + layer, :],
                             a["b_conv_ffn_2"][layer:layer + 1].rearrange("a (k p) -> (a k) p", p=P)) \
                    .then_inc(sem("vec_in"), 16)
            sp.dma_start(fbias, a["fox_forget_b"].rearrange("a h -> h a"), allow_slow_non_contiguous=True) \
                .then_inc(sem("rope_in"), 16)
            sp.dma_start(rope_s[64:96, :, :], rope_t.rearrange("(s p) n -> p s n", s=2)).then_inc(sem("rope_in"), 16)

        N_VEC_DMA = 16 * (len(VEC_ROWS) + 4)

        def load_prologue(sp):
            for j, col in enumerate((W_F, W_KPE, W_CKV, W_CQ, W_CQ + P)):
                w_load(sp, PRO + j, panel(w_in, col))
            sp.wait_ge(sem("forget_lo"), 2)
            for s in range(2):
                sp.dma_start(forget_dram[s], forget_r[:, s].bitcast(F32)).then_inc(sem("forget_out"), 16)

        def act_prologue(act):
            act.wait_ge(sem("x_in"), 16 * 5)
            for t in range(5):
                n = P if t < 4 else META
                if t:
                    act.wait_ge(sem("x_ss"), t)
                act.activation(junk[0:n, :], nat[0:n, t, :], ACT.Square, accum_out=ssx[0:n, t:t + 1]) \
                    .then_inc(sem("x_ss"), 1)
            act.wait_ge(sem("cst_in"), 16)
            act.copy(ident_r[:], ident).then_inc(sem("cst_r"), 1)
            act.copy(mask_r[:], cst[:, 128:256]).then_inc(sem("cst_r"), 1)
            w_hi(act, PRO)
            w_hi(act, PRO + 1)
            act.wait_ge(sem("x_ms"), 2)
            act.activation(sd[:, 0:4], ssx[:, 0:4], ACT.Sqrt).then_inc(sem("x_sd"), 1)
            act.activation(sd[0:META, 4:5], ssx[0:META, 4:5], ACT.Sqrt).then_inc(sem("x_sd"), 1)
            for k in range(KT):
                act.wait_ge(sem("x_tr"), k + 1)
                if k == 0:
                    act.wait_ge(sem("vec"), 1)
                b = 2 * (k % 2)
                act.activation(u[:, k, HI, META:LEN], bank(b), ACT.Copy, scale=vcol("pre_g", k))
                act.activation(u[:, k, HI, 0:META], bank(b + 1, 0, META), ACT.Copy, scale=vcol("pre_g", k)) \
                    .then_inc(sem("u_hi"), 1)
            w_hi(act, PRO + 2)
            w_hi(act, PRO + 3)
            act.wait_ge(sem("f_x"), 1)
            act.activation(fe, fx, ACT.Abs).then_inc(sem("f_act"), 1)
            act.wait_ge(sem("f_act"), 1)
            act.activation(fe, fe, ACT.Exp, scale=-1.0).then_inc(sem("f_act"), 1)
            act.wait_ge(sem("f_act"), 2)
            act.activation(fe, fe, ACT.Ln, bias=1.0).then_inc(sem("f_act"), 1)
            for s in range(2):
                act.wait_ge(sem("f_cum"), s + 1)
                act.copy(forget_r[:, s, HI, :], (fm, fe)[s]).then_inc(sem("forget_hi"), 1)
            act.wait_ge(sem("kpe_rot"), 1)
            act.copy(k_t[64:96, 0, HI, :], kro[64:96, 2, :])
            act.copy(k_t[64:96, 1, HI, :], kro[64:96, 2, :]).then_inc(sem("kpe_hi"), 1)
            act.wait_ge(sem("w_used"), PRO + 3)
            act.wait_ge(sem("pro_meta"), 1)
            act.activation(ksq[:, 0, META:LEN], bank(2), ACT.Square)
            act.activation(ksq[:, 0, 0:META], bank(7, 32, 48), ACT.Square).then_inc(sem("c_sq"), 1)
            w_hi(act, PRO + 4)
            act.wait_ge(sem("c_sum"), 1)
            act.activation(krs[:, 0, META:LEN], bank(5), ACT.Sqrt, scale=1.0 / KV_RANK, bias=EPS)
            act.activation(krs[:, 0, 0:META], bank(6, 0, META), ACT.Sqrt, scale=1.0 / KV_RANK, bias=EPS) \
                .then_inc(sem("c_sd"), 1)
            act.wait_ge(sem("c_n"), 1)
            act.copy(ckv_r[:, HI, :], kn).then_inc(sem("c_hi"), 1)
            w_hi(act, PRO + 5)
            for t in range(2):
                act.wait_ge(sem("w_used"), PRO + 4 + t)
                act.activation(ksq[:, 1 + t, 0:SEQ], bank(3 + t), ACT.Square).then_inc(sem("c_sq"), 1)
            act.wait_ge(sem("c_sum"), 2)
            act.activation(krs[:, 1, 0:SEQ], bank(5), ACT.Sqrt, scale=1.0 / Q_RANK, bias=EPS).then_inc(sem("c_sd"), 1)
            for t in range(2):
                act.wait_ge(sem("c_n"), 2 + t)
                act.copy(cq_r[:, t, HI, :], kn[:, 0:SEQ]).then_inc(sem("c_hi"), 1)

        def pool_prologue(pool):
            pool.memset(ones[:], 1.0).then_inc(sem("ones"), 1)
            pool.memset(v_t.bitcast(F32), 0.0)
            pool.memset(v_m.bitcast(F32), 0.0).then_inc(sem("pads"), 1)
            pool.wait_ge(sem("vec"), 1)
            pool.memset(prob_m, 0.0).then_inc(sem("pads"), 1)

        def dve_prologue(dve):
            dve.wait_ge(sem("x_ss"), 5)
            for n, (rows, lo, hi) in enumerate(((P, 0, 4), (META, 4, 5))):
                dve.tensor_scalar(ssx[0:rows, lo:hi], ssx[0:rows, lo:hi], 1.0 / D, EPS, ALU.mult, ALU.add) \
                    .then_inc(sem("x_ms"), 1)
            dve.wait_ge(sem("x_sd"), 2)
            dve.reciprocal(rsx[:, 0:4], sd[:, 0:4]).then_inc(sem("x_rs"), 1)
            dve.reciprocal(rsx[0:META, 4:5], sd[0:META, 4:5]).then_inc(sem("x_rs"), 1)
            dve.wait_ge(sem("x_rs"), 2)
            for t in (4, 0, 1, 2, 3):
                n = P if t < 4 else META
                dve.tensor_scalar(nat[0:n, t, :], nat[0:n, t, :], rsx[0:n, t:t + 1], None, ALU.mult) \
                    .then_inc(sem("x_n"), 1)
            dve.wait_ge(sem("vec_tr"), 1)
            dve.tensor_copy(vec[:, 0:N_VEC], bank(7, 0, N_VEC))
            for layer in range(2):
                ins = dve.tensor_copy(vec[:, N_VEC + layer * FFN_ROWS:N_VEC + (layer + 1) * FFN_ROWS],
                                      bank(7, 128 * (layer + 1), 128 * (layer + 1) + FFN_ROWS))
            ins.then_inc(sem("vec"), 1)
            w_lo(dve, PRO)
            w_lo(dve, PRO + 1)
            dve.wait_ge(sem("vec"), 1)
            for k in range(KT):
                dve.wait_ge(sem("u_hi"), k + 1)
                b = 2 * (k % 2)
                dve.scalar_tensor_tensor(out=u[:, k, LO, META:LEN], in0=bank(b), scalar=vcol("pre_g", k),
                                         in1=u[:, k, HI, META:LEN], op0=ALU.mult, op1=ALU.subtract)
                dve.scalar_tensor_tensor(out=u[:, k, LO, 0:META], in0=bank(b + 1, 0, META),
                                         scalar=vcol("pre_g", k), in1=u[:, k, HI, 0:META],
                                         op0=ALU.mult, op1=ALU.subtract).then_inc(sem("u_lo"), 1)
            w_lo(dve, PRO + 2)
            w_lo(dve, PRO + 3)
            dve.wait_ge(sem("w_used"), PRO + 1)
            dve.wait_ge(sem("pro_meta"), 1)
            dve.wait_ge(sem("rope_in"), 32)
            dve.tensor_scalar(fx[:, META:LEN], bank(0, rows=slice(0, HEADS)), fbias, None, ALU.add)
            dve.tensor_scalar(fx[:, 0:META], bank(7, 0, META, rows=slice(0, HEADS)), fbias, None, ALU.add) \
                .then_inc(sem("f_x"), 1)
            dve.wait_ge(sem("f_act"), 3)
            dve.scalar_tensor_tensor(out=fm, in0=fx, scalar=0.0, in1=fe, op0=ALU.min, op1=ALU.subtract) \
                .then_inc(sem("f_dve"), 1)
            dve.wait_ge(sem("f_dve"), 1)
            dve.wait_ge(sem("ones"), 1)
            dve.tensor_tensor_scan(fx, ones[0:HEADS, 0:1].to_broadcast([HEADS, LEN]), fm, 0.0, ALU.mult, ALU.add).then_inc(sem("f_dve"), 1)
            dve.wait_ge(sem("f_dve"), 2)
            dve.tensor_scalar(fm, fx, 1.0 / FOX_SCALE, None, ALU.mult).then_inc(sem("f_cum"), 1)
            dve.tensor_scalar(fe, fx, -1.0 / FOX_SCALE, None, ALU.mult).then_inc(sem("f_cum"), 1)
            for s in range(2):
                dve.wait_ge(sem("forget_hi"), s + 1)
                dve.tensor_tensor(forget_r[:, s, LO, :], (fm, fe)[s], forget_r[:, s, HI, :], ALU.subtract) \
                    .then_inc(sem("forget_lo"), 1)
            dve.wait_ge(sem("w_used"), PRO + 2)
            dve.wait_ge(sem("forget_out"), 32)
            for s in range(2):
                rows = slice(32 * s, 32 * s + 32)
                dve.tensor_tensor(kro[64:96, s, META:LEN], bank(1, rows=rows), rope_s[64:96, s, META:LEN], ALU.mult)
                ins = dve.tensor_tensor(kro[64:96, s, 0:META], bank(7, 16, 32, rows=rows),
                                        rope_s[64:96, s, 0:META], ALU.mult)
            ins.then_inc(sem("kpe_t"), 1)
            dve.wait_ge(sem("kpe_t"), 1)
            dve.tensor_tensor(kro[64:96, 2, :], kro[64:96, 0, :], kro[64:96, 1, :], ALU.add).then_inc(sem("kpe_rot"), 1)
            dve.wait_ge(sem("kpe_hi"), 1)
            for hh in range(2):
                ins = dve.tensor_tensor(k_t[64:96, hh, LO, :], kro[64:96, 2, :], k_t[64:96, hh, HI, :], ALU.subtract)
            ins.then_inc(sem("kpe_lo"), 1)
            w_lo(dve, PRO + 4)
            dve.wait_ge(sem("c_sd"), 1)
            dve.reciprocal(krs[:, 0, :], krs[:, 0, :]).then_inc(sem("c_rs"), 1)
            dve.wait_ge(sem("c_rs"), 1)
            dve.scalar_tensor_tensor(out=kn[:, META:LEN], in0=bank(2), scalar=vcol("kv_g"), in1=krs[:, 0, META:LEN],
                                     op0=ALU.mult, op1=ALU.mult)
            dve.scalar_tensor_tensor(out=kn[:, 0:META], in0=bank(7, 32, 48), scalar=vcol("kv_g"),
                                     in1=krs[:, 0, 0:META], op0=ALU.mult, op1=ALU.mult).then_inc(sem("c_n"), 1)
            dve.wait_ge(sem("c_hi"), 1)
            dve.tensor_tensor(ckv_r[:, LO, :], kn, ckv_r[:, HI, :], ALU.subtract).then_inc(sem("c_lo"), 1)
            w_lo(dve, PRO + 5)
            dve.wait_ge(sem("c_sd"), 2)
            dve.reciprocal(krs[:, 1, 0:SEQ], krs[:, 1, 0:SEQ]).then_inc(sem("c_rs"), 1)
            dve.wait_ge(sem("c_rs"), 2)
            for t in range(2):
                dve.wait_ge(sem("c_lo"), 1 + t)
                dve.scalar_tensor_tensor(out=kn[:, 0:SEQ], in0=bank(3 + t), scalar=vcol("q_g", t),
                                         in1=krs[:, 1, 0:SEQ], op0=ALU.mult, op1=ALU.mult).then_inc(sem("c_n"), 1)
                dve.wait_ge(sem("c_hi"), 2 + t)
                dve.tensor_tensor(cq_r[:, t, LO, :], kn[:, 0:SEQ], cq_r[:, t, HI, :], ALU.subtract) \
                    .then_inc(sem("c_lo"), 1)

        def pe_prologue(pe):
            pe.wait_ge(sem("cst_in"), 16)
            pe.wait_ge(sem("vec_in"), N_VEC_DMA)
            pe.transpose(bank(7, 0, N_VEC), stage[0:N_VEC, 0, :], ident[0:N_VEC, 0:N_VEC])
            for layer in range(2):
                ins = pe.transpose(bank(7, 128 * (layer + 1), 128 * (layer + 1) + FFN_ROWS),
                                   stage[0:FFN_ROWS, 1 + layer, :], ident[0:FFN_ROWS, 0:FFN_ROWS])
            ins.then_inc(sem("vec_tr"), 1)
            pe.wait_ge(sem("x_n"), 5)
            for k in range(KT):
                if k >= 2:
                    pe.wait_ge(sem("u_lo"), k - 1)
                b = 2 * (k % 2)
                pe.transpose(bank(b + 1, 0, META), nat[0:META, 4, k * P:(k + 1) * P], ident[0:META, 0:META])
                for t in range(NQ):
                    ins = pe.transpose(bank(b, t * P, (t + 1) * P), nat[:, t, k * P:(k + 1) * P], ident)
                ins.then_inc(sem("x_tr"), 1)
            pe.wait_ge(sem("u_lo"), KT)
            pe.wait_ge(sem("vec"), 1)
            for j in range(3):
                w_ready(pe, PRO + j)
                ins = product(pe, bank(7, 16 * j, 16 * j + 16), PRO + j, u_meta)
                if j == 2:
                    ins.then_inc(sem("pro_meta"), 1)
                product(pe, bank(j), PRO + j, u_real).then_inc(sem("w_used"), 1)
            pe.wait_ge(sem("ones"), 1)
            w_ready(pe, PRO + 3)
            product(pe, bank(3), PRO + 3, u_real).then_inc(sem("w_used"), 1)
            pe.wait_ge(sem("c_sq"), 1)
            pe.matmul(bank(5), ones[:], ksq[:, 0, META:LEN], start=True, stop=True)
            pe.matmul(bank(6, 0, META), ones[:], ksq[:, 0, 0:META], start=True, stop=True).then_inc(sem("c_sum"), 1)
            w_ready(pe, PRO + 4)
            product(pe, bank(4), PRO + 4, u_real).then_inc(sem("w_used"), 1)
            pe.wait_ge(sem("c_sq"), 3)
            pe.wait_ge(sem("c_sd"), 1)
            for t in range(2):
                ins = pe.matmul(bank(5), ones[:], ksq[:, 1 + t, 0:SEQ], start=t == 0, stop=t == 1)
            ins.then_inc(sem("c_sum"), 1)

        def n_real(b):
            return P * (b % NQ + 1)

        def s_cols(b, meta=True):
            return slice(B_S * 512 + 512 - n_real(b), B_S * 512 + 512 + (META if meta else 0))

        def attn_units(s):
            return FIRST[("attn", s)] if isinstance(s, int) else None

        def pe_scores(pe, pr, b, fox):
            hh, i = divmod(b, NQ)
            rows = slice(0, 97 if fox else 96)
            if b == 0:
                pe.wait_ge(sem("q_split"), pr + 1)
                pe.wait_ge(sem("k_split"), pr + 1)
                if fox:
                    pe.wait_ge(sem("rows"), 32 * (pr - PAIRS) + 32)
                else:
                    pe.wait_ge(sem("kpe_lo"), 1)
            if not (isinstance(pr, int) and pr == 0 and b == 0):
                pe.wait_ge(sem("exped"), 8 * pr + b)
            for n, (qs, ks) in enumerate(PASSES):
                pe.matmul(ps[:, s_cols(b, False)], q_t[rows, hh, qs, i * P:(i + 1) * P],
                          k_t[rows, hh, ks, META:META + n_real(b)], start=n == 0, stop=False,
                          skip_group_check=True)
            pe.matmul(bank(B_S, 384, 512), ident_r[:], mask_r[:], start=False, stop=True, skip_group_check=True)
            for n, (qs, ks) in enumerate(PASSES):
                ins = pe.matmul(bank(B_S + 1, 0, META), q_t[rows, hh, qs, i * P:(i + 1) * P],
                                k_t[rows, hh, ks, 0:META], start=n == 0, stop=n == 2)
            ins.then_inc(sem("scores"), 1)

        def pe_transposes(pe, pr, b, prev):
            pe.wait_ge(sem("normed"), 8 * pr + b + 1)
            if b:
                pe.wait_ge(sem("p_split"), 8 * pr + b)
            elif prev:
                pe.wait_ge(sem("pm_split"), pr)
                pe.wait_ge(sem("v_split"), pr + 1)
            base = 512 - n_real(b)
            for j in range(b % NQ + 1):
                ins = pe.transpose(bank(B_T, j * P, (j + 1) * P),
                                   prob[:, b % 2, base + j * P:base + (j + 1) * P], ident)
            ins.then_inc(sem("transposed"), 1)

        def pe_transposes_meta(pe, pr):
            pe.wait_ge(sem("p_split"), 8 * pr + 8)
            pe.wait_ge(sem("normed"), 8 * pr + 8)
            for i in range(NQ):
                ins = pe.transpose(bank(B_T, i * P, (i + 1) * P), prob_m[:, i, :], ident)
            ins.then_inc(sem("pm_transposed"), 1)

        def pe_values(pe, pr, hh):
            pe.wait_ge(sem("p_split"), 8 * pr + 4 * hh + 4)
            if hh == 0:
                pe.wait_ge(sem("v_split"), pr + 1)
                if not (isinstance(pr, int) and pr == 0):
                    pe.wait_ge(sem("gated"), pr)
            for j in range(NQ):
                for n, (vs, pp) in enumerate(PASSES):
                    pe.matmul(bank(B_O, j * P, 512), v_t[:, vs, j, hh, :], p_t[:, hh, pp * NQ + j, j * P:512],
                              start=hh == 0 and j == 0 and n == 0, stop=False, skip_group_check=True)
            if hh == 1:
                pe.wait_ge(sem("pm_split"), pr + 1)
                for n, (vs, pp) in enumerate(PASSES):
                    ins = pe.matmul(bank(B_O), v_m[0:48, vs, :], p_m[0:48, pp, :], start=False, stop=n == 2,
                                    skip_group_check=True)
                ins.then_inc(sem("values"), 1)

        def mla_q(pe, c, hh):
            for n, (k, ws, ms) in enumerate([(k, ws, ms) for k in range(2) for ws, ms in PASSES]):
                g = 2 * k + hh
                ins = pe.matmul(bank(hh), wsp[:, c % 2, ws, g * P:(g + 1) * P], cq_r[:, k, ms, :],
                                start=n == 0, stop=n == 5)
            return ins

        def products_mla(pe, s, c, kk=0, i=0):
            def z(part):
                bounds = (0, 2, 4, 5, 7, 8)
                if part == 0:
                    w_ready(pe, c, i, kk)
                    if not (isinstance(s, int) and s == 0):
                        pe.wait_ge(sem("q_split"), s)
                ins = product(pe, bank(0), c, u_real, range(bounds[part], bounds[part + 1]),
                              start=part == 0, stop=part == 4)
                if part == 4:
                    ins.then_inc(sem("w_used"), 1)

            def qa():
                w_ready(pe, c + 1, i, kk)
                pe.wait_ge(sem("z_read"), s + 1)
                mla_q(pe, c + 1, 0)

            def qb():
                mla_q(pe, c + 1, 1).then_inc(sem("q_done"), 1)

            def k_and_meta():
                if not (isinstance(s, int) and s == 0):
                    pe.wait_ge(sem("k_split"), s)
                    pe.wait_ge(sem("v_split"), s)
                wk = [wsp[:, (c + 1) % 2, part, 512:640] for part in range(2)]
                wv = [wsp[:, (c + 1) % 2, part, 640:768] for part in range(2)]
                for n, (ws, ms) in enumerate(PASSES):
                    pe.matmul(bank(2), wk[ws], ckv_r[:, ms, META:LEN], start=n == 0, stop=n == 2)
                for n, (ws, ms) in enumerate(PASSES):
                    pe.matmul(bank(B_META, 0, META), wk[ws], ckv_r[:, ms, 0:META], start=n == 0, stop=n == 2)
                for n, (ws, ms) in enumerate(PASSES):
                    ins = pe.matmul(bank(B_META, 128, 256), ckv_r[:, ms, 0:P], wv[ws], start=n == 0, stop=n == 2)
                ins.then_inc(sem("k_done"), 1)

            def v():
                if not (isinstance(s, int) and s == 0):
                    pe.wait_ge(sem("pm_split"), s)
                wv = [wsp[:, (c + 1) % 2, part, 640:768] for part in range(2)]
                for t in range(NQ):
                    for n, (ws, ms) in enumerate(PASSES):
                        ins = pe.matmul(bank(B_T, t * P, (t + 1) * P), ckv_r[:, ms, META + t * P:META + (t + 1) * P],
                                        wv[ws], start=n == 0, stop=n == 2)
                ins.then_inc(sem("w_used"), 1)

            parts = [lambda p=p: z(p) for p in range(5)] + [qa, qb, k_and_meta]
            return parts, v

        def products_fox(pe, s, c, kk=0, i=0):
            def weights_still(part, b, j):
                def run():
                    if part == 0:
                        w_ready(pe, c + j, i, kk)
                        if j == 0:
                            pe.wait_ge(sem("q_split"), s)
                        elif j == 1:
                            pe.wait_ge(sem("z_read"), s + 1)
                        else:
                            pe.wait_ge(sem("k_split"), s)
                            pe.wait_ge(sem("v_split"), s)
                    ins = product(pe, bank(b), c + j, u_real, range(4 * part, 4 * part + 4),
                                  start=part == 0, stop=part == 1)
                    if j == 2 and part == 1:
                        ins = product(pe, bank(B_META, 0, META), c + j, u_meta)
                    if part == 1:
                        ins.then_inc(sem("w_used"), 1)
                return run

            def values(part):
                def run():
                    if part == 0:
                        w_ready(pe, c + 3, i, kk)
                    tiles = [(bank(2, t * P, (t + 1) * P), META + t * P) for t in (2 * part, 2 * part + 1)]
                    if part:
                        tiles.append((bank(B_META, 128, 256), 0))
                    for dst, tok in tiles:
                        total = [(k, us, ws) for k in range(KT) for us, ws in PASSES]
                        for n, (k, us, ws) in enumerate(total):
                            ins = pe.matmul(dst, u[:, k, us, tok:tok + P], w_tile(c + 3, ws, k),
                                            start=n == 0, stop=n == len(total) - 1)
                    if part:
                        ins.then_inc(sem("w_used"), 1)
                return run

            parts = [weights_still(0, 0, 0), weights_still(1, 0, 0), weights_still(0, 0, 1), weights_still(1, 0, 1),
                     weights_still(0, 1, 2), weights_still(1, 1, 2), values(0), values(1)]
            return parts, None

        def pe_step(pe, s, attn, gemm, c, kk=0, i=0):
            parts, tail = [], None
            if gemm:
                parts, tail = (products_mla if gemm == "mla" else products_fox)(pe, s, c, kk, i)
            pr = s - 1
            for b in range(8):
                if attn:
                    pe_scores(pe, pr, b, attn == "fox")
                if parts:
                    parts[b]()
                if attn and b:
                    pe_transposes(pe, pr, b - 1, True)
            if attn:
                pe_values(pe, pr, 0)
                pe_transposes(pe, pr, 7, True)
                pe_transposes_meta(pe, pr)
                pe_values(pe, pr, 1)
            if tail:
                tail()

        def act_exp(act, pr, b, fox):
            act.wait_ge(sem("neg"), 8 * pr + b + 1)
            if not (isinstance(pr, int) and pr == 0 and b < 2):
                act.wait_ge(sem("transposed"), 8 * pr + b - 1)
            act.activation(prob[:, b % 2, 512 - n_real(b):LEN], ps[:, s_cols(b)], ACT.Exp, bias=neg[:, b:b + 1],
                           scale=FOX_SCALE if fox else MLA_SCALE, accum_out=rs[:, b:b + 1]) \
                .then_inc(sem("exped"), 1)

        def p_views(b):
            hh, i = divmod(b, NQ)
            src = bank(B_T, 0, (i + 1) * P).rearrange("p (j n) -> p j n", n=P)
            hi, lo = (p_t[:, hh, part * NQ:part * NQ + i + 1, i * P:(i + 1) * P] for part in range(2))
            return src, hi, lo

        def act_p(act, pr, b):
            act.wait_ge(sem("transposed"), 8 * pr + b + 1)
            if not (isinstance(pr, int) and pr == 0):
                act.wait_ge(sem("values"), pr)
            src, hi, _ = p_views(b)
            act.copy(hi, src).then_inc(sem("p_hi"), 1)

        def act_z(act, s, c, kk=0, i=0):
            act.wait_ge(sem("w_used"), num(c, i, kk) + 1)
            act.activation(big[:, idx(s), :], bank(0) if isinstance(s, int) else bank(0).rearrange("p (a n) -> p a n", a=1),
                           ACT.Silu).then_inc(sem("z_read"), 1)

        def qk_pieces(s, what, gemm):
            if what == "q":
                if gemm == "mla":
                    return [(bank(hh, rows=slice(0, NOPE)), q_t[0:NOPE, hh], slice(0, SEQ)) for hh in range(2)] + \
                           [(rot[64:96, hh, :], q_t[64:96, hh], slice(0, SEQ)) for hh in range(2)]
                return [(bank(0, rows=slice(64 * hh, 64 * hh + 64)), q_t[0:HD, hh], slice(0, SEQ)) for hh in range(2)]
            b = 2 if gemm == "mla" else 1
            return [(bank(b, rows=slice(64 * hh, 64 * hh + 64)), k_t[0:HD, hh], slice(META, LEN)) for hh in range(2)] + \
                   [(bank(B_META, 0, META, rows=slice(64 * hh, 64 * hh + 64)), k_t[0:HD, hh], slice(0, META))
                    for hh in range(2)]

        def v_pieces(part, gemm):
            src = bank(B_T if gemm == "mla" else 2).rearrange("p (n h d) -> p n h d", n=NQ, h=2)
            dst = v_t[:, part].rearrange("p n h (a d) -> p n (h a) d", a=2)[:, :, 0:4:3, :]
            out_ = [(src, dst)]
            for hh in range(2):
                out_.append((bank(B_META, 128 + 64 * hh, 192 + 64 * hh, rows=slice(0, META)),
                             v_m[32 * hh:32 * hh + META, part, 64 * hh:64 * hh + 64]))
            return out_

        def act_qk(act, s, c, gemm, kk=0, i=0):
            first_pair = isinstance(s, int) and s == 0
            if gemm == "mla":
                act.wait_ge(sem("q_done"), s + 1)
                act.wait_ge(sem("rotated_one"), 2 * s + 2)
            else:
                act.wait_ge(sem("w_used"), num(c + 1, i, kk) + 1)
            if not first_pair:
                act.wait_ge(sem("scores"), 8 * s)
            for src, dst, cols in qk_pieces(s, "q", gemm):
                ins = act.copy(dst[:, HI, cols], src)
            ins.then_inc(sem("q_hi"), 1)
            if gemm == "mla":
                act.wait_ge(sem("k_done"), s + 1)
            else:
                act.wait_ge(sem("w_used"), num(c + 3, i, kk) + 1)
            for src, dst, cols in qk_pieces(s, "k", gemm):
                ins = act.copy(dst[:, HI, cols], src)
            ins.then_inc(sem("k_hi"), 1)

        def act_v(act, s, c, gemm, kk=0, i=0):
            if isinstance(s, int) and s == 0:
                act.wait_ge(sem("pads"), 1)
            else:
                act.wait_ge(sem("values"), s)
            act.wait_ge(sem("w_used"), num(c + (1 if gemm == "mla" else 3), i, kk) + 1)
            act.wait_ge(sem("k_split"), s + 1)
            for src, dst in v_pieces(HI, gemm):
                ins = act.copy(dst, src)
            ins.then_inc(sem("v_hi"), 1)

        def act_step(act, s, attn, gemm, c, kk=0, i=0, nxt=None):
            pr = s - 1
            for b in range(8):
                if gemm == "fox" and b in (0, 2, 4):
                    w_hi(act, c + 1 + b // 2, i, kk, "full")
                if gemm == "mla" and b == 0:
                    w_hi(act, c + 1, i, kk, "qkv")
                if attn:
                    act_exp(act, pr, b, attn == "fox")
                if gemm and b == (1 if gemm == "fox" else 4):
                    act_z(act, s, c, kk, i)
                if gemm and b == 6:
                    w_hi(act, nxt, i, kk, "full")
                if attn and b:
                    act_p(act, pr, b - 1)
            if gemm:
                act_qk(act, s, c, gemm, kk, i)
            if attn:
                act_p(act, pr, 7)
                act.wait_ge(sem("pm_transposed"), pr + 1)
                act.copy(p_m[0:48, HI, :], bank(B_T, rows=slice(0, 48))).then_inc(sem("pm_hi"), 1)
            if gemm:
                act_v(act, s, c, gemm, kk, i)

        def dve_max(dve, pr, b, fox):
            dve.wait_ge(sem("scores"), 8 * pr + b + 1)
            dve.reduce_max(mx[:, b:b + 1], ps[:, s_cols(b)], AX.X).then_inc(sem("maxed"), 1)
            dve.wait_ge(sem("maxed"), 8 * pr + b + 1)
            dve.tensor_scalar(neg[:, b:b + 1], mx[:, b:b + 1], -(FOX_SCALE if fox else MLA_SCALE), None, ALU.mult) \
                .then_inc(sem("neg"), 1)

        def dve_norm(dve, pr, b):
            hh, i = divmod(b, NQ)
            dve.wait_ge(sem("exped"), 8 * pr + b + 1)
            dve.reciprocal(ri[:, b:b + 1], rs[:, b:b + 1]).then_inc(sem("recip"), 1)
            dve.wait_ge(sem("recip"), 8 * pr + b + 1)
            if b == 0:
                dve.wait_ge(sem("pads"), 2)
                if not (isinstance(pr, int) and pr == 0):
                    dve.wait_ge(sem("pm_transposed"), pr)
            real = prob[:, b % 2, 512 - n_real(b):512]
            dve.tensor_scalar(prob_m[:, i, 32 * hh:32 * hh + META], prob[:, b % 2, 512:LEN], ri[:, b:b + 1], None,
                              ALU.mult)
            dve.tensor_scalar(real, real, ri[:, b:b + 1], None, ALU.mult).then_inc(sem("normed"), 1)

        def dve_p(dve, pr, b):
            dve.wait_ge(sem("p_hi"), 8 * pr + b + 1)
            src, hi, lo = p_views(b)
            dve.tensor_tensor(lo, src, hi, ALU.subtract).then_inc(sem("p_split"), 1)

        def dve_rotate(dve, s):
            dve.wait_ge(sem("q_done"), s + 1)
            if isinstance(s, int) and s == 0:
                dve.wait_ge(sem("vec"), 1)
            else:
                dve.wait_ge(sem("q_split"), s)
            for hh in range(2):
                n = 2 * s + hh
                if hh or not (isinstance(s, int) and s == 0):
                    dve.wait_ge(sem("rotated_one"), n)
                dve.tensor_tensor(rt1[64:96, 0, :], bank(hh, rows=slice(64, 96)), rope_s[64:96, 0, META:LEN], ALU.mult)
                dve.tensor_tensor(rt2[64:96, 0, :], bank(hh, rows=slice(96, 128)), rope_s[64:96, 1, META:LEN],
                                  ALU.mult).then_inc(sem("rotating"), 1)
                dve.wait_ge(sem("rotating"), n + 1)
                dve.tensor_tensor(rot[64:96, hh, :], rt1[64:96, 0, :], rt2[64:96, 0, :], ALU.add) \
                    .then_inc(sem("rotated_one"), 1)

        def dve_qk(dve, s, gemm):
            dve.wait_ge(sem("q_hi"), s + 1)
            for src, dst, cols in qk_pieces(s, "q", gemm):
                ins = dve.tensor_tensor(dst[:, LO, cols], src, dst[:, HI, cols], ALU.subtract)
            ins.then_inc(sem("q_split"), 1)
            dve.wait_ge(sem("k_hi"), s + 1)
            for src, dst, cols in qk_pieces(s, "k", gemm):
                ins = dve.tensor_tensor(dst[:, LO, cols], src, dst[:, HI, cols], ALU.subtract)
            ins.then_inc(sem("k_split"), 1)

        def dve_v(dve, s, gemm):
            dve.wait_ge(sem("v_hi"), s + 1)
            for (src, dst), (_, hi) in zip(v_pieces(LO, gemm), v_pieces(HI, gemm)):
                ins = dve.tensor_tensor(dst, src, hi, ALU.subtract)
            ins.then_inc(sem("v_split"), 1)

        def dve_step(dve, s, attn, gemm, c, kk=0, i=0, nxt=None):
            pr = s - 1
            for b in range(8):
                if attn:
                    dve_max(dve, pr, b, attn == "fox")
                    dve_norm(dve, pr, b)
                if gemm == "fox" and b in (0, 2, 4):
                    w_lo(dve, c + 1 + b // 2, i, kk, "full")
                if gemm == "mla" and b == 0:
                    w_lo(dve, c + 1, i, kk, "qkv")
                if gemm and b == 6:
                    w_lo(dve, nxt, i, kk, "full")
                if attn and b:
                    dve_p(dve, pr, b - 1)
            if gemm == "mla":
                dve_rotate(dve, s)
            if gemm:
                dve_qk(dve, s, gemm)
            if attn:
                dve_p(dve, pr, 7)
                dve.wait_ge(sem("pm_hi"), pr + 1)
                dve.tensor_tensor(p_m[0:48, LO, :], bank(B_T, rows=slice(0, 48)), p_m[0:48, HI, :], ALU.subtract) \
                    .then_inc(sem("pm_split"), 1)
                dve.wait_ge(sem("values"), pr + 1)
                z = big[:, idx(pr), :]
                o = bank(B_O) if isinstance(pr, int) else bank(B_O).rearrange("p (a n) -> p a n", a=1)
                dve.tensor_tensor(z, o, z, ALU.mult).then_inc(sem("gated"), 1)
            if gemm:
                dve_v(dve, s, gemm)

        def pool_rows(pool, g):
            pool.wait_ge(sem("scores"), 8 * (g + PAIRS))
            if isinstance(g, int) and g == 0:
                pool.memset(q_t[64:96].bitcast(F32), 0.0).then_inc(sem("aug"), 1)
                pool.memset(k_t[64:96].bitcast(F32), 0.0).then_inc(sem("aug"), 1)
                pool.memset(k_t[96:97, :, HI, :].bitcast(F32), 1.0)
                pool.memset(k_t[96:97, :, LO, :].bitcast(F32), 0.0).then_inc(sem("aug"), 1)
                pool.wait_ge(sem("aug"), 3)
                pool.memset(q_t[64:65, :, HI, :].bitcast(F32), 1.0).then_inc(sem("aug"), 1)
                pool.wait_ge(sem("aug"), 4)
                pool.wait_ge(sem("forget_out"), 32)
            h0 = 2 * g
            cum = forget_dram[0, bass.ds(h0, 2)]
            pool.dma_start(q_t[96:97].bitcast(F32), cum[:, :, META:LEN].rearrange("(a h) j n -> a h j n", a=1)) \
                .then_inc(sem("rows"), 16)
            pool.dma_start(k_t[64:65].bitcast(F32), forget_dram[1, bass.ds(h0, 2)].rearrange("(a h) j n -> a h j n", a=1)) \
                .then_inc(sem("rows"), 16)

        def steps(eng, step):
            c0 = FIRST[("attn", 0)]
            step(0, None, "mla", c0, 0, 0, c0 + 2)
            step(1, "mla", "mla", c0 + 2, 0, 0, c0 + 4)
            with eng.Fori(2, PAIRS) as i:
                step(i, "mla", "mla", c0, 2, i, c0 + 2)
            c8 = FIRST[("attn", PAIRS)]
            step(PAIRS, "mla", "fox", c8, 0, 0, c8 + 4)
            with eng.Fori(1, PAIRS) as i:
                step(i + PAIRS, "fox", "fox", c8, 4, i, c8 + 4)
            step(STEPS, "fox", None, None)

        def load_attention(sp):
            def mla(s, c, kk, i):
                at_ = (s * P, s * 192, s * 256)
                if not isinstance(s, int):
                    at_ = tuple(sp.snap(x) for x in at_)
                w_load(sp, c, panel(w_in, W_ZM + at_[0]), i, kk)
                uq, ukv = a["w_uq"][0], a["w_ukv"][0]
                w_load(sp, c + 1, [
                    (lambda r: r[:, 0:384].rearrange("p (k n) -> p k n", k=2),
                     uq[:, bass.ds(at_[1], 192)].rearrange("(k p) n -> p k n", p=P)),
                    (lambda r: r[:, 384:640], ukv[:, bass.ds(at_[2], 256)])], i, kk)

            def fox(g, c, kk, i):
                at_ = g * P if isinstance(g, int) else sp.snap(g * P)
                for j, col in enumerate((W_ZF, W_FQ, W_FK, W_FV)):
                    w_load(sp, c + j, panel(w_in, col + at_), i, kk)

            c0, c8 = FIRST[("attn", 0)], FIRST[("attn", PAIRS)]
            mla(0, c0, 0, 0)
            with sp.Fori(1, PAIRS) as i:
                mla(i, c0, 2, i)
            fox(0, c8, 0, 0)
            with sp.Fori(1, PAIRS) as i:
                fox(i, c8, 4, i)

        MIX = FIRST["mix"]

        def load_mix(sp):
            def body(n, first, last):
                for j, (w, col) in enumerate(((w_in, W_GA), (w_in, W_GB), (a["w_br_mla"][0], 0),
                                              (a["w_br_fox"][0], 0))):
                    w_load(sp, MIX + j, panel(w, col + n * P), n, 4)
            loop(sp, KT, body)

        def pe_mix(pe):
            pe.wait_ge(sem("gated"), STEPS)

            def body(n, first, last):
                for j in range(4):
                    c = MIX + j
                    w_ready(pe, c, n, 4)
                    if not first:
                        pe.wait_ge(sem("sig"), 2 * n - 1 + j) if j < 2 else pe.wait_ge(sem("branch"), 2 * n - 3 + j)
                    if j < 2:
                        moving = u_real
                    else:
                        if first:
                            pe.wait_ge(sem("o_lo"), 8 * (j - 1))
                        moving = lambda k, part, j=j: o_r[:, 8 * (j - 2) + k, part, :]
                    product(pe, bank(j), c, moving).then_inc(sem("w_used"), 1)
            loop(pe, KT, body)

        def act_mix(act):
            act.wait_ge(sem("gated"), STEPS)
            w_hi(act, MIX + 1)

            for t in range(16):
                act.copy(o_r[:, t, HI, :], big[:, t, :]).then_inc(sem("o_hi"), 1)

            def body(n, first, last):
                for j in range(2):
                    act.wait_ge(sem("w_used"), MIX + j + 1 + 4 * n)
                    if not first:
                        act.wait_ge(sem("branch"), 2 * n - 1 + j)
                    act.activation(sig[:, j, :], bank(j), ACT.Sigmoid).then_inc(sem("sig"), 1)
                    w_hi(act, MIX + j + 2, n, 4, "full")
                act.wait_ge(sem("w_used"), MIX + 3 + 4 * n)
                w_hi(act, MIX + 4, n, 4, "full")
                act.wait_ge(sem("w_used"), MIX + 4 + 4 * n)
                w_hi(act, MIX + 5, n, 4, "full")
            loop(act, KT, body)

        def dve_mix(dve):
            w_lo(dve, MIX + 1)
            for t in range(16):
                dve.wait_ge(sem("o_hi"), t + 1)
                dve.tensor_tensor(o_r[:, t, LO, :], big[:, t, :], o_r[:, t, HI, :], ALU.subtract) \
                    .then_inc(sem("o_lo"), 1)

            def body(n, first, last):
                for j in range(2):
                    dve.wait_ge(sem("sig"), 2 * n + j + 1)
                    w_lo(dve, MIX + j + 2, n, 4, "full")
                for j in range(2):
                    dve.wait_ge(sem("w_used"), MIX + j + 3 + 4 * n)
                    if not first:
                        dve.wait_ge(sem("mixed"), n)
                    dve.tensor_tensor(sig[:, 2 + j, :], bank(2 + j), sig[:, j, :], ALU.mult).then_inc(sem("branch"), 1)
                    w_lo(dve, MIX + 4 + j, n, 4, "full")
                dve.wait_ge(sem("branch"), 2 * n + 2)
                dst = h[:, idx(n), :]
                s2, s3 = (sig[:, 2 + j, :] if isinstance(n, int) else sig[:, 2 + j:3 + j, :] for j in range(2))
                dve.tensor_tensor(dst, s2, s3, ALU.add).then_inc(sem("mixed"), 1)
            loop(dve, KT, body)

        NORMS = ("out", "e", "eo", "down0", "oo", "down1")

        def tiles_before(tag):
            return KT * NORMS.index(tag)

        def hs_before(tag):
            return KT * (NORMS.index(tag) - 1)

        def norms_done(tag):
            return NORMS.index(tag) + 1

        def res_units(name):
            return 3 if name in (("down", 0), ("down", 1)) else 1

        def pe_residual(pe, name, moving, before, tag):
            c0, per = FIRST[name], res_units(name)
            before(pe)

            def body(i, first, last):
                for j in range(2):
                    if not first:
                        pe.wait_ge(sem("h_tile"), hs_before(tag) + 2 * i + j - 1)
                    if per == 1:
                        w_ready(pe, c0 + j, i, 2)
                        product(pe, bank(j), c0 + j, moving).then_inc(sem("w_used"), 1)
                    else:
                        k0 = 0
                        for m, ks in enumerate(DOWN):
                            c = c0 + 3 * j + m
                            w_ready(pe, c, i, 6)
                            product(pe, bank(j), c, moving, range(k0, k0 + ks), start=m == 0, stop=m == 2, n0=k0) \
                                .then_inc(sem("w_used"), 1)
                            k0 += ks
            loop(pe, KT // 2, body)

        def load_residual(sp, name, dram):
            c0 = FIRST[name]

            def body(i, first, last):
                for j in range(2):
                    if res_units(name) == 1:
                        w_load(sp, c0 + j, panel(dram, (2 * i + j) * P), i, 2)
                    else:
                        k0 = 0
                        for m, ks in enumerate(DOWN):
                            w_load(sp, c0 + 3 * j + m, panel(dram, (2 * i + j) * P, ks, k0), i, 6)
                            k0 += ks
            loop(sp, KT // 2, body)

        def next_kind(c, last, k):
            return None if last else (KINDS[c - k] if c - k >= 0 else None)

        def w_next(split, eng, c, i, k, last, n_steps):
            if last:
                split(eng, c + i * k)
            else:
                split(eng, c, i, k, KINDS[c])

        def act_residual(act, name, gain, tag):
            c0, per = FIRST[name], res_units(name)

            def body(i, first, last):
                for j in range(2):
                    for m in range(per):
                        c = c0 + per * j + m
                        act.wait_ge(sem("w_used"), num(c, i, 2 * per) + 1)
                        if c + 2 - c0 >= 2 * per and last:
                            w_hi(act, c + 2 + i * 2 * per)
                        else:
                            w_hi(act, c + 2, i, 2 * per, KINDS[c + 2])
                    n = 2 * i + j
                    act.wait_ge(sem("h_tile"), hs_before(tag) + n + 1)
                    if not first:
                        act.wait_ge(sem("acc_done"), tiles_before(tag) + n - 1)
                    if gain:
                        hn = h[:, idx(n), :]
                        dst = u[:, n, HI, META:LEN] if isinstance(n, int) else u[:, bass.ds(n, 1), HI, META:LEN]
                        act.activation(dst, hn, ACT.Copy, scale=vcol(*gain_at(gain, n))).then_inc(sem("hs_hi"), 1)
                    sqj = sq[:, j, :] if isinstance(n, int) else sq[:, j:j + 1, :]
                    act.activation(sqj, h[:, idx(n), :], ACT.Square).then_inc(sem("squared"), 1)
            loop(act, KT // 2, body)

        def gain_at(gain, n):
            return (gain[0], gain[1] + n)

        def dve_residual(dve, name, gain, tag):
            c0, per = FIRST[name], res_units(name)

            def body(i, first, last):
                for j in range(2):
                    for m in range(per):
                        c = c0 + per * j + m
                        if c + 2 - c0 >= 2 * per and last:
                            w_lo(dve, c + 2 + i * 2 * per)
                        else:
                            w_lo(dve, c + 2, i, 2 * per, KINDS[c + 2])
                    n = 2 * i + j
                    dve.wait_ge(sem("w_used"), num(c0 + per * j + per - 1, i, 2 * per) + 1)
                    hn = h[:, idx(n), :]
                    b = bank(j) if isinstance(n, int) else bank(j).rearrange("p (a n) -> p a n", a=1)
                    dve.tensor_tensor(hn, b, hn, ALU.add).then_inc(sem("h_tile"), 1)
                    if gain:
                        dve.wait_ge(sem("hs_hi"), hs_before(tag) + n + 1)
                        dst, hi = (u[:, idx(n), part, META:LEN] for part in (LO, HI))
                        dve.scalar_tensor_tensor(out=dst, in0=hn, scalar=vcol(*gain_at(gain, n)), in1=hi,
                                                 op0=ALU.mult, op1=ALU.subtract).then_inc(sem("hs"), 1)
            loop(dve, KT // 2, body)

        def pool_squares(pool, tag):
            for n in range(KT):
                pool.wait_ge(sem("squared"), tiles_before(tag) + n + 1)
                if n == 0:
                    ins = pool.tensor_copy(acc[:, 0, :], sq[:, 0, :])
                else:
                    pool.wait_ge(sem("acc_done"), tiles_before(tag) + n)
                    ins = pool.tensor_tensor(acc[:, 0, :], acc[:, 0, :], sq[:, n % 2, :], ALU.add)
                ins.then_inc(sem("acc_done"), 1)

        def pe_stats(pe, tag, bc=True, tok=False):
            pe.wait_ge(sem("acc_done"), tiles_before(tag) + KT)
            if bc:
                ins = pe.matmul(bank(7), ones[:], acc[:, 0, :], start=True, stop=True)
            if tok:
                for t in range(NQ):
                    ins = pe.matmul(bank(6, t, t + 1), acc[:, 0, t * P:(t + 1) * P], ones[:, 0:1],
                                    start=True, stop=True)
            ins.then_inc(sem("summed"), 1)

        def act_stats(act, tag, bc=True, tok=False):
            act.wait_ge(sem("summed"), norms_done(tag))
            if tok:
                act.activation(sstok, bank(6, 0, NQ), ACT.Sqrt, scale=1.0 / D, bias=EPS).then_inc(sem("rms_tok"), 1)
            if bc:
                act.activation(rbc[:, 0, :], bank(7), ACT.Sqrt, scale=1.0 / D, bias=EPS).then_inc(sem("rms"), 1)

        def dve_stats(dve, tag, bc=True, tok=False):
            if tok:
                dve.wait_ge(sem("rms_tok"), 1 if tag == "down0" else 2)
                dve.reciprocal(rtok, sstok).then_inc(sem("rtok"), 1)
            if bc:
                dve.wait_ge(sem("rms"), norms_done(tag))
                dve.reciprocal(rbc[:, 0, :], rbc[:, 0, :]).then_inc(sem("rbc"), 1)
                dve.wait_ge(sem("rbc"), norms_done(tag))

        OUT = FIRST["out"]

        def load_out(sp):
            for n in range(KT):
                w_load(sp, OUT + n, panel(a["w_out"][0], n * P))
                if n % 2 == 1:
                    t = n // 2
                    if t == 0:
                        sp.wait_ge(sem("mixed"), KT)
                    if t >= 2:
                        sp.wait_ge(sem("x_again"), 2 * t - 2)
                    sp.dma_start(xin[:, t % 2, :], a["x"][0, t * P:(t + 1) * P, :]).then_inc(sem(f"x2_in{t % 2}"), 16)

        def pe_out(pe):
            for n in range(KT):
                w_ready(pe, OUT + n)
                if n == 0:
                    pe.wait_ge(sem("mr_lo"), KT)
                if n >= 4:
                    pe.wait_ge(sem("m2"), n - 3)
                product(pe, bank(n % 4), OUT + n, u_real).then_inc(sem("w_used"), 1)
                t, half = divmod(n, 2)
                if half == 0:
                    pe.wait_ge(sem(f"x2_in{t % 2}"), 16 * (t // 2 + 1))
                if n >= 2:
                    pe.wait_ge(sem("h_x"), n - 1)
                for k in range(4):
                    ins = pe.transpose(bank(4 + half, k * P, (k + 1) * P),
                                       xin[:, t % 2, (4 * half + k) * P:(4 * half + k + 1) * P], ident)
                ins.then_inc(sem("x_again"), 1)
            pe_stats(pe, "out")

        def act_out(act):
            for k in range(KT):
                act.wait_ge(sem("mixed"), k + 1)
                act.copy(u[:, k, HI, META:LEN], h[:, k, :]).then_inc(sem("mr_hi"), 1)
            for n in range(KT):
                act.wait_ge(sem("m2"), n + 1)
                w_hi(act, OUT + n + 2)
                if n >= 2:
                    act.wait_ge(sem("acc_done"), n - 1)
                act.activation(sq[:, n % 2, :], m2[:, n, :], ACT.Square).then_inc(sem("squared"), 1)
                act.wait_ge(sem("x_again"), n + 1)
                t, half = divmod(n, 2)
                act.copy(h[:, 4 * half:4 * half + 4, t * P:(t + 1) * P],
                         bank(4 + half).rearrange("p (k n) -> p k n", k=4)).then_inc(sem("h_x"), 1)
            act_stats(act, "out")
            for n in range(KT):
                act.wait_ge(sem("h_tile"), n + 1)
                act.activation(u[:, n, HI, META:LEN], h[:, n, :], ACT.Copy, scale=vcol("mix_g", n)) \
                    .then_inc(sem("hs_hi"), 1)
                if n >= 2:
                    act.wait_ge(sem("acc_done"), KT + n - 1)
                act.activation(sq[:, n % 2, :], h[:, n, :], ACT.Square).then_inc(sem("squared"), 1)

        def dve_out(dve):
            for k in range(KT):
                dve.wait_ge(sem("mr_hi"), k + 1)
                dve.tensor_tensor(u[:, k, LO, META:LEN], h[:, k, :], u[:, k, HI, META:LEN], ALU.subtract) \
                    .then_inc(sem("mr_lo"), 1)
            for n in range(KT):
                dve.wait_ge(sem("w_used"), OUT + n + 1)
                dve.tensor_copy(m2[:, n, :], bank(n % 4)).then_inc(sem("m2"), 1)
                w_lo(dve, OUT + n + 2)
            dve_stats(dve, "out")
            dve.wait_ge(sem("h_x"), KT)
            for n in range(KT):
                if n >= 2:
                    dve.wait_ge(sem("h_tile"), n - 1)
                dve.tensor_tensor(res_t[:, n % 2, :], m2[:, n, :], rbc[:, 0, :], ALU.mult).then_inc(sem("res"), 1)
                dve.wait_ge(sem("res"), n + 1)
                dve.scalar_tensor_tensor(out=h[:, n, :], in0=res_t[:, n % 2, :], scalar=vcol("post_g", n),
                                         in1=h[:, n, :], op0=ALU.mult, op1=ALU.add).then_inc(sem("h_tile"), 1)
                dve.wait_ge(sem("hs_hi"), n + 1)
                dve.scalar_tensor_tensor(out=u[:, n, LO, META:LEN], in0=h[:, n, :], scalar=vcol("mix_g", n),
                                         in1=u[:, n, HI, META:LEN], op0=ALU.mult, op1=ALU.subtract) \
                    .then_inc(sem("hs"), 1)

        EV = FIRST["even"]
        CH = 4 * P

        def load_even(sp):
            w = a["w_in_even_2"][0]
            for g in range(GROUPS):
                for j, col in enumerate((CH, 2 * CH, 0, 3 * CH)):
                    w_load(sp, EV + 4 * g + j, panel(w, col + g * P))
            wp = a["w_pool_2"][0]
            w_load(sp, FIRST["pool"], [
                (lambda r, lo=lo: r[:, lo * P:(lo + 2) * P].rearrange("p (g n) -> p g n", g=2),
                 wp[lo:lo + 2].rearrange("g p n -> p g n")) for lo in (0, 2)])

        def pe_even(pe):
            pe.wait_ge(sem("hs"), KT)
            for g in range(GROUPS):
                for j in range(4):
                    w_ready(pe, EV + 4 * g + j)
                    if g:
                        pe.wait_ge(sem("e_read"), 4 * (g - 1) + j + 1)
                    product(pe, bank(j), EV + 4 * g + j, u_real).then_inc(sem("w_used"), 1)
                    if g == 0 and j == 0:
                        pe_stats(pe, "e")
            c = FIRST["pool"]
            w_ready(pe, c)
            for g in range(GROUPS):
                pe.wait_ge(sem("pooled"), g + 1)
                pe.wait_ge(sem("e_read"), 4 * (GROUPS - 1) + g + 1)
                for n, (ws, ms) in enumerate(PASSES):
                    ins = pe.matmul(bank(g), w_tile(c, ws, g), pool_r[:, g, ms, :], start=n == 0, stop=n == 2)
                ins.then_inc(sem("pool_mm" if g < GROUPS - 1 else "w_used"), 1)

        def act_even(act):
            for g in range(GROUPS):
                c = EV + 4 * g
                if g == 0:
                    act_stats(act, "e")
                w_hi(act, c + 2)
                act.wait_ge(sem("e_cv"), g + 1)
                act.activation(ecv[:, 0, :], cpad[:, 0, 0:SEQ], ACT.Copy, scale=vcol("conv_a", g)).then_inc(sem("e_t0"), 1)
                w_hi(act, c + 3)
                w_hi(act, c + 4)
                act.wait_ge(sem("e_y"), g + 1)
                act.copy(mix_r[:, g, HI, :], ecv[:, 0, :]).then_inc(sem("e_yhi"), 1)
                w_hi(act, c + 5)
                act.wait_ge(sem("e_p"), g + 1)
                act.copy(pool_r[:, g, HI, :], zf[:, 0, :]).then_inc(sem("e_phi"), 1)
            for g in range(GROUPS):
                if g < GROUPS - 1:
                    act.wait_ge(sem("pool_mm"), g + 1)
                else:
                    act.wait_ge(sem("w_used"), FIRST["pool"] + 1)
                act.activation(mix_r[:, GROUPS + g, HI, :], bank(g), ACT.Copy, scale=vcol("pool_scale", g)) \
                    .then_inc(sem("e_mhi"), 1)
            w_hi(act, FIRST["pool"] + 2)

        def dve_even(dve):
            chain = [0]

            def link(ins):
                chain[0] += 1
                ins.then_inc(sem("e_chain"), 1)
                dve.wait_ge(sem("e_chain"), chain[0])

            dve.memset(cpad[:, 0, 0:2], 0.0)
            link(dve.memset(zpad[:, :, 0:8], 0.0))
            for g in range(GROUPS):
                c = EV + 4 * g
                w = 2 ** (g + 1)
                r = rbc[:, 0, :]
                if g == 0:
                    dve_stats(dve, "e")
                w_lo(dve, c + 2)
                dve.wait_ge(sem("w_used"), c + 1)
                if g:
                    dve.wait_ge(sem("e_t0"), g)
                ins = dve.tensor_tensor(cpad[:, 0, 2:2 + SEQ], bank(0), r, ALU.mult)
                ins.then_inc(sem("e_read"), 1)
                dve.wait_ge(sem("e_read"), 4 * g + 1)
                dve.wait_ge(sem("w_used"), c + 2)
                dve.tensor_tensor(cpad[:, 0, 2:2 + SEQ], bank(1), cpad[:, 0, 2:2 + SEQ], ALU.mult).then_inc(sem("e_read"), 1)
                dve.wait_ge(sem("e_read"), 4 * g + 2)
                dve.tensor_tensor(cpad[:, 0, 2:2 + SEQ], cpad[:, 0, 2:2 + SEQ], r, ALU.mult).then_inc(sem("e_cv"), 1)
                w_lo(dve, c + 3)
                dve.wait_ge(sem("e_t0"), g + 1)
                for tap in (1, 2):
                    link(dve.scalar_tensor_tensor(out=ecv[:, 0, :], in0=cpad[:, 0, tap:tap + SEQ],
                                                  scalar=vcol("conv_a", 4 * tap + g), in1=ecv[:, 0, :],
                                                  op0=ALU.mult, op1=ALU.add))
                w_lo(dve, c + 4)
                dve.wait_ge(sem("w_used"), c + 3)
                dve.tensor_tensor(ecv[:, 0, :], bank(2), ecv[:, 0, :], ALU.mult).then_inc(sem("e_read"), 1)
                dve.wait_ge(sem("e_read"), 4 * g + 3)
                dve.tensor_tensor(ecv[:, 0, :], ecv[:, 0, :], r, ALU.mult).then_inc(sem("e_y"), 1)
                dve.wait_ge(sem("e_yhi"), g + 1)
                link(dve.tensor_tensor(mix_r[:, g, LO, :], ecv[:, 0, :], mix_r[:, g, HI, :], ALU.subtract))
                w_lo(dve, c + 5)
                dve.wait_ge(sem("w_used"), c + 4)
                if g:
                    dve.wait_ge(sem("e_phi"), g)
                dve.tensor_tensor(zpad[:, 0, 8:8 + SEQ], bank(3), r, ALU.mult).then_inc(sem("e_read"), 1)
                dve.wait_ge(sem("e_read"), 4 * g + 4)
                link(dve.tensor_copy(zf[:, 0, :], zpad[:, 0, 8:8 + SEQ]))
                src = 0
                for d in [2 ** e for e in range(g + 1)]:
                    link(dve.tensor_tensor(zpad[:, 1 - src, 8:8 + SEQ], zpad[:, src, 8:8 + SEQ],
                                           zpad[:, src, 8 - d:8 - d + SEQ], ALU.add))
                    src = 1 - src
                s_ = zpad[:, src, 8:8 + SEQ]
                head = w - 1
                link(dve.tensor_tensor(zpad[:, 1 - src, 8:8 + head], s_[:, 0:head], inv_count[:, 0:head], ALU.mult))
                link(dve.tensor_scalar(zpad[:, 1 - src, 8 + head:8 + SEQ], s_[:, head:SEQ], 1.0 / w, None, ALU.mult))
                dve.tensor_tensor(zf[:, 0, :], zpad[:, 1 - src, 8:8 + SEQ], zf[:, 0, :], ALU.subtract) \
                    .then_inc(sem("e_p"), 1)
                dve.wait_ge(sem("e_phi"), g + 1)
                dve.tensor_tensor(pool_r[:, g, LO, :], zf[:, 0, :], pool_r[:, g, HI, :], ALU.subtract) \
                    .then_inc(sem("pooled"), 1)
            for g in range(GROUPS):
                dve.wait_ge(sem("e_mhi"), g + 1)
                dve.scalar_tensor_tensor(out=mix_r[:, GROUPS + g, LO, :], in0=bank(g), scalar=vcol("pool_scale", g),
                                         in1=mix_r[:, GROUPS + g, HI, :], op0=ALU.mult, op1=ALU.subtract) \
                    .then_inc(sem("e_mix"), 1)
            w_lo(dve, FIRST["pool"] + 2)

        def before_even_out(pe):
            pe.wait_ge(sem("e_mix"), GROUPS)

        def load_ffn(sp, layer):
            c0 = FIRST[("ffn", layer)]

            def body(i, first, last):
                for j in range(4):
                    w = a["w_ffn_gate_2" if j % 2 == 0 else "w_ffn_up_2"][layer]
                    w_load(sp, c0 + j, panel(w, (2 * i + j // 2) * P), i, 4)
            loop(sp, FT // 2, body)

        def pe_ffn(pe, layer, tag):
            c0 = FIRST[("ffn", layer)]
            pe.wait_ge(sem("hs"), hs_before(tag) + KT)

            def body(i, first, last):
                for j in range(4):
                    w_ready(pe, c0 + j, i, 4)
                    if not first:
                        f = 2 * i + j // 2
                        pe.wait_ge(sem("ffn_g_read" if j % 2 == 0 else "ffn_a_done"), FT * layer + f - 1)
                    product(pe, bank(j), c0 + j, u_real).then_inc(sem("w_used"), 1)
                    if first and j == 0:
                        pe_stats(pe, tag)
            loop(pe, FT // 2, body)

        def act_ffn(act, layer, tag):
            c0 = FIRST[("ffn", layer)]
            act_stats(act, tag)

            def body(i, first, last):
                for j in range(2):
                    f = 2 * i + j
                    c = c0 + 2 * j
                    act.wait_ge(sem("w_used"), num(c, i, 4) + 1)
                    w_hi(act, c + 2 + i * 4) if last and j else w_hi(act, c + 2, i, 4, "full")
                    act.wait_ge(sem("ffn_g_read"), FT * layer + f + 1)
                    if not first:
                        act.wait_ge(sem("ffn_a_done"), FT * layer + f - 1)
                    act.activation(cnv[:, j, :], gpad[:, j, 0:SEQ], ACT.Copy, scale=ffn_vec(layer, 0, f)) \
                        .then_inc(sem("ffn_tap"), 1)
                    act.wait_ge(sem("ffn_conv"), 2 * FT * layer + 2 * f + 2)
                    act.activation(cnv[:, j, :], cnv[:, j, :], ACT.Silu, bias=ffn_vec(layer, 3, f)) \
                        .then_inc(sem("ffn_silu"), 1)
                    act.wait_ge(sem("w_used"), num(c + 1, i, 4) + 1)
                    w_hi(act, c + 3 + i * 4) if last and j else w_hi(act, c + 3, i, 4, "full")
                    act.wait_ge(sem("ffn_a_done"), FT * layer + f + 1)
                    dst = a_r[:, idx(f), HI, :]
                    act.copy(dst, hid[:, 0, :] if isinstance(f, int) else hid[:, 0:1, :]).then_inc(sem("ffn_a_hi"), 1)
            loop(act, FT // 2, body)

        def pool_ffn(pool, layer, tag):
            pool.wait_ge(sem("rbc"), norms_done(tag))

            def body(i, first, last):
                for j in range(2):
                    pool.wait_ge(sem("ffn_silu"), FT * layer + 2 * i + j + 1)
                    pool.tensor_tensor(cnv[:, j, :], cnv[:, j, :], rbc[:, 0, :], ALU.mult) \
                        .then_inc(sem("ffn_scaled"), 1)
            loop(pool, FT // 2, body)

        def dve_ffn(dve, layer, tag):
            c0 = FIRST[("ffn", layer)]
            dve_stats(dve, tag)
            dve.memset(gpad[:, :, 0:2], 0.0).then_inc(sem("ffn_gz"), 1)

            def body(i, first, last):
                for j in range(2):
                    f = 2 * i + j
                    c = c0 + 2 * j
                    dve.wait_ge(sem("w_used"), num(c, i, 4) + 1)
                    if not first:
                        dve.wait_ge(sem("ffn_conv"), 2 * FT * layer + 2 * f - 2)
                    dve.tensor_tensor(gpad[:, j, 2:2 + SEQ], bank(2 * j), rbc[:, 0, :], ALU.mult) \
                        .then_inc(sem("ffn_g_read"), 1)
                    w_lo(dve, c + 2 + i * 4) if last and j else w_lo(dve, c + 2, i, 4, "full")
                    dve.wait_ge(sem("ffn_tap"), FT * layer + f + 1)
                    for tap in (1, 2):
                        dve.scalar_tensor_tensor(out=cnv[:, j, :], in0=gpad[:, j, tap:tap + SEQ],
                                                 scalar=ffn_vec(layer, tap, f), in1=cnv[:, j, :],
                                                 op0=ALU.mult, op1=ALU.add).then_inc(sem("ffn_conv"), 1)
                        if tap == 1:
                            dve.wait_ge(sem("ffn_conv"), 2 * FT * layer + 2 * f + 1)
                    w_lo(dve, c + 3 + i * 4) if last and j else w_lo(dve, c + 3, i, 4, "full")
                    dve.wait_ge(sem("ffn_scaled"), FT * layer + f + 1)
                    dve.wait_ge(sem("w_used"), num(c + 1, i, 4) + 1)
                    if not (first and j == 0):
                        dve.wait_ge(sem("ffn_a_lo"), FT * layer + f)
                    dve.tensor_tensor(hid[:, 0, :], bank(2 * j + 1), cnv[:, j, :], ALU.mult) \
                        .then_inc(sem("ffn_a_done"), 1)
                    dve.wait_ge(sem("ffn_a_hi"), FT * layer + f + 1)
                    hi, lo = (a_r[:, idx(f), part, :] for part in (HI, LO))
                    hv = hid[:, 0, :] if isinstance(f, int) else hid[:, 0:1, :]
                    dve.tensor_tensor(lo, hv, hi, ALU.subtract).then_inc(sem("ffn_a_lo"), 1)
            loop(dve, FT // 2, body)

        OV, OU = FIRST["odd_v"], FIRST["odd_u"]

        def load_odd(sp):
            w = a["w_in_odd_2"][0]
            for n in range(2):
                w_load(sp, OV + n, panel(w, D + n * P))
            sp.wait_ge(sem("h_tile"), hs_before("down0") + KT)
            sp.dma_start(bbc[:, 0, :], a["b_spatial_2"].rearrange("a h t -> a (h t)").to_broadcast([P, D])) \
                .then_inc(sem("b_in"), 16)
            sp.dma_start(m2[:, 0:2, :].rearrange("p a (b s) -> p (a b) s", s=P),
                         a["w_spatial_2"][0].rearrange("h t s -> t h s")).then_inc(sem("ws_in"), 16)
            for n in range(2, KT):
                w_load(sp, OV + n, panel(w, D + n * P))
            for n in range(KT):
                w_load(sp, OU + n, panel(w, n * P))

        def pe_odd(pe):
            pe.wait_ge(sem("ws_in"), 16)
            pe.wait_ge(sem("h_tile"), hs_before("down0") + KT)
            wn = m2[:, 0:2, :].rearrange("p a (b s) -> p (a b) s", s=P)
            for hd in range(C_HEADS):
                ins = pe.transpose(bank(4 + hd // 4, (hd % 4) * P, (hd % 4 + 1) * P), wn[:, hd, :], ident)
            ins.then_inc(sem("ws_t"), 1)
            pe.wait_ge(sem("hs"), hs_before("down0") + KT)
            for n in range(KT):
                w_ready(pe, OV + n)
                if n >= 4:
                    pe.wait_ge(sem("ov_read"), 4 * (n - 3))
                for t in range(NQ):
                    total = [(k, us, ws) for k in range(KT) for us, ws in PASSES]
                    for m, (k, us, ws) in enumerate(total):
                        ins = pe.matmul(bank(n % 4, t * P, (t + 1) * P), u[:, k, us, META + t * P:META + (t + 1) * P],
                                        w_tile(OV + n, ws, k), start=m == 0, stop=m == len(total) - 1)
                ins.then_inc(sem("w_used"), 1)
                if n == 0:
                    pe_stats(pe, "down0", bc=True, tok=True)
            for n in range(KT):
                w_ready(pe, OU + n)
                pe.wait_ge(sem("ov_read"), 4 * min(n + 5, KT)) if n < 4 else pe.wait_ge(sem("ou_read"), n - 3)
                product(pe, bank(n % 4), OU + n, u_real).then_inc(sem("w_used"), 1)
            pe.wait_ge(sem("vs_lo"), KT)
            for t in range(NQ):
                pe.wait_ge(sem("ws_lo"), t + 1)
                for half in range(2):
                    b = 4 + 2 * (t % 2) + half
                    if t >= 2:
                        pe.wait_ge(sem("gate"), 2 * (t - 2) + half + 1)
                    for q in range(4):
                        hd = 4 * half + q
                        for m, (vs, ws) in enumerate(PASSES):
                            ins = pe.matmul(bank(b, q * P, (q + 1) * P), vs_r[:, t, vs, hd * P:(hd + 1) * P],
                                            ws_r[:, t % 2, ws, hd * P:(hd + 1) * P], start=m == 0, stop=m == 2)
                    ins.then_inc(sem("sgu"), 1)

        def act_odd(act):
            act_stats(act, "down0", bc=True, tok=True)
            for n in range(KT):
                act.wait_ge(sem("w_used"), OV + n + 1)
                w_hi(act, OV + n + 2)
                if n == 0:
                    act.wait_ge(sem("rtok"), 1)
                if n:
                    act.wait_ge(sem("vs_lo"), n)
                for t in range(NQ):
                    act.activation(odt[:, 0, t * P:(t + 1) * P], bank(n % 4, t * P, (t + 1) * P), ACT.Gelu,
                                   scale=rtok[:, t:t + 1]).then_inc(sem("ov_read"), 1)
                act.wait_ge(sem("ov_read"), 4 * n + 4)
                act.copy(vs_r[:, :, HI, n * P:(n + 1) * P], odt[:, 0, :].rearrange("p (t n) -> p t n", t=NQ)) \
                    .then_inc(sem("vs_hi"), 1)
            for n in range(KT):
                act.wait_ge(sem("w_used"), OU + n + 1)
                w_hi(act, OU + n + 2)
                act.wait_ge(sem("ou_read"), n + 1)
                act.activation(m2[:, n, :], m2[:, n, :], ACT.Gelu).then_inc(sem("ou"), 1)
            act.wait_ge(sem("ssv"), 1)
            act.activation(ssv, ssv, ACT.Sqrt, scale=1.0 / D, bias=EPS).then_inc(sem("sdv"), 1)
            for t in range(NQ):
                act.wait_ge(sem("rsv"), 1)
                act.wait_ge(sem("wst"), 2)
                if t >= 2:
                    act.wait_ge(sem("sgu"), 2 * (t - 1))
                act.activation(ws_r[:, t % 2, HI, :], wst[:, 0, :], ACT.Copy, scale=rsv[:, t:t + 1]) \
                    .then_inc(sem("ws_hi"), 1)
            for t in range(NQ):
                for half in range(2):
                    n = 2 * t + half
                    act.wait_ge(sem("gate_y"), n + 1)
                    act.copy(mix_r[:, 4 * half:4 * half + 4, HI, t * P:(t + 1) * P],
                             odt[:, half, :].rearrange("p (k n) -> p k n", k=4)).then_inc(sem("gate_hi"), 1)

        def dve_odd(dve):
            dve.wait_ge(sem("ws_t"), 1)
            dve.wait_ge(sem("b_in"), 16)
            for half in range(2):
                dve.tensor_tensor(wst[:, 0, half * 512:(half + 1) * 512].rearrange("p (h n) -> p h n", h=4),
                                  bank(4 + half).rearrange("p (h n) -> p h n", h=4),
                                  triu.rearrange("p (a n) -> p a n", a=1).to_broadcast([P, 4, P]), ALU.mult) \
                    .then_inc(sem("wst"), 1)
            dve_stats(dve, "down0", bc=True, tok=True)
            sqv = sq[:, 0, :]
            part = st[:, 10:42].rearrange("p (n t) -> p n t", t=NQ)
            for n in range(KT):
                w_lo(dve, OV + n + 2)
                dve.wait_ge(sem("vs_hi"), n + 1)
                v3 = odt[:, 0, :].rearrange("p (t n) -> p t n", t=NQ)
                dve.wait_ge(sem("sqv"), 2 * n) if n else None
                dve.tensor_tensor(sqv, odt[:, 0, :], odt[:, 0, :], ALU.mult).then_inc(sem("sqv"), 1)
                dve.tensor_tensor(vs_r[:, :, LO, n * P:(n + 1) * P], v3, vs_r[:, :, HI, n * P:(n + 1) * P],
                                  ALU.subtract).then_inc(sem("vs_lo"), 1)
                dve.wait_ge(sem("sqv"), 2 * n + 1)
                dve.reduce_sum(part[:, n, :], sqv.rearrange("p (t n) -> p t n", t=NQ), AX.X).then_inc(sem("sqv"), 1)
            dve.wait_ge(sem("sqv"), 2 * KT)
            dve.reduce_sum(ssv, part.rearrange("p n t -> p t n"), AX.X).then_inc(sem("ssv"), 1)
            for n in range(KT):
                w_lo(dve, OU + n + 2)
                dve.wait_ge(sem("w_used"), OU + n + 1)
                if n == 0:
                    dve.wait_ge(sem("wst"), 2)
                dve.tensor_tensor(m2[:, n, :], bank(n % 4), rbc[:, 0, :], ALU.mult).then_inc(sem("ou_read"), 1)
            dve.wait_ge(sem("sdv"), 1)
            dve.reciprocal(rsv, ssv).then_inc(sem("rsv"), 1)
            dve.wait_ge(sem("rsv"), 1)
            dve.wait_ge(sem("ou"), KT)

            def ws_low(t):
                dve.wait_ge(sem("ws_hi"), t + 1)
                dve.scalar_tensor_tensor(out=ws_r[:, t % 2, LO, :], in0=wst[:, 0, :], scalar=rsv[:, t:t + 1],
                                         in1=ws_r[:, t % 2, HI, :], op0=ALU.mult, op1=ALU.subtract) \
                    .then_inc(sem("ws_lo"), 1)

            ws_low(0)
            ws_low(1)
            for t in range(NQ):
                for half in range(2):
                    n = 2 * t + half
                    b = 4 + 2 * (t % 2) + half
                    dve.wait_ge(sem("sgu"), n + 1)
                    if n >= 2:
                        dve.wait_ge(sem("gate_lo"), n - 1)
                    for q in range(4):
                        hd = 4 * half + q
                        ins = dve.scalar_tensor_tensor(out=odt[:, half, q * P:(q + 1) * P],
                                                       in0=bank(b, q * P, (q + 1) * P), scalar=vcol("sgu_g", hd),
                                                       in1=bbc[:, 0, hd * P:(hd + 1) * P], op0=ALU.mult, op1=ALU.add)
                    ins.then_inc(sem("gate"), 1)
                    dve.wait_ge(sem("gate"), n + 1)
                    y = odt[:, half, :].rearrange("p (k n) -> p k n", k=4)
                    dve.tensor_tensor(y, y, m2[:, 4 * half:4 * half + 4, t * P:(t + 1) * P], ALU.mult) \
                        .then_inc(sem("gate_y"), 1)
                    dve.wait_ge(sem("gate_hi"), n + 1)
                    dve.tensor_tensor(mix_r[:, 4 * half:4 * half + 4, LO, t * P:(t + 1) * P], y,
                                      mix_r[:, 4 * half:4 * half + 4, HI, t * P:(t + 1) * P], ALU.subtract) \
                        .then_inc(sem("gate_lo"), 1)
                if t + 2 < NQ:
                    ws_low(t + 2)

        def before_odd_out(pe):
            pe.wait_ge(sem("gate_lo"), 2 * NQ)

        def load_final(sp):
            sp.wait_ge(sem("ffn_a_lo"), 2 * FT)
            sp.dma_start(gfin[:, 0, :], a["final_norm_2"].rearrange("(a n) -> a n", a=1).to_broadcast([P, D])) \
                .then_inc(sem("gf_in"), 16)
            for t in range(NQ):
                sp.wait_ge(sem("fin"), 2 * t + 2)
                sp.dma_start(out[t * P:(t + 1) * P, :], xin[:, t % 2, :]).then_inc(sem(f"stored{t % 2}"), 16)
            for s in range(2):
                sp.wait_ge(sem(f"stored{s}"), 32)

        def pe_final(pe):
            pe.wait_ge(sem("h_tile"), hs_before("down1") + KT)
            for t in range(NQ):
                for half in range(2):
                    n = 2 * t + half
                    if n >= 4:
                        pe.wait_ge(sem("fin_s"), n - 3)
                    for k in range(4):
                        ins = pe.transpose(bank(2 + n % 4, k * P, (k + 1) * P), h[:, 4 * half + k, t * P:(t + 1) * P],
                                           ident)
                    ins.then_inc(sem("fin_t"), 1)
                if t == 0:
                    pe_stats(pe, "down1", bc=False, tok=True)

        def act_final(act):
            act_stats(act, "down1", bc=False, tok=True)
            act.wait_ge(sem("rtok"), 2)
            for t in range(NQ):
                for half in range(2):
                    n = 2 * t + half
                    act.wait_ge(sem("fin_t"), n + 1)
                    if t >= 2:
                        act.wait_ge(sem(f"stored{t % 2}"), 16)
                    act.activation(xin[:, t % 2, half * 512:(half + 1) * 512], bank(2 + n % 4), ACT.Copy,
                                   scale=rtok[:, t:t + 1]).then_inc(sem("fin_s"), 1)

        def dve_final(dve):
            dve_stats(dve, "down1", bc=False, tok=True)
            dve.wait_ge(sem("gf_in"), 16)
            for n in range(2 * NQ):
                t, half = divmod(n, 2)
                dve.wait_ge(sem("fin_s"), n + 1)
                o = xin[:, t % 2, half * 512:(half + 1) * 512]
                dve.tensor_tensor(o, o, gfin[:, 0, half * 512:(half + 1) * 512], ALU.mult).then_inc(sem("fin"), 1)

        def a_tiles(k, part):
            return a_r[:, k, part, :]

        def mix_tiles(k, part):
            return mix_r[:, k, part, :]

        block = ctx.enter_context(nc.Block())

        @block.sync
        def _(sp):
            dma_prologue(sp)
            load_prologue(sp)
            load_attention(sp)
            load_mix(sp)
            load_out(sp)
            load_even(sp)
            load_residual(sp, "even_out", a["w_out_even_2"][0])
            load_ffn(sp, 0)
            load_residual(sp, ("down", 0), a["w_ffn_down_2"][0])
            load_odd(sp)
            load_residual(sp, "odd_out", a["w_out_odd_2"][0])
            load_ffn(sp, 1)
            load_residual(sp, ("down", 1), a["w_ffn_down_2"][1])
            load_final(sp)

        @block.gpsimd
        def _(pool):
            pool_prologue(pool)
            pool_rows(pool, 0)
            with pool.Fori(1, PAIRS) as g:
                pool_rows(pool, g)
            pool_squares(pool, "out")
            pool_squares(pool, "e")
            pool_squares(pool, "eo")
            pool_ffn(pool, 0, "eo")
            pool_squares(pool, "down0")
            pool_squares(pool, "oo")
            pool_ffn(pool, 1, "oo")
            pool_squares(pool, "down1")

        @block.scalar
        def _(act):
            act_prologue(act)
            steps(act, lambda *x: act_step(act, *x))
            act_mix(act)
            act_out(act)
            act_even(act)
            act_residual(act, "even_out", ("ffn_g", 0), "eo")
            act_ffn(act, 0, "eo")
            act_residual(act, ("down", 0), ("mix_g", KT), "down0")
            act_odd(act)
            act_residual(act, "odd_out", ("ffn_g", KT), "oo")
            act_ffn(act, 1, "oo")
            act_residual(act, ("down", 1), None, "down1")
            act_final(act)

        @block.vector
        def _(dve):
            dve_prologue(dve)
            steps(dve, lambda *x: dve_step(dve, *x))
            dve_mix(dve)
            dve_out(dve)
            dve_even(dve)
            dve_residual(dve, "even_out", ("ffn_g", 0), "eo")
            dve_ffn(dve, 0, "eo")
            dve_residual(dve, ("down", 0), ("mix_g", KT), "down0")
            dve_odd(dve)
            dve_residual(dve, "odd_out", ("ffn_g", KT), "oo")
            dve_ffn(dve, 1, "oo")
            dve_residual(dve, ("down", 1), None, "down1")
            dve_final(dve)

        @block.tensor
        def _(pe):
            pe_prologue(pe)
            steps(pe, lambda *x: pe_step(pe, *x[:6]))
            pe_mix(pe)
            pe_out(pe)
            pe_even(pe)
            pe_residual(pe, "even_out", mix_tiles, before_even_out, "eo")
            pe_ffn(pe, 0, "eo")
            pe_residual(pe, ("down", 0), a_tiles, lambda e: e.wait_ge(sem("ffn_a_lo"), FT), "down0")
            pe_odd(pe)
            pe_residual(pe, "odd_out", mix_tiles, before_odd_out, "oo")
            pe_ffn(pe, 1, "oo")
            pe_residual(pe, ("down", 1), a_tiles, lambda e: e.wait_ge(sem("ffn_a_lo"), 2 * FT), "down1")
            pe_final(pe)


def rope_tables():
    half = ROPE // 2
    freq = (np.float32(ROPE_THETA) ** (-np.arange(half, dtype=np.float32) / np.float32(half))).astype(np.float32)
    ang = np.arange(LEN, dtype=np.float32)[None, :] * freq[:, None]
    cos, sin = np.cos(ang).astype(np.float32), np.sin(ang).astype(np.float32)
    return np.concatenate([cos, cos, -sin, sin], axis=0)


def constant_tables():
    i = np.arange(P)
    ident = np.eye(P, dtype=np.float32)
    mask = np.where(i[None, :] > i[:, None], np.float32(MASKED), np.float32(0.0)).astype(np.float32)
    triu = (i[:, None] <= i[None, :]).astype(np.float32)
    counts = np.broadcast_to((np.float32(1.0) / (np.arange(16, dtype=np.float32) + 1)), (P, 16))
    return np.ascontiguousarray(np.concatenate([ident, mask, triu, counts], axis=1))


_INS = ["x", "meta_tokens", "pre_norm_g", "w_in", "fox_forget_b", "mla_q_norm_g", "mla_kv_norm_g", "w_uq",
        "w_ukv", "w_br_mla", "w_br_fox", "w_out", "post_norm_g", "norm_mix_2", "norm_ffn_2", "final_norm_2",
        "w_in_even_2", "conv_a_2", "w_pool_2", "pool_scale_2", "w_out_even_2", "w_in_odd_2", "sgu_norm_2",
        "w_spatial_2", "b_spatial_2", "w_out_odd_2", "w_ffn_gate_2", "w_ffn_up_2", "conv_ffn_2",
        "b_conv_ffn_2", "w_ffn_down_2"]


def kernel(**inputs):
    import concourse.bacc as _bacc
    from concourse.bass_utils import run_bass_kernel_spmd as _run

    nc = _bacc.Bacc("TRN2", target_bir_lowering=False, num_devices=1)
    arrays, aps = {}, {}

    def declare(name, array):
        arrays[f"in_{name}_dram"] = array
        return nc.dram_tensor(f"in_{name}_dram", array.shape, mybir.dt.from_np(array.dtype),
                              kind="ExternalInput").ap()

    for name in _INS:
        aps[name] = declare(name, np.ascontiguousarray(inputs[name]))
    rope = declare("rope_tables", rope_tables())
    consts = declare("constants", constant_tables())
    out = nc.dram_tensor("out_dram", (1, SEQ, D), F32, kind="ExternalOutput").ap()
    hybrid_blocks_kernel(nc, aps, rope, consts, out[0])
    r = _run(nc, [arrays], core_ids=[0])
    return r.results[0]["out_dram"]
```

```python
from contextlib import ExitStack
import math

import numpy as np

import concourse.bass as bass
from concourse import mybir

F32 = mybir.dt.float32
F32R = mybir.dt.float32r
ACT = mybir.ActivationFunctionType
ALU = mybir.AluOpType
AX = mybir.AxisListType

P = 128
D = 1024
KT = D // P
SEQ = 512
META = 16
LEN = SEQ + META
HALF = LEN // 2
NQ = SEQ // P
EPS = 1e-6
HEADS = 16
PAIRS = HEADS // 2
STEPS = 2 * PAIRS
NOPE, ROPE = 64, 32
HD = 64
Q_RANK, KV_RANK = 256, 128
MLA_SCALE = 1.0 / math.sqrt(NOPE + ROPE)
FOX_SCALE = 1.0 / math.sqrt(HD)
ROPE_THETA = 10000.0
MASKED = -1e30
W_CQ = 0
W_CKV = W_CQ + Q_RANK
W_KPE = W_CKV + KV_RANK
W_ZM = W_KPE + ROPE
W_FQ = W_ZM + D
W_FK = W_FQ + D
W_FV = W_FK + D
W_F = W_FV + D
W_ZF = W_F + HEADS
W_GA = W_ZF + D
W_GB = W_GA + D
GROUPS = 4
DFF = 2816
FT = DFF // P
DOWN = (8, 8, 6)
C_HEADS = 8
UNIT = KT * P
VEC_ROWS = (("pre_g", 8), ("q_g", 2), ("kv_g", 1), ("post_g", 8), ("mix_g", 16), ("ffn_g", 16),
            ("pool_scale", 4), ("sgu_g", 8), ("conv_a", 12))
FFN_ROWS = 4 * FT

B_S, B_T, B_O, B_META = 4, 6, 7, 3
V_META = 256
ARENA = 2 * 2 * 2 * SEQ + 2 * 2 * 2 * LEN + 4 * NQ * P + 2 * P + 4 * NQ * SEQ + 2 * SEQ + 4 * SEQ + 2 * LEN


def vec_column(name, k=0):
    at = 0
    for n, rows in VEC_ROWS:
        if n == name:
            return at + k
        at += rows
    raise KeyError(name)


N_VEC = sum(r for _, r in VEC_ROWS)


def plan_units():
    kinds, first = [], {}

    def phase(name, *ks):
        first[name] = len(kinds)
        kinds.extend(ks)

    phase("pro", "full", "kpe", "full", "full", "full")
    for s in range(STEPS):
        phase(("attn", s), *(("full", "qkv", "full") if s < PAIRS else ("full",) * 3))
    phase("mix", *("full",) * (4 * KT))
    phase("out", *("full",) * KT)
    phase("even_z", *("full",) * GROUPS)
    phase("even_c", *("full",) * 3)
    phase("pool", "pool")
    phase("even_c1", *("full",) * (3 * (GROUPS - 1)))
    phase("even_out", *("full",) * KT)
    phase(("ffn", 0), *("full",) * (2 * FT))
    phase(("down", 0), *("full", "full", "six") * KT)
    phase("odd_v", *("full",) * KT)
    phase("odd_u", *("full",) * KT)
    phase("odd_out", *("full",) * KT)
    phase(("ffn", 1), *("full",) * (2 * FT))
    phase(("down", 1), *("full", "full", "six") * KT)
    return kinds, first


KINDS, FIRST = plan_units()


def hybrid_blocks_kernel(nc, a, rope_t, consts, out):
    forget_dram = nc.dram_tensor("forget_rows", [2, HEADS, 2, LEN], F32, kind="Internal").ap()

    with ExitStack() as ctx:
        def sb(name, shape, dt=F32):
            return ctx.enter_context(nc.sbuf_tensor(name, shape, dt))

        sems = {}

        def sem(name):
            if name not in sems:
                sems[name] = ctx.enter_context(nc.semaphore(name))
            return sems[name]

        ps = ctx.enter_context(nc.psum_tensor("ps", [P, 8 * 512], F32))

        def bank(b, lo=0, hi=512, rows=slice(0, P)):
            return ps[rows, b * 512 + lo:b * 512 + hi]

        raw = sb("w_raw", [P, 2, UNIT])
        wsp = sb("w_split", [P, 2, 2, UNIT], F32R)
        u = sb("u", [P, KT, 2, LEN], F32R)
        ra = sb("arena_r", [P, ARENA], F32R)
        big = sb("big", [P, 16, SEQ])
        tmp = sb("tmp", [P, 5120])
        cst = sb("cst", [P, 400])
        ident_r = sb("ident_r", [P, P], F32R)
        mask_r = sb("mask_r", [P, P], F32R)
        ones = sb("ones", [P, P])
        vec = sb("vec", [P, N_VEC + 2 * FFN_ROWS])
        st = sb("stats", [P, 64])
        ident = cst[:, 0:128]
        triu = cst[:, 256:384]
        inv_count = cst[:, 384:400]

        def view(t, at, *dims):
            n = math.prod(dims)
            v = t[:, at:at + n]
            if len(dims) == 2:
                v = v.rearrange("p (a b) -> p a b", a=dims[0])
            elif len(dims) == 3:
                v = v.rearrange("p (a b c) -> p a b c", a=dims[0], b=dims[1])
            elif len(dims) == 4:
                v = v.rearrange("p (a b c d) -> p a b c d", a=dims[0], b=dims[1], c=dims[2])
            return v, at + n

        q_t, at = view(ra, 0, 4, 2, SEQ)
        k_t, at = view(ra, at, 4, 2, LEN)
        v_t, at = view(ra, at, 2, NQ, 2, P)
        v_m, at = view(ra, at, 2, P)
        p_t, at = view(ra, at, 2, 2 * NQ, SEQ)
        p_m, at = view(ra, at, 2, SEQ)
        cq_r, at = view(ra, at, 2, 2, SEQ)
        ckv_r, at = view(ra, at, 2, LEN)
        o_r, _ = view(ra, 0, 16, 2, SEQ)
        mix_r, at = view(ra, 0, KT, 2, SEQ)
        pool_r, _ = view(ra, at, GROUPS, 2, SEQ)
        vs_r, at = view(ra, at, NQ, 2, D)
        ws_r = [view(ra, at + 2 * D * t, 2, D)[0] for t in range(NQ - 1)] + [view(ra, (KT - 2) * 2 * SEQ, 2, D)[0]]
        a_r, _ = view(ra, 0, FT, 2, SEQ)

        prob, at = view(tmp, 0, 2, LEN)
        v_f, _ = view(tmp, at, 1, LEN)
        rot, at = view(tmp, at, 2, SEQ)
        rt, at = view(tmp, at, 2, SEQ)
        prob_m, at = view(tmp, at, NQ, P)
        rope_s, at = view(tmp, at, 2, LEN)
        rbc, at = view(tmp, 0, 1, SEQ)
        acc, at = view(tmp, at, 1, SEQ)
        sq, at = view(tmp, at, 2, SEQ)
        rest = at
        xin, _ = view(tmp, rest, 2, D)
        res_t, _ = view(tmp, rest + 2048, 2, SEQ)
        gfin, _ = view(tmp, rest + 2048, 1, D)
        sig, _ = view(tmp, rest, 4, SEQ)
        gpad, at = view(tmp, rest - 0, 2, 516)
        cnv, at = view(tmp, at, 2, SEQ)
        hid, at = view(tmp, at, 1, SEQ)
        cpad, at = view(tmp, rest, 1, 516)
        ecv, at = view(tmp, at, 1, SEQ)
        zpad, at = view(tmp, at, 3, 8 + SEQ)
        wst, at = view(tmp, rest, 1, D)
        bbc, at = view(tmp, at, 1, D)
        odt, at = view(tmp, at, 2, SEQ)
        h = big[:, 0:KT, :]
        m2 = big[:, KT:16, :]

        ssx, rsx = st[:, 0:5], st[:, 5:10]
        mx, neg, rs, ri = (st[:, 10 + 8 * j:18 + 8 * j] for j in range(4))
        rtok, sstok = st[:, 42:46], st[:, 46:50]
        ssv, rsv = st[:, 50:54], st[:, 54:58]
        ssv_part = st[:, 10:18]
        sd = st[:, 58:63]

        HI, LO = 0, 1
        PASSES = ((HI, HI), (HI, LO), (LO, HI))

        def vcol(name, k=0):
            c = vec_column(name) + k
            return vec[:, c:c + 1] if isinstance(k, int) else vec[:, bass.ds(c, 1)]

        def ffn_vec(layer, row, f):
            c = N_VEC + layer * FFN_ROWS + row * FT + f
            return vec[:, c:c + 1] if isinstance(f, int) else vec[:, bass.ds(c, 1)]

        def idx(i):
            return i if isinstance(i, int) else bass.ds(i, 1)

        def flat(ap, i):
            if isinstance(i, int):
                return ap
            return ap

        def loop(eng, n, body):
            body(0, True, n == 1)
            if n > 3:
                with eng.Fori(1, n - 1) as i:
                    body(i, False, False)
            elif n == 3:
                body(1, False, False)
            if n > 1:
                body(n - 1, False, True)

        def num(c, i=0, k=0):
            return c + i * k if k else c

        def w_load(sp, c, parts, i=0, k=0):
            if c >= 2 or k:
                sp.wait_ge(sem("w_lo"), num(c, i, k) - 1)
            for dst, src in parts:
                sp.dma_start(dst(raw[:, c % 2, :]), src).then_inc(sem(f"w_load{c % 2}"), 16)

        def split_pairs(kind, r, s):
            if kind == "full":
                return [(r[:, 0:UNIT], s[:, 0:UNIT])]
            if kind == "six":
                return [(r[:, 0:6 * P], s[:, 0:6 * P])]
            if kind == "pool":
                return [(r[:, 0:4 * P], s[:, 0:4 * P])]
            if kind == "kpe":
                r3, s3 = (x[:, 0:UNIT].rearrange("p (k n) -> p k n", k=KT) for x in (r, s))
                return [(r3[:, :, 0:32], s3[:, :, 0:32]), (r3[:, :, 16:32], s3[:, :, 32:48]),
                        (r3[:, :, 0:16], s3[:, :, 48:64]), (r3[:, :, 64:128], s3[:, :, 64:128])]
            rq = r[:, 0:384].rearrange("p (g n) -> p g n", g=4)
            sq_ = s[:, 0:512].rearrange("p (g n) -> p g n", g=4)
            rk = r[:, 384:640].rearrange("p (h t d) -> p t h d", h=2, t=2)
            sk = s[:, 512:768].rearrange("p (t h d) -> p t h d", h=2, t=2)
            return [(rq[:, :, 0:96], sq_[:, :, 0:96]), (rq[:, :, 80:96], sq_[:, :, 96:112]),
                    (rq[:, :, 64:80], sq_[:, :, 112:128]),
                    (rk[:, 0], sk[:, 0]), (rk[:, 1], sk[:, 1])]

        def w_hi(act, c, i=0, k=0, kind=None):
            if c >= len(KINDS):
                return
            kind = kind or KINDS[c]
            half = k // 2
            act.wait_ge(sem(f"w_load{c % 2}"), 32 * (c // 2 + 1) + (i * (32 * half) if k else 0))
            if c >= 2:
                act.wait_ge(sem("w_used"), num(c, i, k) - 1)
            pieces = split_pairs(kind, raw[:, c % 2, :], wsp[:, c % 2, HI, :])
            for n, (src, dst) in enumerate(pieces):
                ins = act.copy(dst, src)
            ins.then_inc(sem("w_hi"), 1)

        def w_lo(dve, c, i=0, k=0, kind=None):
            if c >= len(KINDS):
                return
            kind = kind or KINDS[c]
            dve.wait_ge(sem("w_hi"), num(c, i, k) + 1)
            src = split_pairs(kind, raw[:, c % 2, :], wsp[:, c % 2, HI, :])
            dst = split_pairs(kind, raw[:, c % 2, :], wsp[:, c % 2, LO, :])
            for (r, hi), (_, lo) in zip(src, dst):
                ins = dve.tensor_tensor(lo, r, hi, ALU.subtract)
            ins.then_inc(sem("w_lo"), 1)

        def w_ready(pe, c, i=0, k=0):
            pe.wait_ge(sem("w_lo"), num(c, i, k) + 1)

        def w_tile(c, part, k, width=P):
            return wsp[:, c % 2, part, k * P:k * P + width]

        def panel(dram, col, rows=KT, row0=0):
            halves = [(rows // 2, rows), (0, rows // 2)]
            out_ = []
            for lo, hi in halves:
                src = dram[(row0 + lo) * P:(row0 + hi) * P, bass.ds(col, P)] if not isinstance(col, int) \
                    else dram[(row0 + lo) * P:(row0 + hi) * P, col:col + P]
                out_.append((lambda r, lo=lo, hi=hi: r[:, lo * P:hi * P].rearrange("p (k n) -> p k n", k=hi - lo),
                             src.rearrange("(k p) n -> p k n", p=P)))
            return out_

        def product(pe, out_ap, c, moving, ks=range(KT), start=True, stop=True, n0=0, ready=None):
            last = None
            total = [(k, ws, ms) for k in ks for ws, ms in PASSES]
            for n, (k, ws, ms) in enumerate(total):
                if ready and n % len(PASSES) == 0:
                    ready(k)
                last = pe.matmul(out_ap, w_tile(c, ws, k - n0), moving(k, ms),
                                 start=start and n == 0, stop=stop and n == len(total) - 1,
                                 skip_group_check=True)
            return last

        def u_real(k, part):
            return u[:, k, part, META:LEN]

        def u_meta(k, part):
            return u[:, k, part, 0:META]

        PRO = FIRST["pro"]
        nat = big.rearrange("p a b -> p (a b)")[:, 0:5 * D].rearrange("p (t d) -> p t d", t=5)
        junk = big.rearrange("p a b -> p (a b)")[:, 5 * D:6 * D]
        stage = tmp[:, 0:3 * P].rearrange("p (s n) -> p s n", s=3)
        w_in = a["w_in"][0]
        bigf = big.rearrange("p a b -> p (a b)")
        pf = [bigf[:, 6 * D + j * 528:6 * D + (j + 1) * 528] for j in range(3)]
        fx, fe, fm = (t[0:HEADS, :] for t in pf)
        forget_r = ra[0:HEADS, 0:4 * LEN].rearrange("p (s j n) -> p s j n", s=2, j=2)
        ksq = bigf[:, 0:3 * LEN].rearrange("p (t n) -> p t n", t=3)
        krs = bigf[:, 3 * LEN:5 * LEN].rearrange("p (t n) -> p t n", t=2)
        kn = bigf[:, 5 * LEN:6 * LEN]
        kro = bigf[:, 6 * LEN:9 * LEN].rearrange("p (t n) -> p t n", t=3)
        fbias = st[0:HEADS, 63:64]

        def dma_prologue(sp):
            for t in range(NQ):
                sp.dma_start(nat[:, t, :], a["x"][0, t * P:(t + 1) * P, :]).then_inc(sem("x_in"), 16)
                if t == 0:
                    sp.dma_start(nat[0:META, 4, :], a["meta_tokens"]).then_inc(sem("x_in"), 16)
                    sp.dma_start(cst[:], consts).then_inc(sem("cst_in"), 16)
            rows = 0
            for name, n in VEC_ROWS:
                src = {"pre_g": a["pre_norm_g"], "q_g": a["mla_q_norm_g"], "kv_g": a["mla_kv_norm_g"],
                       "post_g": a["post_norm_g"], "mix_g": a["norm_mix_2"], "ffn_g": a["norm_ffn_2"],
                       "pool_scale": a["pool_scale_2"], "sgu_g": a["sgu_norm_2"],
                       "conv_a": a["conv_a_2"][0]}[name]
                sp.dma_start(stage[rows:rows + n, 0, :], src.rearrange("a (k p) -> (a k) p", p=P)) \
                    .then_inc(sem("vec_in"), 16)
                rows += n
            for layer in range(2):
                sp.dma_start(stage[0:3 * FT, 1 + layer, :],
                             a["conv_ffn_2"][layer].rearrange("a (k p) -> (a k) p", p=P)).then_inc(sem("vec_in"), 16)
                sp.dma_start(stage[3 * FT:4 * FT, 1 + layer, :],
                             a["b_conv_ffn_2"][layer:layer + 1].rearrange("a (k p) -> (a k) p", p=P)) \
                    .then_inc(sem("vec_in"), 16)
            sp.dma_start(fbias, a["fox_forget_b"].rearrange("a h -> h a"), allow_slow_non_contiguous=True) \
                .then_inc(sem("rope_in"), 16)
            sp.dma_start(rope_s[64:96, :, :], rope_t.rearrange("(s p) n -> p s n", s=2)).then_inc(sem("rope_in"), 16)

        N_VEC_DMA = 16 * (len(VEC_ROWS) + 4)

        def load_prologue(sp):
            for j, col in enumerate((W_F, W_KPE, W_CKV, W_CQ, W_CQ + P)):
                w_load(sp, PRO + j, panel(w_in, col))
            sp.wait_ge(sem("forget_lo"), 2)
            for s in range(2):
                sp.dma_start(forget_dram[s], forget_r[:, s].bitcast(F32)).then_inc(sem("forget_out"), 16)

        def act_prologue(act):
            act.wait_ge(sem("x_in"), 16 * 5)
            for t in range(5):
                n = P if t < 4 else META
                if t:
                    act.wait_ge(sem("x_ss"), t)
                act.activation(junk[0:n, :], nat[0:n, t, :], ACT.Square, accum_out=ssx[0:n, t:t + 1]) \
                    .then_inc(sem("x_ss"), 1)
            act.wait_ge(sem("cst_in"), 16)
            act.copy(ident_r[:], ident).then_inc(sem("cst_r"), 1)
            act.copy(mask_r[:], cst[:, 128:256]).then_inc(sem("cst_r"), 1)
            w_hi(act, PRO)
            w_hi(act, PRO + 1)
            act.wait_ge(sem("x_ms"), 2)
            act.activation(sd[:, 0:4], ssx[:, 0:4], ACT.Sqrt).then_inc(sem("x_sd"), 1)
            act.activation(sd[0:META, 4:5], ssx[0:META, 4:5], ACT.Sqrt).then_inc(sem("x_sd"), 1)
            for k in range(KT):
                act.wait_ge(sem("x_tr"), k + 1)
                if k == 0:
                    act.wait_ge(sem("vec"), 1)
                b = 2 * (k % 2)
                act.activation(u[:, k, HI, META:LEN], bank(b), ACT.Copy, scale=vcol("pre_g", k))
                act.activation(u[:, k, HI, 0:META], bank(b + 1, 0, META), ACT.Copy, scale=vcol("pre_g", k)) \
                    .then_inc(sem("u_hi"), 1)
            w_hi(act, PRO + 2)
            w_hi(act, PRO + 3)
            act.wait_ge(sem("f_x"), 1)
            act.activation(fe, fx, ACT.Abs).then_inc(sem("f_act"), 1)
            act.wait_ge(sem("f_act"), 1)
            act.activation(fe, fe, ACT.Exp, scale=-1.0).then_inc(sem("f_act"), 1)
            act.wait_ge(sem("f_act"), 2)
            act.activation(fe, fe, ACT.Ln, bias=1.0).then_inc(sem("f_act"), 1)
            for s in range(2):
                act.wait_ge(sem("f_cum"), s + 1)
                act.copy(forget_r[:, s, HI, :], (fm, fe)[s]).then_inc(sem("forget_hi"), 1)
            act.wait_ge(sem("kpe_rot"), 1)
            for t in range(4):
                ins = act.copy(k_t[64:96, t, HI, :], kro[64:96, 2, :])
            ins.then_inc(sem("kpe_hi"), 1)
            act.wait_ge(sem("w_used"), PRO + 3)
            act.wait_ge(sem("pro_meta"), 1)
            act.activation(ksq[:, 0, META:LEN], bank(2), ACT.Square)
            act.activation(ksq[:, 0, 0:META], bank(7, 32, 48), ACT.Square).then_inc(sem("c_sq"), 1)
            w_hi(act, PRO + 4)
            act.wait_ge(sem("c_sum"), 1)
            act.activation(krs[:, 0, META:LEN], bank(5), ACT.Sqrt, scale=1.0 / KV_RANK, bias=EPS)
            act.activation(krs[:, 0, 0:META], bank(6, 0, META), ACT.Sqrt, scale=1.0 / KV_RANK, bias=EPS) \
                .then_inc(sem("c_sd"), 1)
            act.wait_ge(sem("c_n"), 1)
            act.copy(ckv_r[:, HI, :], kn).then_inc(sem("c_hi"), 1)
            w_hi(act, PRO + 5)
            for t in range(2):
                act.wait_ge(sem("w_used"), PRO + 4 + t)
                act.activation(ksq[:, 1 + t, 0:SEQ], bank(3 + t), ACT.Square).then_inc(sem("c_sq"), 1)
            act.wait_ge(sem("c_sum"), 2)
            act.activation(krs[:, 1, 0:SEQ], bank(5), ACT.Sqrt, scale=1.0 / Q_RANK, bias=EPS).then_inc(sem("c_sd"), 1)
            for t in range(2):
                act.wait_ge(sem("c_n"), 2 + t)
                act.copy(cq_r[:, t, HI, :], kn[:, 0:SEQ]).then_inc(sem("c_hi"), 1)

        def pool_prologue(pool):
            pool.memset(ones[:], 1.0).then_inc(sem("ones"), 1)
            pool.memset(v_t.bitcast(F32), 0.0)
            pool.memset(v_m.bitcast(F32), 0.0).then_inc(sem("pads"), 1)
            pool.wait_ge(sem("vec"), 1)
            pool.memset(prob_m, 0.0).then_inc(sem("pads"), 1)

        def dve_prologue(dve):
            dve.wait_ge(sem("x_ss"), 5)
            for n, (rows, lo, hi) in enumerate(((P, 0, 4), (META, 4, 5))):
                dve.tensor_scalar(ssx[0:rows, lo:hi], ssx[0:rows, lo:hi], 1.0 / D, EPS, ALU.mult, ALU.add) \
                    .then_inc(sem("x_ms"), 1)
            dve.wait_ge(sem("x_sd"), 2)
            dve.reciprocal(rsx[:, 0:4], sd[:, 0:4]).then_inc(sem("x_rs"), 1)
            dve.reciprocal(rsx[0:META, 4:5], sd[0:META, 4:5]).then_inc(sem("x_rs"), 1)
            dve.wait_ge(sem("x_rs"), 2)
            for t in (4, 0, 1, 2, 3):
                n = P if t < 4 else META
                dve.tensor_scalar(nat[0:n, t, :], nat[0:n, t, :], rsx[0:n, t:t + 1], None, ALU.mult) \
                    .then_inc(sem("x_n"), 1)
            dve.wait_ge(sem("vec_tr"), 1)
            dve.tensor_copy(vec[:, 0:N_VEC], bank(7, 0, N_VEC))
            for layer in range(2):
                ins = dve.tensor_copy(vec[:, N_VEC + layer * FFN_ROWS:N_VEC + (layer + 1) * FFN_ROWS],
                                      bank(7, 128 * (layer + 1), 128 * (layer + 1) + FFN_ROWS))
            ins.then_inc(sem("vec"), 1)
            w_lo(dve, PRO)
            w_lo(dve, PRO + 1)
            dve.wait_ge(sem("vec"), 1)
            for k in range(KT):
                dve.wait_ge(sem("u_hi"), k + 1)
                b = 2 * (k % 2)
                dve.scalar_tensor_tensor(out=u[:, k, LO, META:LEN], in0=bank(b), scalar=vcol("pre_g", k),
                                         in1=u[:, k, HI, META:LEN], op0=ALU.mult, op1=ALU.subtract)
                dve.scalar_tensor_tensor(out=u[:, k, LO, 0:META], in0=bank(b + 1, 0, META),
                                         scalar=vcol("pre_g", k), in1=u[:, k, HI, 0:META],
                                         op0=ALU.mult, op1=ALU.subtract).then_inc(sem("u_lo"), 1)
            w_lo(dve, PRO + 2)
            w_lo(dve, PRO + 3)
            dve.wait_ge(sem("w_used"), PRO + 1)
            dve.wait_ge(sem("pro_meta"), 1)
            dve.wait_ge(sem("rope_in"), 32)
            dve.tensor_scalar(fx[:, META:LEN], bank(0, rows=slice(0, HEADS)), fbias, None, ALU.add)
            dve.tensor_scalar(fx[:, 0:META], bank(7, 0, META, rows=slice(0, HEADS)), fbias, None, ALU.add) \
                .then_inc(sem("f_x"), 1)
            dve.wait_ge(sem("f_act"), 3)
            dve.scalar_tensor_tensor(out=fm, in0=fx, scalar=0.0, in1=fe, op0=ALU.min, op1=ALU.subtract) \
                .then_inc(sem("f_dve"), 1)
            dve.wait_ge(sem("f_dve"), 1)
            dve.wait_ge(sem("ones"), 1)
            dve.tensor_tensor_scan(fx, ones[0:HEADS, 0:1].to_broadcast([HEADS, LEN]), fm, 0.0, ALU.mult, ALU.add).then_inc(sem("f_dve"), 1)
            dve.wait_ge(sem("f_dve"), 2)
            dve.tensor_scalar(fm, fx, 1.0 / FOX_SCALE, None, ALU.mult).then_inc(sem("f_cum"), 1)
            dve.tensor_scalar(fe, fx, -1.0 / FOX_SCALE, None, ALU.mult).then_inc(sem("f_cum"), 1)
            for s in range(2):
                dve.wait_ge(sem("forget_hi"), s + 1)
                dve.tensor_tensor(forget_r[:, s, LO, :], (fm, fe)[s], forget_r[:, s, HI, :], ALU.subtract) \
                    .then_inc(sem("forget_lo"), 1)
            dve.wait_ge(sem("w_used"), PRO + 2)
            for s in range(2):
                rows = slice(32 * s, 32 * s + 32)
                dve.tensor_tensor(kro[64:96, s, META:LEN], bank(1, rows=rows), rope_s[64:96, s, META:LEN], ALU.mult)
                ins = dve.tensor_tensor(kro[64:96, s, 0:META], bank(7, 16, 32, rows=rows),
                                        rope_s[64:96, s, 0:META], ALU.mult)
            ins.then_inc(sem("kpe_t"), 1)
            dve.wait_ge(sem("kpe_t"), 1)
            dve.tensor_tensor(kro[64:96, 2, :], kro[64:96, 0, :], kro[64:96, 1, :], ALU.add).then_inc(sem("kpe_rot"), 1)
            dve.wait_ge(sem("kpe_hi"), 1)
            for t in range(4):
                ins = dve.tensor_tensor(k_t[64:96, t, LO, :], kro[64:96, 2, :], k_t[64:96, t, HI, :], ALU.subtract)
            ins.then_inc(sem("kpe_lo"), 1)
            w_lo(dve, PRO + 4)
            dve.wait_ge(sem("c_sd"), 1)
            dve.reciprocal(krs[:, 0, :], krs[:, 0, :]).then_inc(sem("c_rs"), 1)
            dve.wait_ge(sem("c_rs"), 1)
            dve.scalar_tensor_tensor(out=kn[:, META:LEN], in0=bank(2), scalar=vcol("kv_g"), in1=krs[:, 0, META:LEN],
                                     op0=ALU.mult, op1=ALU.mult)
            dve.scalar_tensor_tensor(out=kn[:, 0:META], in0=bank(7, 32, 48), scalar=vcol("kv_g"),
                                     in1=krs[:, 0, 0:META], op0=ALU.mult, op1=ALU.mult).then_inc(sem("c_n"), 1)
            dve.wait_ge(sem("c_hi"), 1)
            dve.tensor_tensor(ckv_r[:, LO, :], kn, ckv_r[:, HI, :], ALU.subtract).then_inc(sem("c_lo"), 1)
            w_lo(dve, PRO + 5)
            dve.wait_ge(sem("c_sd"), 2)
            dve.reciprocal(krs[:, 1, 0:SEQ], krs[:, 1, 0:SEQ]).then_inc(sem("c_rs"), 1)
            dve.wait_ge(sem("c_rs"), 2)
            for t in range(2):
                dve.wait_ge(sem("c_lo"), 1 + t)
                dve.scalar_tensor_tensor(out=kn[:, 0:SEQ], in0=bank(3 + t), scalar=vcol("q_g", t),
                                         in1=krs[:, 1, 0:SEQ], op0=ALU.mult, op1=ALU.mult).then_inc(sem("c_n"), 1)
                dve.wait_ge(sem("c_hi"), 2 + t)
                dve.tensor_tensor(cq_r[:, t, LO, :], kn[:, 0:SEQ], cq_r[:, t, HI, :], ALU.subtract) \
                    .then_inc(sem("c_lo"), 1)

        def pe_prologue(pe):
            pe.wait_ge(sem("cst_in"), 16)
            pe.wait_ge(sem("vec_in"), N_VEC_DMA)
            pe.transpose(bank(7, 0, N_VEC), stage[0:N_VEC, 0, :], ident[0:N_VEC, 0:N_VEC])
            for layer in range(2):
                ins = pe.transpose(bank(7, 128 * (layer + 1), 128 * (layer + 1) + FFN_ROWS),
                                   stage[0:FFN_ROWS, 1 + layer, :], ident[0:FFN_ROWS, 0:FFN_ROWS])
            ins.then_inc(sem("vec_tr"), 1)
            pe.wait_ge(sem("x_n"), 5)
            for k in range(KT):
                if k >= 2:
                    pe.wait_ge(sem("u_lo"), k - 1)
                b = 2 * (k % 2)
                pe.transpose(bank(b + 1, 0, META), nat[0:META, 4, k * P:(k + 1) * P], ident[0:META, 0:META])
                for t in range(NQ):
                    ins = pe.transpose(bank(b, t * P, (t + 1) * P), nat[:, t, k * P:(k + 1) * P], ident)
                ins.then_inc(sem("x_tr"), 1)
            pe.wait_ge(sem("u_lo"), KT)
            pe.wait_ge(sem("vec"), 1)
            for j in range(3):
                w_ready(pe, PRO + j)
                ins = product(pe, bank(7, 16 * j, 16 * j + 16), PRO + j, u_meta)
                if j == 2:
                    ins.then_inc(sem("pro_meta"), 1)
                product(pe, bank(j), PRO + j, u_real).then_inc(sem("w_used"), 1)
            pe.wait_ge(sem("ones"), 1)
            w_ready(pe, PRO + 3)
            product(pe, bank(3), PRO + 3, u_real).then_inc(sem("w_used"), 1)
            pe.wait_ge(sem("c_sq"), 1)
            pe.matmul(bank(5), ones[:], ksq[:, 0, META:LEN], start=True, stop=True)
            pe.matmul(bank(6, 0, META), ones[:], ksq[:, 0, 0:META], start=True, stop=True).then_inc(sem("c_sum"), 1)
            w_ready(pe, PRO + 4)
            product(pe, bank(4), PRO + 4, u_real).then_inc(sem("w_used"), 1)
            pe.wait_ge(sem("c_sq"), 3)
            pe.wait_ge(sem("c_sd"), 1)
            for t in range(2):
                ins = pe.matmul(bank(5), ones[:], ksq[:, 1 + t, 0:SEQ], start=t == 0, stop=t == 1)
            ins.then_inc(sem("c_sum"), 1)

        def n_real(b):
            return P * (b % NQ + 1)

        def s_cols(b, meta=True):
            return slice(B_S * 512 + 512 - n_real(b), B_S * 512 + 512 + (META if meta else 0))

        def pe_scores(pe, pr, b, fox, par, turn):
            hh, i = divmod(b, NQ)
            slot = 2 * par + hh
            rows = slice(0, 97 if fox else 96)
            if b == 0:
                pe.wait_ge(sem("q_split"), pr + 1)
                pe.wait_ge(sem("k_split"), pr + 1)
                if fox:
                    pe.wait_ge(sem(f"rows{par}"), 32 * turn + (0 if par else 32))
                else:
                    pe.wait_ge(sem("kpe_lo"), 1)
            if not (isinstance(pr, int) and pr == 0 and b == 0):
                pe.wait_ge(sem("exped"), 8 * pr + b)
                if b == 0:
                    pe.wait_ge(sem("pm_split"), pr)
            for n, (qs, ks) in enumerate(PASSES):
                pe.matmul(ps[:, s_cols(b, False)], q_t[rows, slot, qs, i * P:(i + 1) * P],
                          k_t[rows, slot, ks, META:META + n_real(b)], start=n == 0, stop=False,
                          skip_group_check=True)
            pe.matmul(bank(B_S, 384, 512), ident_r[:], mask_r[:], start=False, stop=True, skip_group_check=True)
            for n, (qs, ks) in enumerate(PASSES):
                ins = pe.matmul(bank(B_S + 1, 0, META), q_t[rows, slot, qs, i * P:(i + 1) * P],
                                k_t[rows, slot, ks, 0:META], start=n == 0, stop=n == 2)
            ins.then_inc(sem("scores"), 1)

        def pe_transposes(pe, pr, b):
            pe.wait_ge(sem("normed"), 8 * pr + b + 1)
            if not (isinstance(pr, int) and pr == 0 and b == 0):
                pe.wait_ge(sem("p_split"), 8 * pr + b)
            base = 512 - n_real(b)
            for j in range(b % NQ + 1):
                ins = pe.transpose(bank(B_T, j * P, (j + 1) * P),
                                   prob[:, b % 2, base + j * P:base + (j + 1) * P], ident)
            ins.then_inc(sem("transposed"), 1)

        def pe_transposes_meta(pe, pr):
            pe.wait_ge(sem("normed"), 8 * pr + 8)
            for i in range(NQ):
                ins = pe.transpose(bank(B_S, i * P, (i + 1) * P), prob_m[:, i, :], ident)
            ins.then_inc(sem("pm_transposed"), 1)

        def pe_values(pe, pr, hh):
            pe.wait_ge(sem("p_split"), 8 * pr + 4 * hh + 4)
            if hh == 0:
                pe.wait_ge(sem("v_split"), pr + 1)
                if not (isinstance(pr, int) and pr == 0):
                    pe.wait_ge(sem("gated"), pr)
            for j in range(NQ):
                for n, (vs, pp) in enumerate(PASSES):
                    pe.matmul(bank(B_O, j * P, 512), v_t[:, vs, j, hh, :], p_t[:, hh, pp * NQ + j, j * P:512],
                              start=hh == 0 and j == 0 and n == 0, stop=False, skip_group_check=True)
            if hh == 1:
                pe.wait_ge(sem("pm_split"), pr + 1)
                for n, (vs, pp) in enumerate(PASSES):
                    ins = pe.matmul(bank(B_O), v_m[0:48, vs, :], p_m[0:48, pp, :], start=False, stop=n == 2,
                                    skip_group_check=True)
                ins.then_inc(sem("values"), 1)

        def mla_q(pe, c, hh):
            for n, (k, ws, ms) in enumerate([(k, ws, ms) for k in range(2) for ws, ms in PASSES]):
                g = 2 * k + hh
                ins = pe.matmul(bank(hh), wsp[:, c % 2, ws, g * P:(g + 1) * P], cq_r[:, k, ms, :],
                                start=n == 0, stop=n == 5)
            return ins

        def products_mla(pe, s, c, kk=0, i=0):
            later = not (isinstance(s, int) and s == 0)

            def z_mla(half):
                if half == 0:
                    w_ready(pe, c, i, kk)
                    if later:
                        pe.wait_ge(sem("q_split"), s)
                ins = product(pe, bank(0), c, u_real, range(4 * half, 4 * half + 4), start=half == 0, stop=half == 1)
                if half:
                    ins.then_inc(sem("w_used"), 1)

            def k_and_meta():
                w_ready(pe, c + 1, i, kk)
                if later:
                    pe.wait_ge(sem("v_split"), s)
                    pe.wait_ge(sem("z_read"), 2 * s)
                wk = [wsp[:, (c + 1) % 2, part, 512:640] for part in range(2)]
                wv = [wsp[:, (c + 1) % 2, part, 640:768] for part in range(2)]
                for n, (ws, ms) in enumerate(PASSES):
                    pe.matmul(bank(2), wk[ws], ckv_r[:, ms, META:LEN], start=n == 0, stop=n == 2)
                for n, (ws, ms) in enumerate(PASSES):
                    pe.matmul(bank(B_META, 0, META), wk[ws], ckv_r[:, ms, 0:META], start=n == 0, stop=n == 2)
                for n, (ws, ms) in enumerate(PASSES):
                    ins = pe.matmul(bank(B_META, V_META, V_META + P), ckv_r[:, ms, 0:P], wv[ws],
                                    start=n == 0, stop=n == 2)
                ins.then_inc(sem("k_done"), 1)
                mla_q(pe, c + 1, 1).then_inc(sem("q1_done"), 1)

            def q():
                pe.wait_ge(sem("z_read"), 2 * s + 1)
                mla_q(pe, c + 1, 0).then_inc(sem("q_done"), 1)

            def z_fox(part):
                if part == 0:
                    w_ready(pe, c + 2, i, kk)
                    pe.wait_ge(sem("k_split"), s + 1)
                ins = product(pe, bank(2), c + 2, u_real, (2 * part, 2 * part + 1), start=part == 0, stop=part == 3)
                if part == 3:
                    ins.then_inc(sem("w_used"), 1)

            def v():
                pe.wait_ge(sem("q1_split"), s + 1)
                wv = [wsp[:, (c + 1) % 2, part, 640:768] for part in range(2)]
                for t in range(NQ):
                    for n, (ws, ms) in enumerate(PASSES):
                        ins = pe.matmul(bank(1, t * P, (t + 1) * P), ckv_r[:, ms, META + t * P:META + (t + 1) * P],
                                        wv[ws], start=n == 0, stop=n == 2)
                ins.then_inc(sem("w_used"), 1)
                z_fox(3)

            return [lambda: z_mla(0), lambda: z_mla(1), k_and_meta, q] + \
                   [lambda part=part: z_fox(part) for part in range(3)] + [v]

        def products_fox(pe, s, c, kk=0, i=0):
            def feature(j, k):
                if k == 0:
                    w_ready(pe, c + j, i, kk)
                    if j == 0:
                        pe.wait_ge(sem("q_split"), s)
                        pe.wait_ge(sem("k_split"), s)
                        if isinstance(s, int) and s == PAIRS:
                            pe.wait_ge(sem("v_split"), s)
                            pe.wait_ge(sem("z_read"), 2 * s)
                    elif j == 1:
                        pe.wait_ge(sem("v_split"), s)
                    else:
                        pe.wait_ge(sem("q_split"), s + 1)
                if j == 0:
                    ins = product(pe, bank(1), c, u_real, (k,), start=k == 0, stop=k == KT - 1)
                else:
                    banks = ((0, 3), (2, 1))[j - 1]
                    for n, (ws, ms) in enumerate(PASSES):
                        for half, b in enumerate(banks):
                            ins = pe.matmul(bank(b, 0, HALF), w_tile(c + j, ws, k),
                                            u[:, k, ms, half * HALF:(half + 1) * HALF],
                                            start=k == 0 and n == 0, stop=k == KT - 1 and n == 2,
                                            skip_group_check=True)
                if k == KT - 1:
                    ins.then_inc(sem("w_used"), 1)

            def part(b):
                for m in range(3 * b, 3 * b + 3):
                    feature(*divmod(m, KT))

            return [lambda b=b: part(b) for b in range(8)]

        def fox_v_transposes(pe, s):
            pe.wait_ge(sem("v_copied"), s - PAIRS + 1)
            for t in range(NQ):
                pe.transpose(bank(2, t * P, (t + 1) * P), v_f[:, 0, META + t * P:META + (t + 1) * P], ident)
            pe.transpose(bank(B_META, V_META, V_META + P, rows=slice(0, META)), v_f[:, 0, 0:META], ident) \
                .then_inc(sem("v_transposed"), 1)

        def pe_step(pe, s, attn, gemm, par, c, kk=0, i=0):
            parts = [None] * 8
            if gemm:
                parts = (products_mla if gemm == "mla" else products_fox)(pe, s, c, kk, i)
            pr = s - 1
            for b in range(8):
                if attn:
                    pe_scores(pe, pr, b, attn == "fox", 1 - par, i)
                if parts[b]:
                    parts[b]()
                if attn and b:
                    pe_transposes(pe, pr, b - 1)
            if attn:
                pe_transposes(pe, pr, 7)
                pe_transposes_meta(pe, pr)
                pe_values(pe, pr, 0)
                pe_values(pe, pr, 1)
            if gemm == "fox":
                fox_v_transposes(pe, s)

        def act_exp(act, pr, b, fox):
            act.wait_ge(sem("neg"), 8 * pr + b + 1)
            if not (isinstance(pr, int) and pr == 0 and b < 2):
                act.wait_ge(sem("transposed"), 8 * pr + b - 1)
            act.activation(prob[:, b % 2, 512 - n_real(b):LEN], ps[:, s_cols(b)], ACT.Exp, bias=neg[:, b:b + 1],
                           scale=FOX_SCALE if fox else MLA_SCALE, accum_out=rs[:, b:b + 1]) \
                .then_inc(sem("exped"), 1)

        def p_views(b):
            hh, i = divmod(b, NQ)
            src = bank(B_T, 0, (i + 1) * P).rearrange("p (j n) -> p j n", n=P)
            hi, lo = (p_t[:, hh, part * NQ:part * NQ + i + 1, i * P:(i + 1) * P] for part in range(2))
            return src, hi, lo

        def act_p(act, pr, b):
            act.wait_ge(sem("transposed"), 8 * pr + b + 1)
            if not (isinstance(pr, int) and pr == 0):
                act.wait_ge(sem("values"), pr)
            src, hi, _ = p_views(b)
            act.copy(hi, src).then_inc(sem("p_hi"), 1)

        def act_z(act, tile, b, c, kk=0, i=0):
            act.wait_ge(sem("w_used"), num(c, i, kk) + 1)
            z = bank(b) if isinstance(tile, int) else bank(b).rearrange("p (a n) -> p a n", a=1)
            act.copy(big[:, idx(tile), :], z).then_inc(sem("z_read"), 1)

        def act_silu(act, tile, n):
            tiles = big[:, tile:tile + n, :] if isinstance(tile, int) else big[:, bass.ds(tile, n), :]
            act.activation(tiles, tiles, ACT.Silu).then_inc(sem("z_silu"), 1)

        def q_pieces(gemm, par, heads=(0, 1)):
            slot, out_ = 2 * par, []
            for hh in heads:
                if gemm == "mla":
                    out_ += [(bank(hh, rows=slice(0, NOPE)), q_t[0:NOPE, slot + hh], slice(0, SEQ)),
                             (rot[64:96, hh, :], q_t[64:96, slot + hh], slice(0, SEQ))]
                else:
                    out_.append((bank(1, rows=slice(64 * hh, 64 * hh + 64)), q_t[0:HD, slot + hh], slice(0, SEQ)))
            return out_

        def k_pieces(gemm, par):
            slot = 2 * par
            if gemm == "mla":
                parts = ((bank(2), slice(META, LEN)), (bank(B_META, 0, META), slice(0, META)))
            else:
                parts = ((bank(0, 0, HALF), slice(0, HALF)), (bank(3, 0, HALF), slice(HALF, LEN)))
            return [(src[64 * hh:64 * hh + 64], k_t[0:HD, slot + hh], cols) for src, cols in parts for hh in range(2)]

        def v_pieces(part, gemm):
            src = bank(1 if gemm == "mla" else 2).rearrange("p (n h d) -> p n h d", n=NQ, h=2)
            dst = v_t[:, part].rearrange("p n h (a d) -> p n (h a) d", a=2)[:, :, 0:4:3, :]
            out_ = [(src, dst)]
            for hh in range(2):
                out_.append((bank(B_META, V_META + 64 * hh, V_META + 64 * hh + 64, rows=slice(0, META)),
                             v_m[32 * hh:32 * hh + META, part, 64 * hh:64 * hh + 64]))
            return out_

        def old_scores_done(eng, s):
            if not (isinstance(s, int) and s < 2):
                eng.wait_ge(sem("scores"), 8 * s - 8)

        def act_q_mla(act, s, hh, par):
            act.wait_ge(sem("rotated"), 2 * s + 2 - hh)
            act.wait_ge(sem("q1_done" if hh else "q_done"), s + 1)
            if isinstance(s, int) and s == 0:
                act.wait_ge(sem("forget_out"), 32)
            old_scores_done(act, s)
            for src, dst, cols in q_pieces("mla", par, (hh,)):
                ins = act.copy(dst[:, HI, cols], src)
            ins.then_inc(sem("q1_hi" if hh else "q_hi"), 1)

        def act_q_fox(act, s, c, par, kk=0, i=0):
            act.wait_ge(sem("w_used"), num(c, i, kk) + 1)
            old_scores_done(act, s)
            for src, dst, cols in q_pieces("fox", par):
                ins = act.copy(dst[:, HI, cols], src)
            ins.then_inc(sem("q_hi"), 1)

        def act_k(act, s, c, gemm, par, kk=0, i=0):
            if gemm == "mla":
                act.wait_ge(sem("k_done"), s + 1)
            else:
                act.wait_ge(sem("w_used"), num(c + 1, i, kk) + 1)
            old_scores_done(act, s)
            for src, dst, cols in k_pieces(gemm, par):
                ins = act.copy(dst[:, HI, cols], src)
            ins.then_inc(sem("k_hi"), 1)

        def act_v_copy(act, s, c, kk=0, i=0):
            act.wait_ge(sem("w_used"), num(c + 2, i, kk) + 1)
            if isinstance(s, int) and s == PAIRS:
                act.wait_ge(sem("q_split"), PAIRS)
            else:
                act.wait_ge(sem("v_transposed"), s - PAIRS)
            act.copy(v_f[:, 0, 0:HALF], bank(2, 0, HALF))
            act.copy(v_f[:, 0, HALF:LEN], bank(1, 0, HALF)).then_inc(sem("v_copied"), 1)

        def act_v(act, s, c, gemm, kk=0, i=0):
            if isinstance(s, int) and s == 0:
                act.wait_ge(sem("pads"), 1)
            else:
                act.wait_ge(sem("values"), s)
            if gemm == "mla":
                act.wait_ge(sem("w_used"), num(c + 1, i, kk) + 1)
            else:
                act.wait_ge(sem("v_transposed"), s - PAIRS + 1)
            act.wait_ge(sem("k_split"), s + 1)
            for src, dst in v_pieces(HI, gemm):
                ins = act.copy(dst, src)
            ins.then_inc(sem("v_hi"), 1)

        def act_step(act, s, attn, gemm, par, c, kk=0, i=0, nxt=None):
            pr = s - 1
            for b in range(8):
                if attn:
                    act_exp(act, pr, b, attn == "fox")
                if gemm == "mla":
                    if b == 0:
                        w_hi(act, c + 1, i, kk, "qkv")
                    elif b == 2:
                        act_z(act, s, 0, c, kk, i)
                        w_hi(act, c + 2, i, kk, "full")
                elif gemm == "fox":
                    if b in (0, 3):
                        w_hi(act, c + (1 if b == 0 else 2), i, kk, "full")
                    elif b == 6:
                        w_hi(act, nxt, i, kk, "full")
                if attn and b:
                    act_p(act, pr, b - 1)
                if gemm and b == (2 if gemm == "mla" else 5):
                    act_k(act, s, c, gemm, par, kk, i)
                if gemm == "mla" and b in (5, 6):
                    act_q_mla(act, s, 6 - b, par)
                elif gemm == "fox" and b == 3:
                    act_q_fox(act, s, c, par, kk, i)
            if gemm == "fox":
                act_v_copy(act, s, c, kk, i)
            if attn:
                act_p(act, pr, 7)
                act.wait_ge(sem("pm_transposed"), pr + 1)
                act.copy(p_m[0:48, HI, :], bank(B_S, rows=slice(0, 48))).then_inc(sem("pm_hi"), 1)
            if gemm == "mla":
                if par:
                    act.wait_ge(sem("z_read"), 2 * s + 1)
                w_hi(act, nxt, i, kk, "full")
                act_z(act, s + PAIRS, 2, c + 2, kk, i)
                if par:
                    act_silu(act, s - 1, 2)
            if isinstance(s, int) and s == PAIRS:
                act.wait_ge(sem("z_read"), 2 * PAIRS)
                act_silu(act, PAIRS, PAIRS)
            if gemm:
                act_v(act, s, c, gemm, kk, i)

        def dve_max(dve, pr, b, fox):
            dve.wait_ge(sem("scores"), 8 * pr + b + 1)
            dve.reduce_max(mx[:, b:b + 1], ps[:, s_cols(b)], AX.X).then_inc(sem("maxed"), 1)
            dve.wait_ge(sem("maxed"), 8 * pr + b + 1)
            dve.tensor_scalar(neg[:, b:b + 1], mx[:, b:b + 1], -(FOX_SCALE if fox else MLA_SCALE), None, ALU.mult) \
                .then_inc(sem("neg"), 1)

        def dve_norm(dve, pr, b):
            hh, i = divmod(b, NQ)
            dve.wait_ge(sem("exped"), 8 * pr + b + 1)
            dve.reciprocal(ri[:, b:b + 1], rs[:, b:b + 1]).then_inc(sem("recip"), 1)
            dve.wait_ge(sem("recip"), 8 * pr + b + 1)
            if b == 0:
                dve.wait_ge(sem("pads"), 2)
                if not (isinstance(pr, int) and pr == 0):
                    dve.wait_ge(sem("pm_transposed"), pr)
            real = prob[:, b % 2, 512 - n_real(b):512]
            dve.tensor_scalar(prob_m[:, i, 32 * hh:32 * hh + META], prob[:, b % 2, 512:LEN], ri[:, b:b + 1], None,
                              ALU.mult)
            dve.tensor_scalar(real, real, ri[:, b:b + 1], None, ALU.mult).then_inc(sem("normed"), 1)

        def dve_p(dve, pr, b):
            dve.wait_ge(sem("p_hi"), 8 * pr + b + 1)
            src, hi, lo = p_views(b)
            dve.tensor_tensor(lo, src, hi, ALU.subtract).then_inc(sem("p_split"), 1)

        def dve_rotate(dve, s, hh):
            dve.wait_ge(sem("q1_done" if hh else "q_done"), s + 1)
            if isinstance(s, int) and s == 0:
                dve.wait_ge(sem("vec"), 1)
            else:
                dve.wait_ge(sem("q_split"), s)
            dve.tensor_tensor(rot[64:96, hh, :], bank(hh, rows=slice(64, 96)), rope_s[64:96, 0, META:LEN], ALU.mult)
            dve.tensor_tensor(rt[64:96, hh, :], bank(hh, rows=slice(96, 128)), rope_s[64:96, 1, META:LEN],
                              ALU.mult).then_inc(sem("rotating"), 1)

        def pool_rotate(pool, s):
            for n, hh in enumerate((1, 0)):
                if n == 0 and isinstance(s, int) and s == 0:
                    pool.wait_ge(sem("pads"), 2)
                else:
                    pool.wait_ge(sem("rotated"), 2 * s + n)
                pool.wait_ge(sem("rotating"), 2 * s + n + 1)
                pool.tensor_tensor(rot[64:96, hh, :], rot[64:96, hh, :], rt[64:96, hh, :], ALU.add) \
                    .then_inc(sem("rotated"), 1)

        def dve_q(dve, s, gemm, par, heads=(0, 1)):
            head_1 = heads == (1,)
            dve.wait_ge(sem("q1_hi" if head_1 else "q_hi"), s + 1)
            for src, dst, cols in q_pieces(gemm, par, heads):
                ins = dve.tensor_tensor(dst[:, LO, cols], src, dst[:, HI, cols], ALU.subtract)
            ins.then_inc(sem("q1_split" if head_1 else "q_split"), 1)

        def dve_k(dve, s, gemm, par):
            dve.wait_ge(sem("k_hi"), s + 1)
            for src, dst, cols in k_pieces(gemm, par):
                ins = dve.tensor_tensor(dst[:, LO, cols], src, dst[:, HI, cols], ALU.subtract)
            ins.then_inc(sem("k_split"), 1)

        def dve_v(dve, s, gemm):
            dve.wait_ge(sem("v_hi"), s + 1)
            for (src, dst), (_, hi) in zip(v_pieces(LO, gemm), v_pieces(HI, gemm)):
                ins = dve.tensor_tensor(dst, src, hi, ALU.subtract)
            ins.then_inc(sem("v_split"), 1)

        def dve_step(dve, s, attn, gemm, par, c, kk=0, i=0, nxt=None):
            pr = s - 1
            for b in range(8):
                if attn:
                    dve_max(dve, pr, b, attn == "fox")
                if gemm == "mla":
                    if b == 3:
                        dve_k(dve, s, gemm, par)
                    elif b in (4, 5):
                        dve_rotate(dve, s, 5 - b)
                    elif b >= 6:
                        dve_q(dve, s, gemm, par, (7 - b,))
                elif gemm == "fox":
                    if b == 4:
                        dve_q(dve, s, gemm, par)
                    elif b == 6:
                        dve_k(dve, s, gemm, par)
                if attn:
                    dve_norm(dve, pr, b)
                if gemm == "mla":
                    if b == 0:
                        w_lo(dve, c + 1, i, kk, "qkv")
                    elif b == 2:
                        w_lo(dve, c + 2, i, kk, "full")
                elif gemm == "fox":
                    if b in (0, 3):
                        w_lo(dve, c + (1 if b == 0 else 2), i, kk, "full")
                    elif b == 6:
                        w_lo(dve, nxt, i, kk, "full")
                if attn and b:
                    dve_p(dve, pr, b - 1)
            if attn:
                dve_p(dve, pr, 7)
                dve.wait_ge(sem("pm_hi"), pr + 1)
                dve.tensor_tensor(p_m[0:48, LO, :], bank(B_S, rows=slice(0, 48)), p_m[0:48, HI, :], ALU.subtract) \
                    .then_inc(sem("pm_split"), 1)
            if gemm == "mla":
                w_lo(dve, nxt, i, kk, "full")
            if attn:
                dve.wait_ge(sem("values"), pr + 1)
                if isinstance(s, int):
                    dve.wait_ge(sem("z_silu"), min((s + 1) // 2, PAIRS // 2) if s <= PAIRS else PAIRS // 2 + 1)
                elif attn == "mla":
                    dve.wait_ge(sem("z_silu"), i + par)
                z = big[:, idx(pr), :]
                o = bank(B_O) if isinstance(pr, int) else bank(B_O).rearrange("p (a n) -> p a n", a=1)
                dve.tensor_tensor(z, o, z, ALU.mult).then_inc(sem("gated"), 1)
            if gemm:
                dve_v(dve, s, gemm)

        def pool_rows(pool, g, par):
            pool.wait_ge(sem("scores"), 8 * (g + PAIRS - 1))
            slots = slice(2 * par, 2 * par + 2)
            if isinstance(g, int):
                pool.wait_ge(sem("rotated"), 2 * PAIRS)
                for n, (dst, value) in enumerate(((q_t[64:96, slots], 0.0), (k_t[64:96, slots], 0.0),
                                                  (k_t[96:97, slots, HI, :], 1.0), (k_t[96:97, slots, LO, :], 0.0),
                                                  (q_t[64:65, slots, HI, :], 1.0))):
                    pool.memset(dst.bitcast(F32), value).then_inc(sem("aug"), 1)
                    pool.wait_ge(sem("aug"), 5 * g + n + 1)
                pool.wait_ge(sem("forget_out"), 32)
            h0 = 2 * g
            cum = forget_dram[0, bass.ds(h0, 2)]
            pool.dma_start(q_t[96:97, slots].bitcast(F32), cum[:, :, META:LEN].rearrange("(a h) j n -> a h j n", a=1)) \
                .then_inc(sem(f"rows{par}"), 16)
            pool.dma_start(k_t[64:65, slots].bitcast(F32),
                           forget_dram[1, bass.ds(h0, 2)].rearrange("(a h) j n -> a h j n", a=1)) \
                .then_inc(sem(f"rows{par}"), 16)

        def pool_attention(pool):
            pool_rotate(pool, 0)
            with pool.Fori(1, PAIRS) as s:
                pool_rotate(pool, s)
            pool_rows(pool, 0, 0)
            pool_rows(pool, 1, 1)
            with pool.Fori(1, PAIRS // 2) as g:
                pool_rows(pool, 2 * g, 0)
                pool_rows(pool, 2 * g + 1, 1)

        def steps(eng, step):
            c0, c8 = FIRST[("attn", 0)], FIRST[("attn", PAIRS)]
            step(0, None, "mla", 0, c0, 0, 0, c0 + 3)
            step(1, "mla", "mla", 1, c0 + 3, 0, 0, c0 + 6)
            with eng.Fori(1, PAIRS // 2) as i:
                for par in range(2):
                    c = c0 + 3 * par
                    step(2 * i + par, "mla", "mla", par, c, 6, i, c + 3)
            step(PAIRS, "mla", "fox", 0, c8, 0, 0, c8 + 3)
            step(PAIRS + 1, "fox", "fox", 1, c8 + 3, 0, 0, c8 + 6)
            with eng.Fori(1, PAIRS // 2) as i:
                for par in range(2):
                    c = c8 + 3 * par
                    step(2 * i + (PAIRS + par), "fox", "fox", par, c, 6, i, c + 3)
            step(STEPS, "fox", None, 0, None, 0, PAIRS // 2)

        def load_attention(sp):
            def mla(s, c, kk, i):
                at_ = (s * P, s * 192, s * 256)
                if not isinstance(s, int):
                    at_ = tuple(sp.snap(x) for x in at_)
                w_load(sp, c, panel(w_in, W_ZM + at_[0]), i, kk)
                uq, ukv = a["w_uq"][0], a["w_ukv"][0]
                w_load(sp, c + 1, [
                    (lambda r: r[:, 0:384].rearrange("p (k n) -> p k n", k=2),
                     uq[:, bass.ds(at_[1], 192)].rearrange("(k p) n -> p k n", p=P)),
                    (lambda r: r[:, 384:640], ukv[:, bass.ds(at_[2], 256)])], i, kk)
                w_load(sp, c + 2, panel(w_in, W_ZF + at_[0]), i, kk)

            def fox(g, c, kk, i):
                at_ = g * P if isinstance(g, int) else sp.snap(g * P)
                for j, col in enumerate((W_FQ, W_FK, W_FV)):
                    w_load(sp, c + j, panel(w_in, col + at_), i, kk)

            c0, c8 = FIRST[("attn", 0)], FIRST[("attn", PAIRS)]
            for kind, c in ((mla, c0), (fox, c8)):
                kind(0, c, 0, 0)
                kind(1, c + 3, 0, 0)
                with sp.Fori(1, PAIRS // 2) as i:
                    kind(2 * i, c, 6, i)
                    kind(2 * i + 1, c + 3, 6, i)

        MIX = FIRST["mix"]

        def load_mix(sp):
            def body(n, first, last):
                for j, (w, col) in enumerate(((w_in, W_GA), (w_in, W_GB), (a["w_br_mla"][0], 0),
                                              (a["w_br_fox"][0], 0))):
                    w_load(sp, MIX + j, panel(w, col + n * P), n, 4)
            loop(sp, KT, body)

        def pe_mix(pe):
            pe.wait_ge(sem("gated"), STEPS)

            def body(n, first, last):
                for j in range(4):
                    c = MIX + j
                    w_ready(pe, c, n, 4)
                    if not first:
                        pe.wait_ge(sem("sig"), 2 * n - 1 + j) if j < 2 else pe.wait_ge(sem("branch"), 2 * n - 3 + j)
                    if j < 2:
                        moving = u_real
                    else:
                        if first:
                            pe.wait_ge(sem("o_lo"), 8 * (j - 1))
                        moving = lambda k, part, j=j: o_r[:, 8 * (j - 2) + k, part, :]
                    product(pe, bank(j), c, moving).then_inc(sem("w_used"), 1)
            loop(pe, KT, body)

        def act_mix(act):
            act.wait_ge(sem("gated"), STEPS)
            w_hi(act, MIX + 1)

            for t in range(16):
                act.copy(o_r[:, t, HI, :], big[:, t, :]).then_inc(sem("o_hi"), 1)

            def body(n, first, last):
                for j in range(2):
                    act.wait_ge(sem("w_used"), MIX + j + 1 + 4 * n)
                    if not first:
                        act.wait_ge(sem("branch"), 2 * n - 1 + j)
                    act.activation(sig[:, j, :], bank(j), ACT.Sigmoid).then_inc(sem("sig"), 1)
                    w_hi(act, MIX + j + 2, n, 4, "full")
                if last:
                    for k in range(KT - 1):
                        act.wait_ge(sem("mixed"), k + 1)
                        act.copy(u[:, k, HI, META:LEN], h[:, k, :]).then_inc(sem("mr_hi"), 1)
                act.wait_ge(sem("w_used"), MIX + 3 + 4 * n)
                w_hi(act, MIX + 4, n, 4, "full")
                act.wait_ge(sem("w_used"), MIX + 4 + 4 * n)
                w_hi(act, MIX + 5, n, 4, "full")
                if last:
                    for k in (KT - 1,):
                        act.wait_ge(sem("mixed"), k + 1)
                        act.copy(u[:, k, HI, META:LEN], h[:, k, :]).then_inc(sem("mr_hi"), 1)
            loop(act, KT, body)

        def mixed_lo(dve, ks):
            for k in ks:
                dve.wait_ge(sem("mr_hi"), k + 1)
                dve.tensor_tensor(u[:, k, LO, META:LEN], h[:, k, :], u[:, k, HI, META:LEN], ALU.subtract) \
                    .then_inc(sem("mr_lo"), 1)

        def dve_mix(dve):
            w_lo(dve, MIX + 1)
            for t in range(16):
                dve.wait_ge(sem("o_hi"), t + 1)
                dve.tensor_tensor(o_r[:, t, LO, :], big[:, t, :], o_r[:, t, HI, :], ALU.subtract) \
                    .then_inc(sem("o_lo"), 1)

            def body(n, first, last):
                for j in range(2):
                    dve.wait_ge(sem("sig"), 2 * n + j + 1)
                    w_lo(dve, MIX + j + 2, n, 4, "full")
                for j in range(2):
                    if last:
                        mixed_lo(dve, range(4 * j, min(4 * j + 4, KT - 1)))
                    dve.wait_ge(sem("w_used"), MIX + j + 3 + 4 * n)
                    if not first:
                        dve.wait_ge(sem("mixed"), n)
                    dve.tensor_tensor(sig[:, 2 + j, :], bank(2 + j), sig[:, j, :], ALU.mult).then_inc(sem("branch"), 1)
                    w_lo(dve, MIX + 4 + j, n, 4, "full")
                dve.wait_ge(sem("branch"), 2 * n + 2)
                dst = h[:, idx(n), :]
                s2, s3 = (sig[:, 2 + j, :] if isinstance(n, int) else sig[:, 2 + j:3 + j, :] for j in range(2))
                dve.tensor_tensor(dst, s2, s3, ALU.add).then_inc(sem("mixed"), 1)
            loop(dve, KT, body)

        NORMS = ("out", "e", "eo", "down0", "oo", "down1")

        def tiles_before(tag):
            return KT * NORMS.index(tag)

        def hs_before(tag):
            return KT * (NORMS.index(tag) - 1)

        def norms_done(tag):
            return NORMS.index(tag) + 1

        def res_units(name):
            return 3 if name in (("down", 0), ("down", 1)) else 1

        def pe_residual(pe, name, moving, ready, tag, banks_read, order=range(KT)):
            c0, per = FIRST[name], res_units(name)
            for name_, count in banks_read:
                pe.wait_ge(sem(name_), count)

            def body(i, first, last):
                for j in range(2):
                    if not first:
                        pe.wait_ge(sem("h_tile"), hs_before(tag) + 2 * i + j - 1)
                    if per == 1:
                        w_ready(pe, c0 + j, i, 2)
                        product(pe, bank(j), c0 + j, moving, order, ready=ready if first and j == 0 else None) \
                            .then_inc(sem("w_used"), 1)
                    else:
                        k0 = 0
                        for m, ks in enumerate(DOWN):
                            c = c0 + 3 * j + m
                            w_ready(pe, c, i, 6)
                            product(pe, bank(j), c, moving, range(k0, k0 + ks), start=m == 0, stop=m == 2, n0=k0,
                                    ready=ready if first and j == 0 else None) \
                                .then_inc(sem("w_used"), 1)
                            k0 += ks
            loop(pe, KT // 2, body)

        def load_residual(sp, name, dram):
            c0 = FIRST[name]

            def body(i, first, last):
                for j in range(2):
                    if res_units(name) == 1:
                        w_load(sp, c0 + j, panel(dram, (2 * i + j) * P), i, 2)
                    else:
                        k0 = 0
                        for m, ks in enumerate(DOWN):
                            w_load(sp, c0 + 3 * j + m, panel(dram, (2 * i + j) * P, ks, k0), i, 6)
                            k0 += ks
            loop(sp, KT // 2, body)

        def next_kind(c, last, k):
            return None if last else (KINDS[c - k] if c - k >= 0 else None)

        def w_next(split, eng, c, i, k, last, n_steps):
            if last:
                split(eng, c + i * k)
            else:
                split(eng, c, i, k, KINDS[c])

        def act_residual(act, name, gain, tag):
            c0, per = FIRST[name], res_units(name)

            def body(i, first, last):
                for j in range(2):
                    for m in range(per):
                        c = c0 + per * j + m
                        act.wait_ge(sem("w_used"), num(c, i, 2 * per) + 1)
                        if c + 2 - c0 >= 2 * per and last:
                            w_hi(act, c + 2 + i * 2 * per)
                        else:
                            w_hi(act, c + 2, i, 2 * per, KINDS[c + 2])
                    n = 2 * i + j
                    act.wait_ge(sem("h_tile"), hs_before(tag) + n + 1)
                    if not first:
                        act.wait_ge(sem("acc_done"), tiles_before(tag) + n - 1)
                    if gain:
                        hn = h[:, idx(n), :]
                        dst = u[:, n, HI, META:LEN] if isinstance(n, int) else u[:, bass.ds(n, 1), HI, META:LEN]
                        act.activation(dst, hn, ACT.Copy, scale=vcol(*gain_at(gain, n))).then_inc(sem("hs_hi"), 1)
                    sqj = sq[:, j, :] if isinstance(n, int) else sq[:, j:j + 1, :]
                    act.activation(sqj, h[:, idx(n), :], ACT.Square).then_inc(sem("squared"), 1)
            loop(act, KT // 2, body)

        def gain_at(gain, n):
            return (gain[0], gain[1] + n)

        def dve_residual(dve, name, gain, tag):
            c0, per = FIRST[name], res_units(name)

            def body(i, first, last):
                for j in range(2):
                    for m in range(per):
                        c = c0 + per * j + m
                        if c + 2 - c0 >= 2 * per and last:
                            w_lo(dve, c + 2 + i * 2 * per)
                        else:
                            w_lo(dve, c + 2, i, 2 * per, KINDS[c + 2])
                    n = 2 * i + j
                    dve.wait_ge(sem("w_used"), num(c0 + per * j + per - 1, i, 2 * per) + 1)
                    hn = h[:, idx(n), :]
                    b = bank(j) if isinstance(n, int) else bank(j).rearrange("p (a n) -> p a n", a=1)
                    dve.tensor_tensor(hn, b, hn, ALU.add).then_inc(sem("h_tile"), 1)
                    if gain:
                        dve.wait_ge(sem("hs_hi"), hs_before(tag) + n + 1)
                        dst, hi = (u[:, idx(n), part, META:LEN] for part in (LO, HI))
                        dve.scalar_tensor_tensor(out=dst, in0=hn, scalar=vcol(*gain_at(gain, n)), in1=hi,
                                                 op0=ALU.mult, op1=ALU.subtract).then_inc(sem("hs"), 1)
            loop(dve, KT // 2, body)

        def pool_squares(pool, tag):
            for n in range(KT):
                pool.wait_ge(sem("squared"), tiles_before(tag) + n + 1)
                if n == 0:
                    ins = pool.tensor_copy(acc[:, 0, :], sq[:, 0, :])
                else:
                    pool.wait_ge(sem("acc_done"), tiles_before(tag) + n)
                    ins = pool.tensor_tensor(acc[:, 0, :], acc[:, 0, :], sq[:, n % 2, :], ALU.add)
                ins.then_inc(sem("acc_done"), 1)

        def pe_stats(pe, tag, bc=True, tok=False):
            pe.wait_ge(sem("acc_done"), tiles_before(tag) + KT)
            if bc:
                ins = pe.matmul(bank(7), ones[:], acc[:, 0, :], start=True, stop=True)
            if tok:
                for t in range(NQ):
                    ins = pe.matmul(bank(6, t, t + 1), acc[:, 0, t * P:(t + 1) * P], ones[:, 0:1],
                                    start=True, stop=True)
            ins.then_inc(sem("summed"), 1)

        def act_stats(act, tag, bc=True, tok=False):
            act.wait_ge(sem("summed"), norms_done(tag))
            if tok:
                act.activation(sstok, bank(6, 0, NQ), ACT.Sqrt, scale=1.0 / D, bias=EPS).then_inc(sem("rms_tok"), 1)
            if bc:
                act.activation(rbc[:, 0, :], bank(7), ACT.Sqrt, scale=1.0 / D, bias=EPS).then_inc(sem("rms"), 1)

        def dve_stats(dve, tag, bc=True, tok=False):
            if tok:
                dve.wait_ge(sem("rms_tok"), 1 if tag == "down0" else 2)
                dve.reciprocal(rtok, sstok).then_inc(sem("rtok"), 1)
            if bc:
                dve.wait_ge(sem("rms"), norms_done(tag))
                dve.reciprocal(rbc[:, 0, :], rbc[:, 0, :]).then_inc(sem("rbc"), 1)
                dve.wait_ge(sem("rbc"), norms_done(tag))

        OUT = FIRST["out"]

        def load_out(sp):
            for n in range(KT):
                w_load(sp, OUT + n, panel(a["w_out"][0], n * P))
                if n % 2 == 1:
                    t = n // 2
                    if t == 0:
                        sp.wait_ge(sem("mixed"), KT)
                    if t >= 2:
                        sp.wait_ge(sem("x_again"), 2 * t - 2)
                    sp.dma_start(xin[:, t % 2, :], a["x"][0, t * P:(t + 1) * P, :]).then_inc(sem(f"x2_in{t % 2}"), 16)

        def pe_out(pe):
            for n in range(KT):
                w_ready(pe, OUT + n)
                if n >= 4:
                    pe.wait_ge(sem("m2"), n - 3)
                product(pe, bank(n % 4), OUT + n, u_real,
                        ready=(lambda k: pe.wait_ge(sem("mr_lo"), k + 1)) if n == 0 else None) \
                    .then_inc(sem("w_used"), 1)
                t, half = divmod(n, 2)
                if half == 0:
                    pe.wait_ge(sem(f"x2_in{t % 2}"), 16 * (t // 2 + 1))
                if n >= 2:
                    pe.wait_ge(sem("h_x"), n - 1)
                for k in range(4):
                    ins = pe.transpose(bank(4 + half, k * P, (k + 1) * P),
                                       xin[:, t % 2, (4 * half + k) * P:(4 * half + k + 1) * P], ident)
                ins.then_inc(sem("x_again"), 1)
            pe_stats(pe, "out")

        def act_out(act):
            for n in range(KT):
                act.wait_ge(sem("m2"), n + 1)
                if n < KT - 1:
                    w_hi(act, OUT + n + 2)
                if n >= 2:
                    act.wait_ge(sem("acc_done"), n - 1)
                act.activation(sq[:, n % 2, :], m2[:, n, :], ACT.Square).then_inc(sem("squared"), 1)
                if n == KT - 1:
                    w_hi(act, OUT + n + 2)
                act.wait_ge(sem("x_again"), n + 1)
                t, half = divmod(n, 2)
                act.copy(h[:, 4 * half:4 * half + 4, t * P:(t + 1) * P],
                         bank(4 + half).rearrange("p (k n) -> p k n", k=4)).then_inc(sem("h_x"), 1)
            act_stats(act, "out")
            for n in range(KT):
                act.wait_ge(sem("h_tile"), n + 1)
                act.activation(u[:, n, HI, META:LEN], h[:, n, :], ACT.Copy, scale=vcol("mix_g", n)) \
                    .then_inc(sem("hs_hi"), 1)
                if n >= 2:
                    act.wait_ge(sem("acc_done"), KT + n - 1)
                act.activation(sq[:, n % 2, :], h[:, n, :], ACT.Square).then_inc(sem("squared"), 1)

        def dve_out(dve):
            mixed_lo(dve, (KT - 1,))
            for n in range(KT):
                dve.wait_ge(sem("w_used"), OUT + n + 1)
                dve.tensor_copy(m2[:, n, :], bank(n % 4)).then_inc(sem("m2"), 1)
                w_lo(dve, OUT + n + 2)
            dve_stats(dve, "out")
            dve.wait_ge(sem("h_x"), KT)

            def h_low(n):
                dve.wait_ge(sem("hs_hi"), n + 1)
                dve.scalar_tensor_tensor(out=u[:, n, LO, META:LEN], in0=h[:, n, :], scalar=vcol("mix_g", n),
                                         in1=u[:, n, HI, META:LEN], op0=ALU.mult, op1=ALU.subtract) \
                    .then_inc(sem("hs"), 1)

            for n in range(KT):
                if n >= 2:
                    dve.wait_ge(sem("h_tile"), n - 1)
                dve.tensor_tensor(res_t[:, n % 2, :], m2[:, n, :], rbc[:, 0, :], ALU.mult).then_inc(sem("res"), 1)
                dve.wait_ge(sem("res"), n + 1)
                dve.scalar_tensor_tensor(out=h[:, n, :], in0=res_t[:, n % 2, :], scalar=vcol("post_g", n),
                                         in1=h[:, n, :], op0=ALU.mult, op1=ALU.add).then_inc(sem("h_tile"), 1)
                if n:
                    h_low(n - 1)
            h_low(KT - 1)

        EZ, EC, POOL = FIRST["even_z"], FIRST["even_c"], FIRST["pool"]
        CH = 4 * P

        def conv_unit(g):
            return EC + 3 * g + (1 if g else 0)

        def conv_bank(g, j):
            return j if g % 2 else 4 + j

        def load_even(sp):
            w = a["w_in_even_2"][0]
            for g in range(GROUPS):
                w_load(sp, EZ + g, panel(w, 3 * CH + g * P))
            wp = a["w_pool_2"][0]
            for g in range(GROUPS):
                for j, col in enumerate((CH, 2 * CH, 0)):
                    w_load(sp, conv_unit(g) + j, panel(w, col + g * P))
                if g == 0:
                    w_load(sp, POOL, [
                        (lambda r, lo=lo: r[:, lo * P:(lo + 2) * P].rearrange("p (g n) -> p g n", g=2),
                         wp[lo:lo + 2].rearrange("g p n -> p g n")) for lo in (0, 2)])

        def pe_even(pe):
            pe.wait_ge(sem("m2"), KT)
            w_ready(pe, EZ)
            w_ready(pe, EZ + 1)
            for k in range(KT):
                h_ready(pe, "e")(k)
                for g in range(2):
                    ins = product(pe, bank(g), EZ + g, u_real, (k,), start=k == 0, stop=k == KT - 1)
                    if k == KT - 1:
                        ins.then_inc(sem("w_used"), 1)
            pe_stats(pe, "e")
            for g in (2, 3):
                w_ready(pe, EZ + g)
                product(pe, bank(g), EZ + g, u_real).then_inc(sem("w_used"), 1)
            for g in range(GROUPS):
                for j in range(3):
                    w_ready(pe, conv_unit(g) + j)
                    if g == 0 and j == 2:
                        pe.wait_ge(sem("h_tile"), KT)
                    elif g == 1:
                        pe.wait_ge(sem("e_mix"), j + 1)
                    elif g >= 2:
                        pe.wait_ge(sem("e_read"), 3 * (g - 2) + j + 1)
                    product(pe, bank(conv_bank(g, j)), conv_unit(g) + j, u_real).then_inc(sem("w_used"), 1)
                if g == 0:
                    w_ready(pe, POOL)
                    for q in range(GROUPS):
                        pe.wait_ge(sem("pooled"), q + 1)
                        for n, (ws, ms) in enumerate(PASSES):
                            ins = pe.matmul(bank(q), w_tile(POOL, ws, q), pool_r[:, q, ms, :], start=n == 0,
                                            stop=n == 2)
                        ins.then_inc(sem("pool_mm" if q < GROUPS - 1 else "w_used"), 1)

        def act_even(act):
            units = iter(range(EZ + 2, EZ + 4 * GROUPS + 3))
            w_hi(act, next(units))
            w_hi(act, next(units))
            act_stats(act, "e")
            for g in range(GROUPS):
                if g:
                    w_hi(act, next(units))
                act.wait_ge(sem("e_p"), g + 1)
                act.copy(pool_r[:, g, HI, :], zpad[:, pooled_slot(g), 8:8 + SEQ]).then_inc(sem("e_phi"), 1)
            for g in range(GROUPS):
                c = conv_unit(g)
                w_hi(act, next(units))
                act.wait_ge(sem("e_read"), 3 * g + 2)
                act.activation(ecv[:, 0, :], cpad[:, 0, 0:SEQ], ACT.Copy, scale=vcol("conv_a", g)).then_inc(sem("e_t0"), 1)
                w_hi(act, next(units))
                if g == 0:
                    for q in range(GROUPS):
                        if q < GROUPS - 1:
                            act.wait_ge(sem("pool_mm"), q + 1)
                        else:
                            act.wait_ge(sem("w_used"), POOL + 1)
                        act.activation(mix_r[:, GROUPS + q, HI, :], bank(q), ACT.Copy, scale=vcol("pool_scale", q)) \
                            .then_inc(sem("e_mhi"), 1)
                if g < GROUPS - 1:
                    w_hi(act, next(units))
                act.wait_ge(sem("e_y"), g + 1)
                act.copy(mix_r[:, g, HI, :], ecv[:, 0, :]).then_inc(sem("e_yhi"), 1)
                if g == 0:
                    w_hi(act, next(units))

        def pooled_slot(g):
            return 2 - g % 2

        def dve_even(dve):
            chain = [0]

            def link(ins):
                chain[0] += 1
                ins.then_inc(sem("e_chain"), 1)
                dve.wait_ge(sem("e_chain"), chain[0])

            dve.memset(cpad[:, 0, 0:2], 0.0)
            link(dve.memset(zpad[:, :, 0:8], 0.0))
            units = iter(range(EZ + 2, EZ + 4 * GROUPS + 3))
            w_lo(dve, next(units))
            w_lo(dve, next(units))
            dve_stats(dve, "e")
            r, r2 = rbc[:, 0, :], sq[:, 0, :]
            link(dve.tensor_tensor(r2, r, r, ALU.mult))
            z = zpad[:, 0, 8:8 + SEQ]
            for g in range(GROUPS):
                w = 2 ** (g + 1)
                if g:
                    w_lo(dve, next(units))
                dve.wait_ge(sem("w_used"), EZ + g + 1)
                link(dve.tensor_tensor(z, bank(g), r, ALU.mult))
                src = 0
                for e in range(g + 1):
                    dst, d = 1 + e % 2, 2 ** e
                    link(dve.tensor_tensor(zpad[:, dst, 8:8 + SEQ], zpad[:, src, 8:8 + SEQ],
                                           zpad[:, src, 8 - d:8 - d + SEQ], ALU.add))
                    src = dst
                dst = 3 - src
                total, pooled = zpad[:, src, 8:8 + SEQ], zpad[:, dst, 8:8 + SEQ]
                head = w - 1
                link(dve.tensor_tensor(total[:, 0:head], total[:, 0:head], inv_count[:, 0:head], ALU.mult))
                dve.tensor_tensor(pooled[:, 0:head], total[:, 0:head], z[:, 0:head], ALU.subtract)
                dve.scalar_tensor_tensor(out=pooled[:, head:SEQ], in0=total[:, head:SEQ], scalar=1.0 / w,
                                         in1=z[:, head:SEQ], op0=ALU.mult, op1=ALU.subtract).then_inc(sem("e_p"), 1)
                dve.wait_ge(sem("e_phi"), g + 1)
                dve.tensor_tensor(pool_r[:, g, LO, :], pooled, pool_r[:, g, HI, :], ALU.subtract) \
                    .then_inc(sem("pooled"), 1)
            for g in range(GROUPS):
                c = conv_unit(g)
                cv = cpad[:, 0, 2:2 + SEQ]
                w_lo(dve, next(units))
                dve.wait_ge(sem("w_used"), c + 1)
                if g:
                    dve.wait_ge(sem("e_t0"), g)
                dve.tensor_tensor(cv, bank(conv_bank(g, 0)), r2, ALU.mult).then_inc(sem("e_read"), 1)
                dve.wait_ge(sem("e_read"), 3 * g + 1)
                dve.wait_ge(sem("w_used"), c + 2)
                dve.tensor_tensor(cv, bank(conv_bank(g, 1)), cv, ALU.mult).then_inc(sem("e_read"), 1)
                w_lo(dve, next(units))
                dve.wait_ge(sem("e_t0"), g + 1)
                for tap in (1, 2):
                    link(dve.scalar_tensor_tensor(out=ecv[:, 0, :], in0=cpad[:, 0, tap:tap + SEQ],
                                                  scalar=vcol("conv_a", 4 * tap + g), in1=ecv[:, 0, :],
                                                  op0=ALU.mult, op1=ALU.add))
                if g == 0:
                    for q in range(GROUPS):
                        dve.wait_ge(sem("e_mhi"), q + 1)
                        dve.scalar_tensor_tensor(out=mix_r[:, GROUPS + q, LO, :], in0=bank(q),
                                                 scalar=vcol("pool_scale", q), in1=mix_r[:, GROUPS + q, HI, :],
                                                 op0=ALU.mult, op1=ALU.subtract).then_inc(sem("e_mix"), 1)
                if g < GROUPS - 1:
                    w_lo(dve, next(units))
                dve.wait_ge(sem("w_used"), c + 3)
                dve.tensor_tensor(ecv[:, 0, :], bank(conv_bank(g, 2)), ecv[:, 0, :], ALU.mult).then_inc(sem("e_read"), 1)
                dve.wait_ge(sem("e_read"), 3 * g + 3)
                dve.tensor_tensor(ecv[:, 0, :], ecv[:, 0, :], r, ALU.mult).then_inc(sem("e_y"), 1)
                dve.wait_ge(sem("e_yhi"), g + 1)
                dve.tensor_tensor(mix_r[:, g, LO, :], ecv[:, 0, :], mix_r[:, g, HI, :], ALU.subtract) \
                    .then_inc(sem("e_ylo"), 1)
                if g == 0:
                    w_lo(dve, next(units))

        def even_mix_ready(pe, k):
            pe.wait_ge(sem("e_ylo"), k + 1) if k < GROUPS else pe.wait_ge(sem("e_mix"), k - GROUPS + 1)

        def load_ffn(sp, layer):
            c0 = FIRST[("ffn", layer)]

            def body(i, first, last):
                for j in range(4):
                    w = a["w_ffn_gate_2" if j % 2 == 0 else "w_ffn_up_2"][layer]
                    w_load(sp, c0 + j, panel(w, (2 * i + j // 2) * P), i, 4)
            loop(sp, FT // 2, body)

        def pe_ffn(pe, layer, tag):
            c0 = FIRST[("ffn", layer)]
            def body(i, first, last):
                for j in range(4):
                    w_ready(pe, c0 + j, i, 4)
                    if first and j < 2:
                        pe.wait_ge(sem("h_tile"), hs_before(tag) + KT - 1 + j)
                    if not first:
                        f = 2 * i + j // 2
                        pe.wait_ge(sem("ffn_g_read" if j % 2 == 0 else "ffn_a_done"), FT * layer + f - 1)
                    product(pe, bank(j), c0 + j, u_real, ready=h_ready(pe, tag) if first and j == 0 else None) \
                        .then_inc(sem("w_used"), 1)
                    if first and j == 0:
                        pe_stats(pe, tag)
            loop(pe, FT // 2, body)

        def act_ffn(act, layer, tag):
            c0 = FIRST[("ffn", layer)]
            act_stats(act, tag)

            def body(i, first, last):
                for j in range(2):
                    f = 2 * i + j
                    c = c0 + 2 * j
                    act.wait_ge(sem("w_used"), num(c, i, 4) + 1)
                    w_hi(act, c + 2 + i * 4) if last and j else w_hi(act, c + 2, i, 4, "full")
                    act.wait_ge(sem("ffn_g_read"), FT * layer + f + 1)
                    if not first:
                        act.wait_ge(sem("ffn_a_done"), FT * layer + f - 1)
                    act.activation(cnv[:, j, :], gpad[:, j, 0:SEQ], ACT.Copy, scale=ffn_vec(layer, 0, f)) \
                        .then_inc(sem("ffn_tap"), 1)
                    act.wait_ge(sem("ffn_conv"), 2 * FT * layer + 2 * f + 2)
                    act.activation(cnv[:, j, :], cnv[:, j, :], ACT.Silu, bias=ffn_vec(layer, 3, f)) \
                        .then_inc(sem("ffn_silu"), 1)
                    act.wait_ge(sem("w_used"), num(c + 1, i, 4) + 1)
                    w_hi(act, c + 3 + i * 4) if last and j else w_hi(act, c + 3, i, 4, "full")
                    act.wait_ge(sem("ffn_a_done"), FT * layer + f + 1)
                    dst = a_r[:, idx(f), HI, :]
                    act.copy(dst, hid[:, 0, :] if isinstance(f, int) else hid[:, 0:1, :]).then_inc(sem("ffn_a_hi"), 1)
            loop(act, FT // 2, body)

        def pool_ffn(pool, layer, tag):
            pool.wait_ge(sem("rbc"), norms_done(tag))

            def body(i, first, last):
                for j in range(2):
                    pool.wait_ge(sem("ffn_silu"), FT * layer + 2 * i + j + 1)
                    pool.tensor_tensor(cnv[:, j, :], cnv[:, j, :], rbc[:, 0, :], ALU.mult) \
                        .then_inc(sem("ffn_scaled"), 1)
            loop(pool, FT // 2, body)

        def dve_ffn(dve, layer, tag):
            c0 = FIRST[("ffn", layer)]
            dve_stats(dve, tag)
            dve.memset(gpad[:, :, 0:2], 0.0).then_inc(sem("ffn_gz"), 1)

            def body(i, first, last):
                for j in range(2):
                    f = 2 * i + j
                    c = c0 + 2 * j
                    dve.wait_ge(sem("w_used"), num(c, i, 4) + 1)
                    if not first:
                        dve.wait_ge(sem("ffn_conv"), 2 * FT * layer + 2 * f - 2)
                    dve.tensor_tensor(gpad[:, j, 2:2 + SEQ], bank(2 * j), rbc[:, 0, :], ALU.mult) \
                        .then_inc(sem("ffn_g_read"), 1)
                    w_lo(dve, c + 2 + i * 4) if last and j else w_lo(dve, c + 2, i, 4, "full")
                    dve.wait_ge(sem("ffn_tap"), FT * layer + f + 1)
                    for tap in (1, 2):
                        dve.scalar_tensor_tensor(out=cnv[:, j, :], in0=gpad[:, j, tap:tap + SEQ],
                                                 scalar=ffn_vec(layer, tap, f), in1=cnv[:, j, :],
                                                 op0=ALU.mult, op1=ALU.add).then_inc(sem("ffn_conv"), 1)
                        if tap == 1:
                            dve.wait_ge(sem("ffn_conv"), 2 * FT * layer + 2 * f + 1)
                    w_lo(dve, c + 3 + i * 4) if last and j else w_lo(dve, c + 3, i, 4, "full")
                    dve.wait_ge(sem("ffn_scaled"), FT * layer + f + 1)
                    dve.wait_ge(sem("w_used"), num(c + 1, i, 4) + 1)
                    if not (first and j == 0):
                        dve.wait_ge(sem("ffn_a_lo"), FT * layer + f)
                    dve.tensor_tensor(hid[:, 0, :], bank(2 * j + 1), cnv[:, j, :], ALU.mult) \
                        .then_inc(sem("ffn_a_done"), 1)
                    dve.wait_ge(sem("ffn_a_hi"), FT * layer + f + 1)
                    hi, lo = (a_r[:, idx(f), part, :] for part in (HI, LO))
                    hv = hid[:, 0, :] if isinstance(f, int) else hid[:, 0:1, :]
                    dve.tensor_tensor(lo, hv, hi, ALU.subtract).then_inc(sem("ffn_a_lo"), 1)
            loop(dve, FT // 2, body)

        OV, OU = FIRST["odd_v"], FIRST["odd_u"]

        def load_odd(sp):
            w = a["w_in_odd_2"][0]
            for m in range(KT):
                half, kp = divmod(m, KT // 2)
                w_load(sp, OV + m, [
                    (lambda r, j=j: r[:, j * SEQ:(j + 1) * SEQ],
                     w[(2 * kp + j) * P:(2 * kp + j + 1) * P, D + half * SEQ:D + (half + 1) * SEQ])
                    for j in range(2)])
                if m == 1:
                    sp.wait_ge(sem("h_tile"), hs_before("down0") + KT)
                    sp.dma_start(bbc[:, 0, :], a["b_spatial_2"].rearrange("a h t -> a (h t)").to_broadcast([P, D])) \
                        .then_inc(sem("b_in"), 16)
                    sp.dma_start(m2[:, 0:2, :].rearrange("p a (b s) -> p (a b) s", s=P),
                                 a["w_spatial_2"][0].rearrange("h t s -> t h s")).then_inc(sem("ws_in"), 16)
            for n in range(KT):
                w_load(sp, OU + n, panel(w, n * P))

        def pe_odd(pe):
            for m in range(KT):
                half, kp = divmod(m, KT // 2)
                w_ready(pe, OV + m)
                if half == 0:
                    pe.wait_ge(sem("hs"), hs_before("down0") + 2 * kp + 2)
                if m == KT // 2:
                    pe.wait_ge(sem("rms"), norms_done("down0"))
                    pe.wait_ge(sem("rms_tok"), 1)
                    pe.wait_ge(sem("wst"), 2)
                for t in (0, 2, 3, 1):
                    if m == 0:
                        pe.wait_ge(sem("h_tile"), hs_before("down0") + KT - 1 + (t == 1))
                    for j in range(2):
                        k = 2 * kp + j
                        for n, (us, ws) in enumerate(PASSES):
                            ins = pe.matmul(bank(4 * half + t), u[:, k, us, META + t * P:META + (t + 1) * P],
                                            wsp[:, (OV + m) % 2, ws, j * SEQ:(j + 1) * SEQ],
                                            start=k == 0 and n == 0, stop=k == KT - 1 and n == 2,
                                            skip_group_check=True)
                ins.then_inc(sem("w_used"), 1)
                if m == 0:
                    pe_stats(pe, "down0", bc=True, tok=True)
                    pe.wait_ge(sem("ws_in"), 16)
                    wn = m2[:, 0:2, :].rearrange("p a (b s) -> p (a b) s", s=P)
                    for hd in range(C_HEADS):
                        ins = pe.transpose(bank(4 + hd // 4, (hd % 4) * P, (hd % 4 + 1) * P), wn[:, hd, :], ident)
                    ins.then_inc(sem("ws_t"), 1)

            def u_product(n):
                w_ready(pe, OU + n)
                pe.wait_ge(sem("ov_read"), n + 1) if n < 4 else pe.wait_ge(sem("ou_read"), n - 3)
                product(pe, bank(n % 4), OU + n, u_real).then_inc(sem("w_used"), 1)

            def spatial(hd):
                if hd == 0:
                    pe.wait_ge(sem("vs_lo"), 2 * NQ)
                if hd >= 4:
                    pe.wait_ge(sem("gate"), hd - 3)
                for t in range(NQ):
                    if hd == 0:
                        pe.wait_ge(sem("ws_lo"), t + 1)
                    for m, (vs, ws) in enumerate(PASSES):
                        ins = pe.matmul(bank(4 + hd % 4, t * P, (t + 1) * P), vs_r[:, t, vs, hd * P:(hd + 1) * P],
                                        ws_r[t][:, ws, hd * P:(hd + 1) * P], start=m == 0, stop=m == 2)
                ins.then_inc(sem("sgu"), 1)

            for n in range(KT):
                u_product(n)
            for hd in range(C_HEADS):
                spatial(hd)

        V_CHUNKS = {4: (0,), 5: (1,), 6: (2,), 7: (3,), 8: (4, 5), 9: (6, 7)}

        def act_odd(act):
            act_stats(act, "down0", bc=True, tok=True)
            for m in range(2 * KT):
                act.wait_ge(sem("w_used"), OV + m + 1)
                w_hi(act, OV + m + 2)
                for n in V_CHUNKS.get(m, ()):
                    half, t = divmod(n, NQ)
                    v = odt[:, n % 2, :]
                    if n == 0:
                        act.wait_ge(sem("rtok"), 1)
                    if n >= 2:
                        act.wait_ge(sem("vs_lo"), n - 1)
                    act.activation(v, bank(4 * half + t), ACT.Gelu, scale=rtok[:, t:t + 1]).then_inc(sem("ov_read"), 1)
                    act.wait_ge(sem("ov_read"), n + 1)
                    act.copy(vs_r[:, t, HI, half * SEQ:(half + 1) * SEQ], v).then_inc(sem("vs_hi"), 1)
                    if n:
                        act.wait_ge(sem("sqv"), n)
                    act.activation(sq[:, 0, :], v, ACT.Square, accum_out=ssv_part[:, n:n + 1]).then_inc(sem("sqv"), 1)
                if m == 10:
                    act.wait_ge(sem("ssv"), 1)
                    act.activation(ssv, ssv, ACT.Sqrt, scale=1.0 / D, bias=EPS).then_inc(sem("sdv"), 1)
                if 11 <= m < 15:
                    t = m - 11
                    if t == 0:
                        act.wait_ge(sem("rsv"), 1)
                        act.wait_ge(sem("wst"), 2)
                    act.activation(ws_r[t][:, HI, :], wst[:, 0, :], ACT.Copy, scale=rsv[:, t:t + 1]) \
                        .then_inc(sem("ws_hi"), 1)
                if m >= KT:
                    n = m - KT
                    act.wait_ge(sem("ou_read"), n + 1)
                    act.activation(m2[:, n, :], m2[:, n, :], ACT.Gelu).then_inc(sem("ou"), 1)
            for hd in range(C_HEADS):
                act.wait_ge(sem("gate_y"), hd + 1)
                if hd == C_HEADS - 2:
                    act.wait_ge(sem("sgu"), C_HEADS)
                act.copy(mix_r[:, hd, HI, :], odt[:, hd % 2, :]).then_inc(sem("gate_hi"), 1)

        def dve_odd(dve):
            w_lo(dve, OV + 2)
            dve_stats(dve, "down0", bc=True, tok=True)
            dve.wait_ge(sem("ws_t"), 1)
            dve.wait_ge(sem("b_in"), 16)
            for half in range(2):
                dve.tensor_tensor(wst[:, 0, half * 512:(half + 1) * 512].rearrange("p (h n) -> p h n", h=4),
                                  bank(4 + half).rearrange("p (h n) -> p h n", h=4),
                                  triu.rearrange("p (a n) -> p a n", a=1).to_broadcast([P, 4, P]), ALU.mult) \
                    .then_inc(sem("wst"), 1)
            for m in range(1, 2 * KT):
                w_lo(dve, OV + m + 2)
                for n in V_CHUNKS.get(m, ()):
                    half, t = divmod(n, NQ)
                    hi, lo = (vs_r[:, t, part, half * SEQ:(half + 1) * SEQ] for part in (HI, LO))
                    dve.wait_ge(sem("vs_hi"), n + 1)
                    dve.tensor_tensor(lo, odt[:, n % 2, :], hi, ALU.subtract).then_inc(sem("vs_lo"), 1)
                if m == 10:
                    dve.wait_ge(sem("sqv"), 2 * NQ)
                    dve.tensor_tensor(ssv, ssv_part[:, 0:4], ssv_part[:, 4:8], ALU.add).then_inc(sem("ssv"), 1)
                    dve.wait_ge(sem("sdv"), 1)
                    dve.reciprocal(rsv, ssv).then_inc(sem("rsv"), 1)
                    dve.wait_ge(sem("rsv"), 1)
                if 11 <= m < 15:
                    t = m - 11
                    dve.wait_ge(sem("ws_hi"), t + 1)
                    dve.scalar_tensor_tensor(out=ws_r[t][:, LO, :], in0=wst[:, 0, :], scalar=rsv[:, t:t + 1],
                                             in1=ws_r[t][:, HI, :], op0=ALU.mult, op1=ALU.subtract) \
                        .then_inc(sem("ws_lo"), 1)
                if m >= KT:
                    n = m - KT
                    dve.wait_ge(sem("w_used"), OU + n + 1)
                    dve.tensor_tensor(m2[:, n, :], bank(n % 4), rbc[:, 0, :], ALU.mult).then_inc(sem("ou_read"), 1)
            for hd in range(C_HEADS):
                y = odt[:, hd % 2, :]
                dve.wait_ge(sem("sgu"), hd + 1)
                if hd >= 2:
                    dve.wait_ge(sem("gate_lo"), hd - 1)
                dve.scalar_tensor_tensor(out=y.rearrange("p (t n) -> p t n", t=NQ),
                                         in0=bank(4 + hd % 4).rearrange("p (t n) -> p t n", t=NQ),
                                         scalar=vcol("sgu_g", hd),
                                         in1=bbc[:, :, hd * P:(hd + 1) * P].to_broadcast([P, NQ, P]),
                                         op0=ALU.mult, op1=ALU.add).then_inc(sem("gate"), 1)
                dve.wait_ge(sem("gate"), hd + 1)
                dve.wait_ge(sem("ou"), hd + 1)
                dve.tensor_tensor(y, y, m2[:, hd, :], ALU.mult).then_inc(sem("gate_y"), 1)
                if hd:
                    dve_gate_lo(dve, hd - 1)
            dve_gate_lo(dve, C_HEADS - 1)

        def dve_gate_lo(dve, hd):
            dve.wait_ge(sem("gate_hi"), hd + 1)
            dve.tensor_tensor(mix_r[:, hd, LO, :], odt[:, hd % 2, :], mix_r[:, hd, HI, :], ALU.subtract) \
                .then_inc(sem("gate_lo"), 1)

        def h_ready(pe, tag):
            return lambda k: pe.wait_ge(sem("hs"), hs_before(tag) + k + 1)

        def load_final(sp):
            sp.wait_ge(sem("ffn_a_lo"), 2 * FT)
            sp.dma_start(gfin[:, 0, :], a["final_norm_2"].rearrange("(a n) -> a n", a=1).to_broadcast([P, D])) \
                .then_inc(sem("gf_in"), 16)
            for t in range(NQ):
                sp.wait_ge(sem("fin"), 2 * t + 2)
                sp.dma_start(out[t * P:(t + 1) * P, :], xin[:, t % 2, :]).then_inc(sem(f"stored{t % 2}"), 16)
            for s in range(2):
                sp.wait_ge(sem(f"stored{s}"), 32)

        def pe_final(pe):
            pe.wait_ge(sem("h_tile"), hs_before("down1") + KT)
            for t in range(NQ):
                for half in range(2):
                    n = 2 * t + half
                    if n >= 4:
                        pe.wait_ge(sem("fin_s"), n - 3)
                    for k in range(4):
                        ins = pe.transpose(bank(2 + n % 4, k * P, (k + 1) * P), h[:, 4 * half + k, t * P:(t + 1) * P],
                                           ident)
                    ins.then_inc(sem("fin_t"), 1)
                if t == 0:
                    pe_stats(pe, "down1", bc=False, tok=True)

        def act_final(act):
            act_stats(act, "down1", bc=False, tok=True)
            act.wait_ge(sem("rtok"), 2)
            for t in range(NQ):
                for half in range(2):
                    n = 2 * t + half
                    act.wait_ge(sem("fin_t"), n + 1)
                    if t >= 2:
                        act.wait_ge(sem(f"stored{t % 2}"), 16)
                    act.activation(xin[:, t % 2, half * 512:(half + 1) * 512], bank(2 + n % 4), ACT.Copy,
                                   scale=rtok[:, t:t + 1]).then_inc(sem("fin_s"), 1)

        def dve_final(dve):
            dve_stats(dve, "down1", bc=False, tok=True)
            dve.wait_ge(sem("gf_in"), 16)
            for n in range(2 * NQ):
                t, half = divmod(n, 2)
                dve.wait_ge(sem("fin_s"), n + 1)
                o = xin[:, t % 2, half * 512:(half + 1) * 512]
                dve.tensor_tensor(o, o, gfin[:, 0, half * 512:(half + 1) * 512], ALU.mult).then_inc(sem("fin"), 1)

        def a_tiles(k, part):
            return a_r[:, k, part, :]

        def mix_tiles(k, part):
            return mix_r[:, k, part, :]

        block = ctx.enter_context(nc.Block())

        @block.sync
        def _(sp):
            dma_prologue(sp)
            load_prologue(sp)
            load_attention(sp)
            load_mix(sp)
            load_out(sp)
            load_even(sp)
            load_residual(sp, "even_out", a["w_out_even_2"][0])
            load_ffn(sp, 0)
            load_residual(sp, ("down", 0), a["w_ffn_down_2"][0])
            load_odd(sp)
            load_residual(sp, "odd_out", a["w_out_odd_2"][0])
            load_ffn(sp, 1)
            load_residual(sp, ("down", 1), a["w_ffn_down_2"][1])
            load_final(sp)

        @block.gpsimd
        def _(pool):
            pool_prologue(pool)
            pool_attention(pool)
            pool_squares(pool, "out")
            pool_squares(pool, "e")
            pool_squares(pool, "eo")
            pool_ffn(pool, 0, "eo")
            pool_squares(pool, "down0")
            pool_squares(pool, "oo")
            pool_ffn(pool, 1, "oo")
            pool_squares(pool, "down1")

        @block.scalar
        def _(act):
            act_prologue(act)
            steps(act, lambda *x: act_step(act, *x))
            act_mix(act)
            act_out(act)
            act_even(act)
            act_residual(act, "even_out", ("ffn_g", 0), "eo")
            act_ffn(act, 0, "eo")
            act_residual(act, ("down", 0), ("mix_g", KT), "down0")
            act_odd(act)
            act_residual(act, "odd_out", ("ffn_g", KT), "oo")
            act_ffn(act, 1, "oo")
            act_residual(act, ("down", 1), None, "down1")
            act_final(act)

        @block.vector
        def _(dve):
            dve_prologue(dve)
            steps(dve, lambda *x: dve_step(dve, *x))
            dve_mix(dve)
            dve_out(dve)
            dve_even(dve)
            dve_residual(dve, "even_out", ("ffn_g", 0), "eo")
            dve_ffn(dve, 0, "eo")
            dve_residual(dve, ("down", 0), ("mix_g", KT), "down0")
            dve_odd(dve)
            dve_residual(dve, "odd_out", ("ffn_g", KT), "oo")
            dve_ffn(dve, 1, "oo")
            dve_residual(dve, ("down", 1), None, "down1")
            dve_final(dve)

        @block.tensor
        def _(pe):
            pe_prologue(pe)
            steps(pe, lambda *x: pe_step(pe, *x[:7]))
            pe_mix(pe)
            pe_out(pe)
            pe_even(pe)
            pe_residual(pe, "even_out", mix_tiles, lambda k: even_mix_ready(pe, k), "eo",
                        (("e_read", 3 * GROUPS - 1),), (4, 5, 6, 7, 0, 1, 2, 3))
            pe_ffn(pe, 0, "eo")
            pe_residual(pe, ("down", 0), a_tiles, lambda k: pe.wait_ge(sem("ffn_a_lo"), k + 1), "down0",
                        (("ffn_g_read", FT - 1), ("ffn_a_done", FT - 1)))
            pe_odd(pe)
            pe_residual(pe, "odd_out", mix_tiles, lambda k: pe.wait_ge(sem("gate_lo"), k + 1), "oo",
                        (("ou_read", KT),))
            pe_ffn(pe, 1, "oo")
            pe_residual(pe, ("down", 1), a_tiles, lambda k: pe.wait_ge(sem("ffn_a_lo"), FT + k + 1), "down1",
                        (("ffn_g_read", 2 * FT - 1), ("ffn_a_done", 2 * FT - 1)))
            pe_final(pe)


def rope_tables():
    half = ROPE // 2
    freq = (np.float32(ROPE_THETA) ** (-np.arange(half, dtype=np.float32) / np.float32(half))).astype(np.float32)
    ang = np.arange(LEN, dtype=np.float32)[None, :] * freq[:, None]
    cos, sin = np.cos(ang).astype(np.float32), np.sin(ang).astype(np.float32)
    return np.concatenate([cos, cos, -sin, sin], axis=0)


def constant_tables():
    i = np.arange(P)
    ident = np.eye(P, dtype=np.float32)
    mask = np.where(i[None, :] > i[:, None], np.float32(MASKED), np.float32(0.0)).astype(np.float32)
    triu = (i[:, None] <= i[None, :]).astype(np.float32)
    counts = np.broadcast_to((np.float32(1.0) / (np.arange(16, dtype=np.float32) + 1)), (P, 16))
    return np.ascontiguousarray(np.concatenate([ident, mask, triu, counts], axis=1))


_INS = ["x", "meta_tokens", "pre_norm_g", "w_in", "fox_forget_b", "mla_q_norm_g", "mla_kv_norm_g", "w_uq",
        "w_ukv", "w_br_mla", "w_br_fox", "w_out", "post_norm_g", "norm_mix_2", "norm_ffn_2", "final_norm_2",
        "w_in_even_2", "conv_a_2", "w_pool_2", "pool_scale_2", "w_out_even_2", "w_in_odd_2", "sgu_norm_2",
        "w_spatial_2", "b_spatial_2", "w_out_odd_2", "w_ffn_gate_2", "w_ffn_up_2", "conv_ffn_2",
        "b_conv_ffn_2", "w_ffn_down_2"]


def kernel(**inputs):
    import concourse.bacc as _bacc
    from concourse.bass_utils import run_bass_kernel_spmd as _run

    nc = _bacc.Bacc("TRN2", target_bir_lowering=False, num_devices=1)
    arrays, aps = {}, {}

    def declare(name, array):
        arrays[f"in_{name}_dram"] = array
        return nc.dram_tensor(f"in_{name}_dram", array.shape, mybir.dt.from_np(array.dtype),
                              kind="ExternalInput").ap()

    for name in _INS:
        aps[name] = declare(name, np.ascontiguousarray(inputs[name]))
    rope = declare("rope_tables", rope_tables())
    consts = declare("constants", constant_tables())
    out = nc.dram_tensor("out_dram", (1, SEQ, D), F32, kind="ExternalOutput").ap()
    hybrid_blocks_kernel(nc, aps, rope, consts, out[0])
    r = _run(nc, [arrays], core_ids=[0])
    return r.results[0]["out_dram"]
```

```python
from contextlib import ExitStack
import math

import numpy as np

import concourse.bass as bass
from concourse import mybir

F32 = mybir.dt.float32
F32R = mybir.dt.float32r
ACT = mybir.ActivationFunctionType
ALU = mybir.AluOpType
AX = mybir.AxisListType

P = 128
D = 1024
KT = D // P
SEQ = 512
META = 16
LEN = SEQ + META
HALF = LEN // 2
NQ = SEQ // P
EPS = 1e-6
HEADS = 16
PAIRS = HEADS // 2
STEPS = 2 * PAIRS
NOPE, ROPE = 64, 32
HD = 64
Q_RANK, KV_RANK = 256, 128
MLA_SCALE = 1.0 / math.sqrt(NOPE + ROPE)
FOX_SCALE = 1.0 / math.sqrt(HD)
ROPE_THETA = 10000.0
MASKED = -1e30
W_CQ = 0
W_CKV = W_CQ + Q_RANK
W_KPE = W_CKV + KV_RANK
W_ZM = W_KPE + ROPE
W_FQ = W_ZM + D
W_FK = W_FQ + D
W_FV = W_FK + D
W_F = W_FV + D
W_ZF = W_F + HEADS
W_GA = W_ZF + D
W_GB = W_GA + D
GROUPS = 4
DFF = 2816
FT = DFF // P
DOWN = (8, 8, 6)
C_HEADS = 8
UNIT = KT * P
VEC_ROWS = (("pre_g", 8), ("q_g", 2), ("kv_g", 1), ("post_g", 8), ("mix_g", 16), ("ffn_g", 16),
            ("pool_scale", 4), ("sgu_g", 8), ("conv_a", 12))
FFN_ROWS = 4 * FT

B_S, B_T, B_O, B_META = 4, 6, 7, 3
V_META = 256
ARENA = 2 * 2 * 2 * SEQ + 2 * 2 * 2 * LEN + 4 * NQ * P + 2 * P + 4 * NQ * SEQ + 2 * SEQ + 4 * SEQ + 2 * LEN


def vec_column(name, k=0):
    at = 0
    for n, rows in VEC_ROWS:
        if n == name:
            return at + k
        at += rows
    raise KeyError(name)


N_VEC = sum(r for _, r in VEC_ROWS)


def plan_units():
    kinds, first = [], {}

    def phase(name, *ks):
        first[name] = len(kinds)
        kinds.extend(ks)

    phase("pro", "full", "kf", "full", "full")
    for s in range(STEPS):
        phase(("attn", s), *(("full", "qkv", "full") if s < PAIRS else ("full",) * 3))
    phase("mix", *("full",) * (4 * KT))
    phase("out", *("full",) * KT)
    phase("even_z", *("full",) * GROUPS)
    phase("even_c", *("full",) * 3)
    phase("pool", "pool")
    phase("even_c1", *("full",) * (3 * (GROUPS - 1)))
    phase("even_out", *("full",) * KT)
    phase(("ffn", 0), *("full",) * (2 * FT))
    phase(("down", 0), *("full", "full", "six") * KT)
    phase("odd_v", *("full",) * KT)
    phase("odd_u", *("full",) * KT)
    phase("odd_out", *("full",) * KT)
    phase(("ffn", 1), *("full",) * (2 * FT))
    phase(("down", 1), *("full", "full", "six") * KT)
    return kinds, first


KINDS, FIRST = plan_units()


def hybrid_blocks_kernel(nc, a, rope_t, consts, out):
    forget_dram = nc.dram_tensor("forget_rows", [HEADS, 2, LEN], F32, kind="Internal").ap()

    with ExitStack() as ctx:
        def sb(name, shape, dt=F32):
            return ctx.enter_context(nc.sbuf_tensor(name, shape, dt))

        sems = {}

        def sem(name):
            if name not in sems:
                sems[name] = ctx.enter_context(nc.semaphore(name))
            return sems[name]

        ps = ctx.enter_context(nc.psum_tensor("ps", [P, 8 * 512], F32))

        def bank(b, lo=0, hi=512, rows=slice(0, P)):
            return ps[rows, b * 512 + lo:b * 512 + hi]

        raw = sb("w_raw", [P, 2, UNIT])
        wsp = sb("w_split", [P, 2, 2, UNIT], F32R)
        u = sb("u", [P, KT, 2, LEN], F32R)
        ra = sb("arena_r", [P, ARENA], F32R)
        big = sb("big", [P, 16, SEQ])
        tmp = sb("tmp", [P, 5120])
        cst = sb("cst", [P, 400])
        ident_r = sb("ident_r", [P, P], F32R)
        mask_r = sb("mask_r", [P, P], F32R)
        ones = sb("ones", [P, P])
        vec = sb("vec", [P, N_VEC + 2 * FFN_ROWS])
        st = sb("stats", [P, 64])
        ident = cst[:, 0:128]
        triu = cst[:, 256:384]
        inv_count = cst[:, 384:400]

        def view(t, at, *dims):
            n = math.prod(dims)
            v = t[:, at:at + n]
            if len(dims) == 2:
                v = v.rearrange("p (a b) -> p a b", a=dims[0])
            elif len(dims) == 3:
                v = v.rearrange("p (a b c) -> p a b c", a=dims[0], b=dims[1])
            elif len(dims) == 4:
                v = v.rearrange("p (a b c d) -> p a b c d", a=dims[0], b=dims[1], c=dims[2])
            return v, at + n

        q_t, at = view(ra, 0, 4, 2, SEQ)
        k_t, at = view(ra, at, 4, 2, LEN)
        v_t, at = view(ra, at, 2, NQ, 2, P)
        v_m, at = view(ra, at, 2, P)
        p_t, at = view(ra, at, 2, 2 * NQ, SEQ)
        p_m, at = view(ra, at, 2, SEQ)
        cq_r, at = view(ra, at, 2, 2, SEQ)
        ckv_r, at = view(ra, at, 2, LEN)
        o_r, _ = view(ra, 0, 16, 2, SEQ)
        mix_r, at = view(ra, 0, KT, 2, SEQ)
        pool_r, _ = view(ra, at, GROUPS, 2, SEQ)
        vs_r, at = view(ra, at, NQ, 2, D)
        ws_r = [view(ra, at + 2 * D * t, 2, D)[0] for t in range(NQ - 1)] + [view(ra, (KT - 2) * 2 * SEQ, 2, D)[0]]
        a_r, _ = view(ra, 0, FT, 2, SEQ)

        prob, at = view(tmp, 0, 2, LEN)
        v_f, _ = view(tmp, at, 1, LEN)
        rot, at = view(tmp, at, 2, SEQ)
        rt, at = view(tmp, at, 2, SEQ)
        prob_m, at = view(tmp, at, NQ, P)
        rope_s, at = view(tmp, at, 2, LEN)
        rbc, at = view(tmp, 0, 1, SEQ)
        acc, at = view(tmp, at, 1, SEQ)
        sq, at = view(tmp, at, 2, SEQ)
        rest = at
        xin, _ = view(tmp, rest, 2, D)
        res_t, _ = view(tmp, rest + 2048, 2, SEQ)
        gfin, _ = view(tmp, rest + 2048, 1, D)
        sig, _ = view(tmp, rest, 4, SEQ)
        gpad, at = view(tmp, rest, 2, 516)
        cnv, at = view(tmp, at, 2, SEQ)
        hid, at = view(tmp, at, 1, SEQ)
        cpad, at = view(tmp, rest, 1, 516)
        ecv, at = view(tmp, at, 1, SEQ)
        zpad, at = view(tmp, at, 3, 8 + SEQ)
        wst, at = view(tmp, rest, 1, D)
        bbc, at = view(tmp, at, 1, D)
        odt, at = view(tmp, at, 2, SEQ)
        h = big[:, 0:KT, :]
        m2 = big[:, KT:16, :]

        ssx, rsx = st[:, 0:5], st[:, 5:10]
        mx, neg, rs, ri = (st[:, 10 + 8 * j:18 + 8 * j] for j in range(4))
        rtok, sstok = st[:, 42:46], st[:, 46:50]
        ssv, rsv = st[:, 50:54], st[:, 54:58]
        ssv_part = st[:, 10:18]
        sd = st[:, 58:63]

        HI, LO = 0, 1
        PASSES = ((HI, HI), (HI, LO), (LO, HI))

        def vcol(name, k=0):
            c = vec_column(name) + k
            return vec[:, c:c + 1] if isinstance(k, int) else vec[:, bass.ds(c, 1)]

        def ffn_vec(layer, row, f):
            c = N_VEC + layer * FFN_ROWS + row * FT + f
            return vec[:, c:c + 1] if isinstance(f, int) else vec[:, bass.ds(c, 1)]

        def idx(i):
            return i if isinstance(i, int) else bass.ds(i, 1)

        def loop(eng, n, body):
            body(0, True, n == 1)
            if n > 3:
                with eng.Fori(1, n - 1) as i:
                    body(i, False, False)
            elif n == 3:
                body(1, False, False)
            if n > 1:
                body(n - 1, False, True)

        def num(c, i=0, k=0):
            return c + i * k if k else c

        def w_load(sp, c, parts, i=0, k=0):
            if c >= 2 or k:
                sp.wait_ge(sem("w_lo"), num(c, i, k) - 1)
            for dst, src in parts:
                sp.dma_start(dst(raw[:, c % 2, :]), src).then_inc(sem(f"w_load{c % 2}"), 16)

        def split_pairs(kind, r, s):
            if kind == "full":
                return [(r[:, 0:UNIT], s[:, 0:UNIT])]
            if kind == "six":
                return [(r[:, 0:6 * P], s[:, 0:6 * P])]
            if kind == "pool":
                return [(r[:, 0:4 * P], s[:, 0:4 * P])]
            if kind == "kf":
                r3, s3 = (x[:, 0:UNIT].rearrange("p (k n) -> p k n", k=KT) for x in (r, s))
                return [(r3[:, :, 0:16], s3[:, :, 0:16]), (r3[:, :, 0:16], s3[:, :, 16:32]),
                        (r3[:, :, 32:64], s3[:, :, 32:64]), (r3[:, :, 48:64], s3[:, :, 64:80]),
                        (r3[:, :, 32:48], s3[:, :, 80:96])]
            rq = r[:, 0:384].rearrange("p (g n) -> p g n", g=4)
            sq_ = s[:, 0:512].rearrange("p (g n) -> p g n", g=4)
            rk = r[:, 384:640].rearrange("p (h t d) -> p t h d", h=2, t=2)
            sk = s[:, 512:768].rearrange("p (t h d) -> p t h d", h=2, t=2)
            return [(rq[:, :, 0:96], sq_[:, :, 0:96]), (rq[:, :, 80:96], sq_[:, :, 96:112]),
                    (rq[:, :, 64:80], sq_[:, :, 112:128]),
                    (rk[:, 0], sk[:, 0]), (rk[:, 1], sk[:, 1])]

        def w_hi(act, c, i=0, k=0, kind=None):
            if c >= len(KINDS):
                return
            kind = kind or KINDS[c]
            half = k // 2
            act.wait_ge(sem(f"w_load{c % 2}"), 32 * (c // 2 + 1) + (i * (32 * half) if k else 0))
            if c >= 2:
                act.wait_ge(sem("w_used"), num(c, i, k) - 1)
            pieces = split_pairs(kind, raw[:, c % 2, :], wsp[:, c % 2, HI, :])
            for n, (src, dst) in enumerate(pieces):
                ins = act.copy(dst, src)
            ins.then_inc(sem("w_hi"), 1)

        def w_lo(dve, c, i=0, k=0, kind=None):
            if c >= len(KINDS):
                return
            kind = kind or KINDS[c]
            dve.wait_ge(sem("w_hi"), num(c, i, k) + 1)
            src = split_pairs(kind, raw[:, c % 2, :], wsp[:, c % 2, HI, :])
            dst = split_pairs(kind, raw[:, c % 2, :], wsp[:, c % 2, LO, :])
            for (r, hi), (_, lo) in zip(src, dst):
                ins = dve.tensor_tensor(lo, r, hi, ALU.subtract)
            ins.then_inc(sem("w_lo"), 1)

        def w_ready(pe, c, i=0, k=0):
            pe.wait_ge(sem("w_lo"), num(c, i, k) + 1)

        def w_tile(c, part, k, width=P):
            return wsp[:, c % 2, part, k * P:k * P + width]

        def panel(dram, col, rows=KT, row0=0):
            halves = [(rows // 2, rows), (0, rows // 2)]
            out_ = []
            for lo, hi in halves:
                src = dram[(row0 + lo) * P:(row0 + hi) * P, bass.ds(col, P)] if not isinstance(col, int) \
                    else dram[(row0 + lo) * P:(row0 + hi) * P, col:col + P]
                out_.append((lambda r, lo=lo, hi=hi: r[:, lo * P:hi * P].rearrange("p (k n) -> p k n", k=hi - lo),
                             src.rearrange("(k p) n -> p k n", p=P)))
            return out_

        def product(pe, out_ap, c, moving, ks=range(KT), start=True, stop=True, n0=0, ready=None):
            last = None
            total = [(k, ws, ms) for k in ks for ws, ms in PASSES]
            for n, (k, ws, ms) in enumerate(total):
                if ready and n % len(PASSES) == 0:
                    ready(k)
                last = pe.matmul(out_ap, w_tile(c, ws, k - n0), moving(k, ms),
                                 start=start and n == 0, stop=stop and n == len(total) - 1,
                                 skip_group_check=True)
            return last

        def u_real(k, part):
            return u[:, k, part, META:LEN]

        PRO = FIRST["pro"]
        nat = big.rearrange("p a b -> p (a b)")[:, 0:5 * D].rearrange("p (t d) -> p t d", t=5)
        junk = big.rearrange("p a b -> p (a b)")[:, 5 * D:6 * D]
        stage = tmp[:, 0:3 * P].rearrange("p (s n) -> p s n", s=3)
        w_in = a["w_in"][0]
        bigf = big.rearrange("p a b -> p (a b)")
        dg = bigf[:, 6 * D:6 * D + 5 * P].rearrange("p (t n) -> p t n", t=5)
        mt = bigf[:, 6 * D + 5 * P:6 * D + 6 * P].rearrange("p (k n) -> p k n", k=KT)
        ksq = bigf[:, 0:3 * LEN].rearrange("p (t n) -> p t n", t=3)
        krs = bigf[:, 3 * LEN:5 * LEN].rearrange("p (t n) -> p t n", t=2)
        kn = bigf[:, 5 * LEN:7 * LEN].rearrange("p (t n) -> p t n", t=2)
        kro = bigf[:, 9 * SEQ:9 * SEQ + 3 * LEN].rearrange("p (t n) -> p t n", t=3)
        pf = [bigf[:, 9 * SEQ + (3 + j) * LEN:9 * SEQ + (4 + j) * LEN] for j in range(3)]
        fx, fe, fm = (t[0:HEADS, :] for t in pf)
        forget_r = p_t[0:HEADS, 1].rearrange("p j n -> p (j n)")[:, 0:2 * LEN] \
            .rearrange("p (j n) -> p j n", j=2)
        fbias = st[0:HEADS, 63:64]

        def dma_prologue(sp):
            for t in range(NQ):
                sp.dma_start(nat[:, t, :], a["x"][0, t * P:(t + 1) * P, :]).then_inc(sem(f"x_in{t}"), 16)
                if t == 0:
                    sp.dma_start(nat[0:META, 4, :], a["meta_tokens"]).then_inc(sem("meta_in"), 16)
                    sp.dma_start(cst[:], consts).then_inc(sem("cst_in"), 16)
            rows = 0
            for name, n in VEC_ROWS:
                src = {"pre_g": a["pre_norm_g"], "q_g": a["mla_q_norm_g"], "kv_g": a["mla_kv_norm_g"],
                       "post_g": a["post_norm_g"], "mix_g": a["norm_mix_2"], "ffn_g": a["norm_ffn_2"],
                       "pool_scale": a["pool_scale_2"], "sgu_g": a["sgu_norm_2"],
                       "conv_a": a["conv_a_2"][0]}[name]
                sp.dma_start(stage[rows:rows + n, 0, :], src.rearrange("a (k p) -> (a k) p", p=P)) \
                    .then_inc(sem("vec_in"), 16)
                rows += n
            for layer in range(2):
                sp.dma_start(stage[0:3 * FT, 1 + layer, :],
                             a["conv_ffn_2"][layer].rearrange("a (k p) -> (a k) p", p=P)).then_inc(sem("vec_in"), 16)
                sp.dma_start(stage[3 * FT:4 * FT, 1 + layer, :],
                             a["b_conv_ffn_2"][layer:layer + 1].rearrange("a (k p) -> (a k) p", p=P)) \
                    .then_inc(sem("vec_in"), 16)
            sp.dma_start(fbias, a["fox_forget_b"].rearrange("a h -> h a"), allow_slow_non_contiguous=True) \
                .then_inc(sem("rope_in"), 16)
            sp.dma_start(rope_s[64:96, :, :], rope_t.rearrange("(s p) n -> p s n", s=2)).then_inc(sem("rope_in"), 16)

        N_VEC_DMA = 16 * (len(VEC_ROWS) + 4)

        def load_prologue(sp):
            w_load(sp, PRO, panel(w_in, W_CKV))
            w_load(sp, PRO + 1, [
                (lambda r, at_=at_, n=n: r[:, 0:UNIT].rearrange("p (k n) -> p k n", k=KT)[:, :, at_:at_ + n],
                 w_in[:, col:col + n].rearrange("(k p) n -> p k n", p=P))
                for at_, n, col in ((0, HEADS, W_F), (32, ROPE, W_KPE))])
            for t in range(2):
                w_load(sp, PRO + 2 + t, panel(w_in, W_CQ + t * P))

        def act_prologue(act):
            for t in range(5):
                n = P if t < 4 else META
                act.wait_ge(sem(f"x_in{t}" if t < 4 else "meta_in"), 16)
                if t:
                    act.wait_ge(sem("x_ss"), t)
                else:
                    act.wait_ge(sem("x_ms"), 1)
                act.activation(junk[0:n, :], nat[0:n, t, :], ACT.Square, accum_out=ssx[0:n, t:t + 1]) \
                    .then_inc(sem("x_ss"), 1)
            act.wait_ge(sem("x_ss"), 5)
            act.activation(sd, ssx, ACT.Sqrt, scale=1.0 / D, bias=EPS).then_inc(sem("x_sd"), 1)
            w_hi(act, PRO)
            act.wait_ge(sem("cst_in"), 16)
            act.copy(ident_r[:], ident).then_inc(sem("cst_r"), 1)
            act.copy(mask_r[:], cst[:, 128:256]).then_inc(sem("cst_r"), 1)
            act.wait_ge(sem("meta_t"), 2)
            act.copy(u[:, :, HI, 0:META], mt).then_inc(sem("u_hi"), 1)
            for k in range(KT):
                act.wait_ge(sem("x_tr"), k + 1)
                act.activation(u[:, k, HI, META:LEN], bank(k % 4), ACT.Copy, scale=vcol("pre_g", k)) \
                    .then_inc(sem("u_hi"), 1)
                if k == 3:
                    w_hi(act, PRO + 1)
            act.wait_ge(sem("w_used"), PRO + 1)
            w_hi(act, PRO + 2)
            for half in range(2):
                ins = act.activation(ksq[:, 0, half * HALF:(half + 1) * HALF], bank(5 + half, 0, HALF), ACT.Square)
            ins.then_inc(sem("c_sq"), 1)
            act.wait_ge(sem("w_used"), PRO + 2)
            w_hi(act, PRO + 3)
            act.wait_ge(sem("c_sum"), 1)
            for half, b in enumerate((3, 0)):
                ins = act.activation(krs[:, 0, half * HALF:(half + 1) * HALF], bank(b, 0, HALF), ACT.Sqrt,
                                     scale=1.0 / KV_RANK, bias=EPS)
            ins.then_inc(sem("c_sd"), 1)
            act.wait_ge(sem("f_x"), 1)
            act.activation(fe, fx, ACT.Abs).then_inc(sem("f_act"), 1)
            act.wait_ge(sem("f_act"), 1)
            act.activation(fe, fe, ACT.Exp, scale=-1.0).then_inc(sem("f_act"), 1)
            act.wait_ge(sem("f_act"), 2)
            act.activation(fe, fe, ACT.Ln, bias=1.0).then_inc(sem("f_act"), 1)
            act.wait_ge(sem("w_used"), PRO + 3)
            w_hi(act, PRO + 4)
            act.activation(ksq[:, 1, 0:SEQ], bank(7), ACT.Square).then_inc(sem("c_sq"), 1)
            act.wait_ge(sem("c_n"), 1)
            act.copy(ckv_r[:, HI, :], kn[:, 0, :]).then_inc(sem("c_hi"), 1)
            act.wait_ge(sem("kpe_rot"), 1)
            for t in range(4):
                ins = act.copy(k_t[64:96, t, HI, :], kro[64:96, 2, :])
            ins.then_inc(sem("kpe_hi"), 1)
            act.wait_ge(sem("w_used"), PRO + 4)
            act.activation(ksq[:, 2, 0:SEQ], bank(1), ACT.Square).then_inc(sem("c_sq"), 1)
            act.wait_ge(sem("f_cum"), 1)
            act.copy(forget_r[:, HI, :], fm).then_inc(sem("forget_hi"), 1)
            act.wait_ge(sem("c_sum"), 2)
            act.activation(krs[:, 1, 0:SEQ], bank(3), ACT.Sqrt, scale=1.0 / Q_RANK, bias=EPS).then_inc(sem("c_sd"), 1)
            for t in range(2):
                act.wait_ge(sem("c_n"), 2 + t)
                act.copy(cq_r[:, t, HI, :], kn[:, 1 - t, 0:SEQ]).then_inc(sem("c_hi"), 1)

        def pool_prologue(pool):
            pool.memset(ones[:], 1.0).then_inc(sem("ones"), 1)
            pool.memset(v_t.bitcast(F32), 0.0)
            pool.memset(v_m.bitcast(F32), 0.0).then_inc(sem("pads"), 1)
            pool.wait_ge(sem("vec"), 1)
            pool.memset(prob_m, 0.0).then_inc(sem("pads"), 1)

        def dve_prologue(dve):
            dve.memset(ssx[:, 4:5], 1.0).then_inc(sem("x_ms"), 1)
            dve.wait_ge(sem("x_sd"), 1)
            dve.reciprocal(rsx, sd).then_inc(sem("x_rs"), 1)
            dve.wait_ge(sem("x_rs"), 1)
            dve.wait_ge(sem("cst_in"), 16)
            for t in (4, 0, 1, 2, 3):
                n = P if t < 4 else META
                ins = dve.tensor_scalar(dg[0:n, t, 0:n], cst[0:n, 0:n], rsx[0:n, t:t + 1], None, ALU.mult)
            ins.then_inc(sem("x_dg"), 1)
            dve.wait_ge(sem("vec_tr"), 1)
            dve.tensor_copy(vec[:, 0:N_VEC], bank(7, 0, N_VEC))
            for layer in range(2):
                ins = dve.tensor_copy(vec[:, N_VEC + layer * FFN_ROWS:N_VEC + (layer + 1) * FFN_ROWS],
                                      bank(7, 128 * (layer + 1), 128 * (layer + 1) + FFN_ROWS))
            ins.then_inc(sem("vec"), 1)
            dve.wait_ge(sem("vec"), 1)
            dve.wait_ge(sem("meta_t"), 1)
            gains = vec[:, 0:KT].rearrange("p (k a) -> p k a", a=1).to_broadcast([P, KT, META])
            dve.tensor_tensor(mt, bank(4, 0, KT * META).rearrange("p (k n) -> p k n", k=KT), gains, ALU.mult) \
                .then_inc(sem("meta_t"), 1)
            w_lo(dve, PRO)
            dve.wait_ge(sem("u_hi"), 1)
            dve.tensor_tensor(u[:, :, LO, 0:META], mt, u[:, :, HI, 0:META], ALU.subtract).then_inc(sem("u_lo"), 1)
            for k in range(KT):
                dve.wait_ge(sem("u_hi"), k + 2)
                dve.scalar_tensor_tensor(out=u[:, k, LO, META:LEN], in0=bank(k % 4), scalar=vcol("pre_g", k),
                                         in1=u[:, k, HI, META:LEN], op0=ALU.mult, op1=ALU.subtract) \
                    .then_inc(sem("u_lo"), 1)
                if k == 4:
                    w_lo(dve, PRO + 1)
            w_lo(dve, PRO + 2)
            w_lo(dve, PRO + 3)
            halves = [(b, slice(half * HALF, (half + 1) * HALF)) for half, b in enumerate((4, 2))]
            dve.wait_ge(sem("w_used"), PRO + 2)
            dve.wait_ge(sem("rope_in"), 32)
            for b, cols in halves:
                ins = dve.tensor_scalar(fx[:, cols], bank(b, 0, HALF, rows=slice(0, HEADS)), fbias, None, ALU.add)
            ins.then_inc(sem("f_x"), 1)
            dve.wait_ge(sem("c_sd"), 1)
            dve.reciprocal(krs[:, 0, :], krs[:, 0, :]).then_inc(sem("c_rs"), 1)
            dve.wait_ge(sem("c_rs"), 1)
            for half in range(2):
                cols = slice(half * HALF, (half + 1) * HALF)
                ins = dve.scalar_tensor_tensor(out=kn[:, 0, cols], in0=bank(5 + half, 0, HALF), scalar=vcol("kv_g"),
                                               in1=krs[:, 0, cols], op0=ALU.mult, op1=ALU.mult)
            ins.then_inc(sem("c_n"), 1)
            for s in range(2):
                for b, cols in halves:
                    ins = dve.tensor_tensor(kro[64:96, s, cols], bank(b, 0, HALF, rows=slice(32 + 32 * s, 64 + 32 * s)),
                                            rope_s[64:96, s, cols], ALU.mult)
            ins.then_inc(sem("kpe_t"), 1)
            dve.wait_ge(sem("kpe_t"), 1)
            dve.tensor_tensor(kro[64:96, 2, :], kro[64:96, 0, :], kro[64:96, 1, :], ALU.add).then_inc(sem("kpe_rot"), 1)
            dve.wait_ge(sem("f_act"), 3)
            dve.scalar_tensor_tensor(out=fm, in0=fx, scalar=0.0, in1=fe, op0=ALU.min, op1=ALU.subtract) \
                .then_inc(sem("f_dve"), 1)
            dve.wait_ge(sem("f_dve"), 1)
            dve.wait_ge(sem("ones"), 1)
            dve.tensor_tensor_scan(fx, ones[0:HEADS, 0:1].to_broadcast([HEADS, LEN]), fm, 0.0, ALU.mult, ALU.add) \
                .then_inc(sem("f_dve"), 1)
            dve.wait_ge(sem("f_dve"), 2)
            dve.tensor_scalar(fm, fx, 1.0 / FOX_SCALE, None, ALU.mult).then_inc(sem("f_cum"), 1)
            w_lo(dve, PRO + 4)
            dve.wait_ge(sem("c_hi"), 1)
            dve.tensor_tensor(ckv_r[:, LO, :], kn[:, 0, :], ckv_r[:, HI, :], ALU.subtract).then_inc(sem("c_lo"), 1)
            dve.wait_ge(sem("kpe_hi"), 1)
            for t in range(4):
                ins = dve.tensor_tensor(k_t[64:96, t, LO, :], kro[64:96, 2, :], k_t[64:96, t, HI, :], ALU.subtract)
            ins.then_inc(sem("kpe_lo"), 1)
            dve.wait_ge(sem("forget_hi"), 1)
            dve.tensor_tensor(forget_r[:, LO, :], fm, forget_r[:, HI, :], ALU.subtract).then_inc(sem("forget_lo"), 1)
            dve.wait_ge(sem("c_sd"), 2)
            dve.reciprocal(krs[:, 1, 0:SEQ], krs[:, 1, 0:SEQ]).then_inc(sem("c_rs"), 1)
            dve.wait_ge(sem("c_rs"), 2)
            dve.wait_ge(sem("c_lo"), 1)
            for t, b in enumerate((7, 1)):
                dve.scalar_tensor_tensor(out=kn[:, 1 - t, 0:SEQ], in0=bank(b), scalar=vcol("q_g", t),
                                         in1=krs[:, 1, 0:SEQ], op0=ALU.mult, op1=ALU.mult).then_inc(sem("c_n"), 1)
            for t in range(2):
                dve.wait_ge(sem("c_hi"), 2 + t)
                dve.tensor_tensor(cq_r[:, t, LO, :], kn[:, 1 - t, 0:SEQ], cq_r[:, t, HI, :], ALU.subtract) \
                    .then_inc(sem("c_lo"), 1)

        def pe_prologue(pe):
            pe.wait_ge(sem("cst_in"), 16)
            pe.wait_ge(sem("vec_in"), N_VEC_DMA)
            pe.transpose(bank(7, 0, N_VEC), stage[0:N_VEC, 0, :], ident[0:N_VEC, 0:N_VEC])
            for layer in range(2):
                ins = pe.transpose(bank(7, 128 * (layer + 1), 128 * (layer + 1) + FFN_ROWS),
                                   stage[0:FFN_ROWS, 1 + layer, :], ident[0:FFN_ROWS, 0:FFN_ROWS])
            ins.then_inc(sem("vec_tr"), 1)
            pe.wait_ge(sem("x_dg"), 1)
            for k in range(KT):
                ins = pe.matmul(bank(4, k * META, (k + 1) * META), nat[0:META, 4, k * P:(k + 1) * P],
                                dg[0:META, 4, 0:META], start=True, stop=True)
            ins.then_inc(sem("meta_t"), 1)

            def halves(c, k, banks, width=P):
                for n, (ws, ms) in enumerate(PASSES):
                    for half, b in enumerate(banks):
                        ins = pe.matmul(bank(b, 0, HALF, rows=slice(0, width)), w_tile(c, ws, k, width),
                                        u[:, k, ms, half * HALF:(half + 1) * HALF],
                                        start=k == 0 and n == 0, stop=k == KT - 1 and n == 2, skip_group_check=True)
                return ins

            def ckv(k):
                if k == 0:
                    w_ready(pe, PRO)
                pe.wait_ge(sem("u_lo"), k + 2)
                ins = halves(PRO, k, (5, 6))
                if k == KT - 1:
                    ins.then_inc(sem("w_used"), 1)

            for k in range(KT):
                if k >= 4:
                    pe.wait_ge(sem("u_lo"), k - 2)
                for t in range(NQ):
                    ins = pe.matmul(bank(k % 4, t * P, (t + 1) * P), nat[:, t, k * P:(k + 1) * P], dg[:, t, :],
                                    start=True, stop=True)
                ins.then_inc(sem("x_tr"), 1)
                if k >= 2:
                    ckv(k - 2)
            ckv(KT - 2)
            ckv(KT - 1)
            w_ready(pe, PRO + 1)
            for k in range(KT):
                ins = halves(PRO + 1, k, (4, 2), 96)
            ins.then_inc(sem("w_used"), 1)
            pe.wait_ge(sem("ones"), 1)
            pe.wait_ge(sem("c_sq"), 1)
            for half, b in enumerate((3, 0)):
                ins = pe.matmul(bank(b, 0, HALF), ones[:], ksq[:, 0, half * HALF:(half + 1) * HALF],
                                start=True, stop=True)
            ins.then_inc(sem("c_sum"), 1)
            pe.wait_ge(sem("vec"), 1)
            for t, b in enumerate((7, 1)):
                w_ready(pe, PRO + 2 + t)
                product(pe, bank(b), PRO + 2 + t, u_real).then_inc(sem("w_used"), 1)
            pe.wait_ge(sem("c_sq"), 3)
            pe.wait_ge(sem("c_sd"), 1)
            for t in range(2):
                ins = pe.matmul(bank(3), ones[:], ksq[:, 1 + t, 0:SEQ], start=t == 0, stop=t == 1)
            ins.then_inc(sem("c_sum"), 1)

        MIX = FIRST["mix"]

        def n_real(b):
            return P * (b % NQ + 1)

        def s_cols(b, meta=True):
            return slice(B_S * 512 + 512 - n_real(b), B_S * 512 + 512 + (META if meta else 0))

        def pe_scores(pe, pr, b, fox, par, turn):
            hh, i = divmod(b, NQ)
            slot = 2 * par + hh
            rows = slice(0, 97 if fox else 96)
            if b == 0:
                pe.wait_ge(sem("q_split"), pr + 1)
                pe.wait_ge(sem("k_split"), pr + 1)
                if fox:
                    pe.wait_ge(sem(f"rows{par}"), 32 * turn + (0 if par else 32))
                else:
                    pe.wait_ge(sem("kpe_lo"), 1)
                    pe.wait_ge(sem("cst_r"), 2)
            if not (isinstance(pr, int) and pr == 0 and b == 0):
                pe.wait_ge(sem("exped"), 8 * pr + b)
                if b == 0:
                    pe.wait_ge(sem("pm_split"), pr)
            for n, (qs, ks) in enumerate(PASSES):
                pe.matmul(ps[:, s_cols(b, False)], q_t[rows, slot, qs, i * P:(i + 1) * P],
                          k_t[rows, slot, ks, META:META + n_real(b)], start=n == 0, stop=False,
                          skip_group_check=True)
            pe.matmul(bank(B_S, 384, 512), ident_r[:], mask_r[:], start=False, stop=True, skip_group_check=True)
            for n, (qs, ks) in enumerate(PASSES):
                ins = pe.matmul(bank(B_S + 1, 0, META), q_t[rows, slot, qs, i * P:(i + 1) * P],
                                k_t[rows, slot, ks, 0:META], start=n == 0, stop=n == 2)
            ins.then_inc(sem("scores"), 1)

        def pe_transposes(pe, pr, b):
            pe.wait_ge(sem("normed"), 8 * pr + b + 1)
            if not (isinstance(pr, int) and pr == 0 and b == 0):
                pe.wait_ge(sem("p_split"), 8 * pr + b)
            base = 512 - n_real(b)
            for j in range(b % NQ + 1):
                ins = pe.transpose(bank(B_T, j * P, (j + 1) * P),
                                   prob[:, b % 2, base + j * P:base + (j + 1) * P], ident)
            ins.then_inc(sem("transposed"), 1)

        def pe_transposes_meta(pe, pr):
            pe.wait_ge(sem("normed"), 8 * pr + 8)
            for i in range(NQ):
                ins = pe.transpose(bank(B_S, i * P, (i + 1) * P), prob_m[:, i, :], ident)
            ins.then_inc(sem("pm_transposed"), 1)

        def pe_values(pe, pr, hh, blocks=range(NQ)):
            pe.wait_ge(sem("p_split"), 8 * pr + 4 * hh + 4)
            if hh == 0 and 0 in blocks:
                pe.wait_ge(sem("v_split"), pr + 1)
                if not (isinstance(pr, int) and pr == 0):
                    pe.wait_ge(sem("gated"), pr)
            for j in blocks:
                for n, (vs, pp) in enumerate(PASSES):
                    pe.matmul(bank(B_O, j * P, 512), v_t[:, vs, j, hh, :], p_t[:, hh, pp * NQ + j, j * P:512],
                              start=hh == 0 and j == 0 and n == 0, stop=False, skip_group_check=True)
            if hh == 1:
                pe.wait_ge(sem("pm_split"), pr + 1)
                for n, (vs, pp) in enumerate(PASSES):
                    ins = pe.matmul(bank(B_O), v_m[0:48, vs, :], p_m[0:48, pp, :], start=False, stop=n == 2,
                                    skip_group_check=True)
                ins.then_inc(sem("values"), 1)

        def mla_q(pe, c, hh):
            for n, (k, ws, ms) in enumerate([(k, ws, ms) for k in range(2) for ws, ms in PASSES]):
                g = 2 * k + hh
                ins = pe.matmul(bank(hh), wsp[:, c % 2, ws, g * P:(g + 1) * P], cq_r[:, k, ms, :],
                                start=n == 0, stop=n == 5)
            return ins

        def products_mla(pe, s, c, kk=0, i=0):
            later = not (isinstance(s, int) and s == 0)

            def z_mla(half):
                if half == 0:
                    w_ready(pe, c, i, kk)
                    if later:
                        pe.wait_ge(sem("q_split"), s)
                ins = product(pe, bank(0), c, u_real, range(4 * half, 4 * half + 4), start=half == 0, stop=half == 1)
                if half:
                    ins.then_inc(sem("w_used"), 1)

            def k_and_meta():
                w_ready(pe, c + 1, i, kk)
                if later:
                    pe.wait_ge(sem("v_split"), s)
                    pe.wait_ge(sem("z_read"), 2 * s)
                else:
                    pe.wait_ge(sem("c_lo"), 3)
                wk = [wsp[:, (c + 1) % 2, part, 512:640] for part in range(2)]
                wv = [wsp[:, (c + 1) % 2, part, 640:768] for part in range(2)]
                for n, (ws, ms) in enumerate(PASSES):
                    pe.matmul(bank(2), wk[ws], ckv_r[:, ms, META:LEN], start=n == 0, stop=n == 2)
                for n, (ws, ms) in enumerate(PASSES):
                    pe.matmul(bank(B_META, 0, META), wk[ws], ckv_r[:, ms, 0:META], start=n == 0, stop=n == 2)
                for n, (ws, ms) in enumerate(PASSES):
                    ins = pe.matmul(bank(B_META, V_META, V_META + P), ckv_r[:, ms, 0:P], wv[ws],
                                    start=n == 0, stop=n == 2)
                ins.then_inc(sem("k_done"), 1)
                mla_q(pe, c + 1, 1).then_inc(sem("q1_done"), 1)

            def q():
                pe.wait_ge(sem("z_read"), 2 * s + 1)
                mla_q(pe, c + 1, 0).then_inc(sem("q_done"), 1)

            def z_fox(part):
                if part == 0:
                    w_ready(pe, c + 2, i, kk)
                    pe.wait_ge(sem("k_split"), s + 1)
                ins = product(pe, bank(2), c + 2, u_real, (2 * part, 2 * part + 1), start=part == 0, stop=part == 3)
                if part == 3:
                    ins.then_inc(sem("w_used"), 1)

            def v():
                pe.wait_ge(sem("q1_split"), s + 1)
                wv = [wsp[:, (c + 1) % 2, part, 640:768] for part in range(2)]
                for t in range(NQ):
                    for n, (ws, ms) in enumerate(PASSES):
                        ins = pe.matmul(bank(1, t * P, (t + 1) * P), ckv_r[:, ms, META + t * P:META + (t + 1) * P],
                                        wv[ws], start=n == 0, stop=n == 2)
                ins.then_inc(sem("w_used"), 1)
                z_fox(3)

            return [lambda: z_mla(0), lambda: z_mla(1), k_and_meta, q] + \
                   [lambda part=part: z_fox(part) for part in range(3)] + [v]

        def products_fox(pe, s, c, kk=0, i=0):
            def feature(j, k):
                if k == 0:
                    w_ready(pe, c + j, i, kk)
                    if j == 0:
                        pe.wait_ge(sem("q_split"), s)
                        pe.wait_ge(sem("k_split"), s)
                        if isinstance(s, int) and s == PAIRS:
                            pe.wait_ge(sem("v_split"), s)
                            pe.wait_ge(sem("z_read"), 2 * s)
                    elif j == 1:
                        pe.wait_ge(sem("v_split"), s)
                    else:
                        pe.wait_ge(sem("q_split"), s + 1)
                if j == 0:
                    ins = product(pe, bank(1), c, u_real, (k,), start=k == 0, stop=k == KT - 1)
                else:
                    banks = ((0, 3), (2, 1))[j - 1]
                    for n, (ws, ms) in enumerate(PASSES):
                        for half, b in enumerate(banks):
                            ins = pe.matmul(bank(b, 0, HALF), w_tile(c + j, ws, k),
                                            u[:, k, ms, half * HALF:(half + 1) * HALF],
                                            start=k == 0 and n == 0, stop=k == KT - 1 and n == 2,
                                            skip_group_check=True)
                if k == KT - 1:
                    ins.then_inc(sem("w_used"), 1)

            def part(b):
                for m in range(3 * b, 3 * b + 3):
                    feature(*divmod(m, KT))

            return [lambda b=b: part(b) for b in range(8)]

        def products_gates(pe):
            def part(b):
                j, q = divmod(b, 4)
                if q == 0:
                    w_ready(pe, MIX + j)
                if b == 0:
                    pe.wait_ge(sem("k_split"), STEPS)
                ins = product(pe, bank(j), MIX + j, u_real, (2 * q, 2 * q + 1), start=q == 0, stop=q == 3)
                if q == 3:
                    ins.then_inc(sem("w_used"), 1)

            return [lambda b=b: part(b) for b in range(8)]

        def fox_v_transposes(pe, s):
            pe.wait_ge(sem("v_copied"), s - PAIRS + 1)
            for t in range(NQ):
                pe.transpose(bank(2, t * P, (t + 1) * P), v_f[:, 0, META + t * P:META + (t + 1) * P], ident)
            pe.transpose(bank(B_META, V_META, V_META + P, rows=slice(0, META)), v_f[:, 0, 0:META], ident) \
                .then_inc(sem("v_transposed"), 1)

        def pe_step(pe, s, attn, gemm, par, c, kk=0, i=0):
            parts = [None] * 8
            if gemm == "gates":
                parts = products_gates(pe)
            elif gemm:
                parts = (products_mla if gemm == "mla" else products_fox)(pe, s, c, kk, i)
            pr = s - 1
            for b in range(8):
                if attn:
                    pe_scores(pe, pr, b, attn == "fox", 1 - par, i)
                if parts[b]:
                    parts[b]()
                if attn and b:
                    pe_transposes(pe, pr, b - 1)
            if attn:
                pe_values(pe, pr, 0, (0, 1))
                pe_transposes(pe, pr, 7)
                pe_transposes_meta(pe, pr)
                pe_values(pe, pr, 0, (2, 3))
            if gemm == "fox":
                fox_v_transposes(pe, s)
            if attn:
                pe_values(pe, pr, 1)

        def act_exp(act, pr, b, fox):
            act.wait_ge(sem("neg"), 8 * pr + b + 1)
            if not (isinstance(pr, int) and pr == 0 and b < 2):
                act.wait_ge(sem("transposed"), 8 * pr + b - 1)
            act.activation(prob[:, b % 2, 512 - n_real(b):LEN], ps[:, s_cols(b)], ACT.Exp, bias=neg[:, b:b + 1],
                           scale=FOX_SCALE if fox else MLA_SCALE, accum_out=rs[:, b:b + 1]) \
                .then_inc(sem("exped"), 1)

        def p_views(b):
            hh, i = divmod(b, NQ)
            src = bank(B_T, 0, (i + 1) * P).rearrange("p (j n) -> p j n", n=P)
            hi, lo = (p_t[:, hh, part * NQ:part * NQ + i + 1, i * P:(i + 1) * P] for part in range(2))
            return src, hi, lo

        def act_p(act, pr, b):
            act.wait_ge(sem("transposed"), 8 * pr + b + 1)
            if not (isinstance(pr, int) and pr == 0):
                act.wait_ge(sem("values"), pr)
            if isinstance(pr, int) and pr == 0 and b == NQ:
                act.wait_ge(sem("forget_out"), 16)
            src, hi, _ = p_views(b)
            act.copy(hi, src).then_inc(sem("p_hi"), 1)

        def act_z(act, tile, b, c, kk=0, i=0):
            act.wait_ge(sem("w_used"), num(c, i, kk) + 1)
            z = bank(b) if isinstance(tile, int) else bank(b).rearrange("p (a n) -> p a n", a=1)
            act.copy(big[:, idx(tile), :], z).then_inc(sem("z_read"), 1)

        def act_silu(act, tile, n):
            tiles = big[:, tile:tile + n, :] if isinstance(tile, int) else big[:, bass.ds(tile, n), :]
            act.activation(tiles, tiles, ACT.Silu).then_inc(sem("z_silu"), 1)

        def q_pieces(gemm, par, heads=(0, 1)):
            slot, out_ = 2 * par, []
            for hh in heads:
                if gemm == "mla":
                    out_ += [(bank(hh, rows=slice(0, NOPE)), q_t[0:NOPE, slot + hh], slice(0, SEQ)),
                             (rot[64:96, hh, :], q_t[64:96, slot + hh], slice(0, SEQ))]
                else:
                    out_.append((bank(1, rows=slice(64 * hh, 64 * hh + 64)), q_t[0:HD, slot + hh], slice(0, SEQ)))
            return out_

        def k_pieces(gemm, par):
            slot = 2 * par
            if gemm == "mla":
                parts = ((bank(2), slice(META, LEN)), (bank(B_META, 0, META), slice(0, META)))
            else:
                parts = ((bank(0, 0, HALF), slice(0, HALF)), (bank(3, 0, HALF), slice(HALF, LEN)))
            return [(src[64 * hh:64 * hh + 64], k_t[0:HD, slot + hh], cols) for src, cols in parts for hh in range(2)]

        def v_pieces(part, gemm):
            src = bank(1 if gemm == "mla" else 2).rearrange("p (n h d) -> p n h d", n=NQ, h=2)
            dst = v_t[:, part].rearrange("p n h (a d) -> p n (h a) d", a=2)[:, :, 0:4:3, :]
            out_ = [(src, dst)]
            for hh in range(2):
                out_.append((bank(B_META, V_META + 64 * hh, V_META + 64 * hh + 64, rows=slice(0, META)),
                             v_m[32 * hh:32 * hh + META, part, 64 * hh:64 * hh + 64]))
            return out_

        def old_scores_done(eng, s):
            if not (isinstance(s, int) and s < 2):
                eng.wait_ge(sem("scores"), 8 * s - 8)

        def act_q_mla(act, s, hh, par):
            act.wait_ge(sem("rotated"), 2 * s + 2 - hh)
            act.wait_ge(sem("q1_done" if hh else "q_done"), s + 1)
            old_scores_done(act, s)
            for src, dst, cols in q_pieces("mla", par, (hh,)):
                ins = act.copy(dst[:, HI, cols], src)
            ins.then_inc(sem("q1_hi" if hh else "q_hi"), 1)

        def act_q_fox(act, s, c, par, kk=0, i=0):
            act.wait_ge(sem("w_used"), num(c, i, kk) + 1)
            old_scores_done(act, s)
            for src, dst, cols in q_pieces("fox", par):
                ins = act.copy(dst[:, HI, cols], src)
            ins.then_inc(sem("q_hi"), 1)

        def act_k(act, s, c, gemm, par, kk=0, i=0):
            if gemm == "mla":
                act.wait_ge(sem("k_done"), s + 1)
            else:
                act.wait_ge(sem("w_used"), num(c + 1, i, kk) + 1)
            old_scores_done(act, s)
            for src, dst, cols in k_pieces(gemm, par):
                ins = act.copy(dst[:, HI, cols], src)
            ins.then_inc(sem("k_hi"), 1)

        def act_v_copy(act, s, c, kk=0, i=0):
            act.wait_ge(sem("w_used"), num(c + 2, i, kk) + 1)
            if isinstance(s, int) and s == PAIRS:
                act.wait_ge(sem("q_split"), PAIRS)
            else:
                act.wait_ge(sem("v_transposed"), s - PAIRS)
            act.copy(v_f[:, 0, 0:HALF], bank(2, 0, HALF))
            act.copy(v_f[:, 0, HALF:LEN], bank(1, 0, HALF)).then_inc(sem("v_copied"), 1)

        def act_v(act, s, c, gemm, kk=0, i=0):
            if isinstance(s, int) and s == 0:
                act.wait_ge(sem("pads"), 1)
            else:
                act.wait_ge(sem("values"), s)
            if gemm == "mla":
                act.wait_ge(sem("w_used"), num(c + 1, i, kk) + 1)
            else:
                act.wait_ge(sem("v_transposed"), s - PAIRS + 1)
            act.wait_ge(sem("k_split"), s + 1)
            for src, dst in v_pieces(HI, gemm):
                ins = act.copy(dst, src)
            ins.then_inc(sem("v_hi"), 1)

        def act_step(act, s, attn, gemm, par, c, kk=0, i=0, nxt=None):
            pr = s - 1
            for b in range(8):
                if attn:
                    act_exp(act, pr, b, attn == "fox")
                if gemm == "mla":
                    if b == 0:
                        w_hi(act, c + 1, i, kk, "qkv")
                    elif b == 2:
                        act_z(act, s, 0, c, kk, i)
                        w_hi(act, c + 2, i, kk, "full")
                elif gemm == "gates":
                    if b in (0, 5):
                        w_hi(act, MIX + (1 if b == 0 else 2))
                elif gemm == "fox":
                    if b in (0, 3):
                        w_hi(act, c + (1 if b == 0 else 2), i, kk, "full")
                    elif b == 6:
                        w_hi(act, nxt, i, kk, "full")
                if attn and b:
                    act_p(act, pr, b - 1)
                if gemm in ("mla", "fox") and b == (2 if gemm == "mla" else 5):
                    act_k(act, s, c, gemm, par, kk, i)
                if gemm == "mla" and b in (5, 6):
                    act_q_mla(act, s, 6 - b, par)
                elif gemm == "fox" and b == 3:
                    act_q_fox(act, s, c, par, kk, i)
            if gemm == "fox":
                act_v_copy(act, s, c, kk, i)
            if attn:
                act_p(act, pr, 7)
                act.wait_ge(sem("pm_transposed"), pr + 1)
                act.copy(p_m[0:48, HI, :], bank(B_S, rows=slice(0, 48))).then_inc(sem("pm_hi"), 1)
            if gemm == "gates":
                w_hi(act, MIX + 3)
            if gemm == "mla":
                if par:
                    act.wait_ge(sem("z_read"), 2 * s + 1)
                w_hi(act, nxt, i, kk, "full")
                act_z(act, s + PAIRS, 2, c + 2, kk, i)
                if par:
                    act_silu(act, s - 1, 2)
            if isinstance(s, int) and s == PAIRS:
                act.wait_ge(sem("z_read"), 2 * PAIRS)
                act_silu(act, PAIRS, PAIRS)
            if gemm in ("mla", "fox"):
                act_v(act, s, c, gemm, kk, i)

        def dve_max(dve, pr, b, fox):
            dve.wait_ge(sem("scores"), 8 * pr + b + 1)
            dve.reduce_max(mx[:, b:b + 1], ps[:, s_cols(b)], AX.X).then_inc(sem("maxed"), 1)
            dve.wait_ge(sem("maxed"), 8 * pr + b + 1)
            dve.tensor_scalar(neg[:, b:b + 1], mx[:, b:b + 1], -(FOX_SCALE if fox else MLA_SCALE), None, ALU.mult) \
                .then_inc(sem("neg"), 1)

        def dve_norm(dve, pr, b):
            hh, i = divmod(b, NQ)
            dve.wait_ge(sem("exped"), 8 * pr + b + 1)
            dve.reciprocal(ri[:, b:b + 1], rs[:, b:b + 1]).then_inc(sem("recip"), 1)
            dve.wait_ge(sem("recip"), 8 * pr + b + 1)
            if b == 0:
                dve.wait_ge(sem("pads"), 2)
                if not (isinstance(pr, int) and pr == 0):
                    dve.wait_ge(sem("pm_transposed"), pr)
            real = prob[:, b % 2, 512 - n_real(b):512]
            dve.tensor_scalar(prob_m[:, i, 32 * hh:32 * hh + META], prob[:, b % 2, 512:LEN], ri[:, b:b + 1], None,
                              ALU.mult)
            dve.tensor_scalar(real, real, ri[:, b:b + 1], None, ALU.mult).then_inc(sem("normed"), 1)

        def dve_p(dve, pr, b):
            dve.wait_ge(sem("p_hi"), 8 * pr + b + 1)
            src, hi, lo = p_views(b)
            dve.tensor_tensor(lo, src, hi, ALU.subtract).then_inc(sem("p_split"), 1)

        def dve_rotate(dve, s, hh):
            dve.wait_ge(sem("q1_done" if hh else "q_done"), s + 1)
            if isinstance(s, int) and s == 0:
                dve.wait_ge(sem("vec"), 1)
            else:
                dve.wait_ge(sem("q_split"), s)
            dve.tensor_tensor(rot[64:96, hh, :], bank(hh, rows=slice(64, 96)), rope_s[64:96, 0, META:LEN], ALU.mult)
            dve.tensor_tensor(rt[64:96, hh, :], bank(hh, rows=slice(96, 128)), rope_s[64:96, 1, META:LEN],
                              ALU.mult).then_inc(sem("rotating"), 1)

        def pool_rotate(pool, s):
            for n, hh in enumerate((1, 0)):
                if n == 0 and isinstance(s, int) and s == 0:
                    pool.wait_ge(sem("pads"), 2)
                else:
                    pool.wait_ge(sem("rotated"), 2 * s + n)
                pool.wait_ge(sem("rotating"), 2 * s + n + 1)
                pool.tensor_tensor(rot[64:96, hh, :], rot[64:96, hh, :], rt[64:96, hh, :], ALU.add) \
                    .then_inc(sem("rotated"), 1)

        def dve_q(dve, s, gemm, par, heads=(0, 1)):
            head_1 = heads == (1,)
            dve.wait_ge(sem("q1_hi" if head_1 else "q_hi"), s + 1)
            for src, dst, cols in q_pieces(gemm, par, heads):
                ins = dve.tensor_tensor(dst[:, LO, cols], src, dst[:, HI, cols], ALU.subtract)
            ins.then_inc(sem("q1_split" if head_1 else "q_split"), 1)

        def dve_k(dve, s, gemm, par):
            dve.wait_ge(sem("k_hi"), s + 1)
            for src, dst, cols in k_pieces(gemm, par):
                ins = dve.tensor_tensor(dst[:, LO, cols], src, dst[:, HI, cols], ALU.subtract)
            ins.then_inc(sem("k_split"), 1)

        def dve_v(dve, s, gemm):
            dve.wait_ge(sem("v_hi"), s + 1)
            for (src, dst), (_, hi) in zip(v_pieces(LO, gemm), v_pieces(HI, gemm)):
                ins = dve.tensor_tensor(dst, src, hi, ALU.subtract)
            ins.then_inc(sem("v_split"), 1)

        def dve_gate(dve, pr, silus=PAIRS // 2 + 1):
            dve.wait_ge(sem("values"), pr + 1)
            dve.wait_ge(sem("z_silu"), silus)
            z = big[:, idx(pr), :]
            o = bank(B_O) if isinstance(pr, int) else bank(B_O).rearrange("p (a n) -> p a n", a=1)
            dve.tensor_tensor(z, o, z, ALU.mult).then_inc(sem("gated"), 1)

        def dve_step(dve, s, attn, gemm, par, c, kk=0, i=0, nxt=None):
            pr = s - 1
            for b in range(8):
                if attn:
                    dve_max(dve, pr, b, attn == "fox")
                if attn and b == 0:
                    if not (isinstance(s, int) and s == 1):
                        if isinstance(s, int):
                            dve_gate(dve, s - 2, min((s - 2) // 2 + 1, PAIRS // 2 + 1))
                        else:
                            dve_gate(dve, s - 2, i if attn == "mla" else PAIRS // 2 + 1)
                    dve_v(dve, s - 1, attn)
                if gemm == "mla":
                    if b == 3:
                        dve_k(dve, s, gemm, par)
                    elif b in (4, 5):
                        dve_rotate(dve, s, 5 - b)
                    elif b >= 6:
                        dve_q(dve, s, gemm, par, (7 - b,))
                elif gemm == "fox":
                    if b == 4:
                        dve_q(dve, s, gemm, par)
                    elif b == 6:
                        dve_k(dve, s, gemm, par)
                if attn:
                    dve_norm(dve, pr, b)
                if gemm == "mla":
                    if b == 0:
                        w_lo(dve, c + 1, i, kk, "qkv")
                    elif b == 2:
                        w_lo(dve, c + 2, i, kk, "full")
                elif gemm == "gates":
                    if b in (0, 5):
                        w_lo(dve, MIX + (1 if b == 0 else 2))
                elif gemm == "fox":
                    if b in (0, 3):
                        w_lo(dve, c + (1 if b == 0 else 2), i, kk, "full")
                    elif b == 6:
                        w_lo(dve, nxt, i, kk, "full")
                if attn and b:
                    dve_p(dve, pr, b - 1)
            if attn:
                dve_p(dve, pr, 7)
                dve.wait_ge(sem("pm_hi"), pr + 1)
                dve.tensor_tensor(p_m[0:48, LO, :], bank(B_S, rows=slice(0, 48)), p_m[0:48, HI, :], ALU.subtract) \
                    .then_inc(sem("pm_split"), 1)
            if gemm == "mla":
                w_lo(dve, nxt, i, kk, "full")
            elif gemm == "gates":
                w_lo(dve, MIX + 3)
                dve_gate(dve, pr)

        def pool_rows(pool, g, par):
            pool.wait_ge(sem("scores"), 8 * (g + PAIRS - 1))
            slots = slice(2 * par, 2 * par + 2)
            if isinstance(g, int):
                pool.wait_ge(sem("rotated"), 2 * PAIRS)
                for n, (dst, value) in enumerate(((q_t[64:96, slots], 0.0), (k_t[64:96, slots], 0.0),
                                                  (k_t[96:97, slots, HI, :], 1.0), (k_t[96:97, slots, LO, :], 0.0),
                                                  (q_t[64:65, slots, HI, :], -1.0))):
                    pool.memset(dst.bitcast(F32), value).then_inc(sem("aug"), 1)
                    pool.wait_ge(sem("aug"), 5 * g + n + 1)
                pool.wait_ge(sem("forget_out"), 16)
            h0 = 2 * g
            cum = forget_dram[bass.ds(h0, 2)]
            pool.dma_start(q_t[96:97, slots].bitcast(F32), cum[:, :, META:LEN].rearrange("(a h) j n -> a h j n", a=1)) \
                .then_inc(sem(f"rows{par}"), 16)
            pool.dma_start(k_t[64:65, slots].bitcast(F32),
                           cum.rearrange("(a h) j n -> a h j n", a=1)) \
                .then_inc(sem(f"rows{par}"), 16)

        def pool_attention(pool):
            pool_rotate(pool, 0)
            pool.wait_ge(sem("forget_lo"), 1)
            pool.dma_start(forget_dram, forget_r.bitcast(F32)).then_inc(sem("forget_out"), 16)
            with pool.Fori(1, PAIRS) as s:
                pool_rotate(pool, s)
            pool_rows(pool, 0, 0)
            pool_rows(pool, 1, 1)
            with pool.Fori(1, PAIRS // 2) as g:
                pool_rows(pool, 2 * g, 0)
                pool_rows(pool, 2 * g + 1, 1)

        def steps(eng, step):
            c0, c8 = FIRST[("attn", 0)], FIRST[("attn", PAIRS)]
            step(0, None, "mla", 0, c0, 0, 0, c0 + 3)
            step(1, "mla", "mla", 1, c0 + 3, 0, 0, c0 + 6)
            with eng.Fori(1, PAIRS // 2) as i:
                for par in range(2):
                    c = c0 + 3 * par
                    step(2 * i + par, "mla", "mla", par, c, 6, i, c + 3)
            step(PAIRS, "mla", "fox", 0, c8, 0, 0, c8 + 3)
            step(PAIRS + 1, "fox", "fox", 1, c8 + 3, 0, 0, c8 + 6)
            with eng.Fori(1, PAIRS // 2) as i:
                for par in range(2):
                    c = c8 + 3 * par
                    step(2 * i + (PAIRS + par), "fox", "fox", par, c, 6, i, c + 3)
            step(STEPS, "fox", "gates", 0, None, 0, PAIRS // 2)

        def load_attention(sp):
            def mla(s, c, kk, i):
                at_ = (s * P, s * 192, s * 256)
                if not isinstance(s, int):
                    at_ = tuple(sp.snap(x) for x in at_)
                w_load(sp, c, panel(w_in, W_ZM + at_[0]), i, kk)
                uq, ukv = a["w_uq"][0], a["w_ukv"][0]
                w_load(sp, c + 1, [
                    (lambda r: r[:, 0:384].rearrange("p (k n) -> p k n", k=2),
                     uq[:, bass.ds(at_[1], 192)].rearrange("(k p) n -> p k n", p=P)),
                    (lambda r: r[:, 384:640], ukv[:, bass.ds(at_[2], 256)])], i, kk)
                w_load(sp, c + 2, panel(w_in, W_ZF + at_[0]), i, kk)

            def fox(g, c, kk, i):
                at_ = g * P if isinstance(g, int) else sp.snap(g * P)
                for j, col in enumerate((W_FQ, W_FK, W_FV)):
                    w_load(sp, c + j, panel(w_in, col + at_), i, kk)

            c0, c8 = FIRST[("attn", 0)], FIRST[("attn", PAIRS)]
            for kind, c in ((mla, c0), (fox, c8)):
                kind(0, c, 0, 0)
                kind(1, c + 3, 0, 0)
                with sp.Fori(1, PAIRS // 2) as i:
                    kind(2 * i, c, 6, i)
                    kind(2 * i + 1, c + 3, 6, i)

        def load_mix(sp):
            def body(n, first, last):
                for j, (w, col) in enumerate(((w_in, W_GA), (w_in, W_GB), (a["w_br_mla"][0], 0),
                                              (a["w_br_fox"][0], 0))):
                    w_load(sp, MIX + j, panel(w, col + n * P), n, 4)
            loop(sp, KT, body)

        def pe_mix(pe):
            pe.wait_ge(sem("gated"), STEPS)

            def body(n, first, last):
                for j in range(2 if first else 0, 4):
                    c = MIX + j
                    w_ready(pe, c, n, 4)
                    if not first:
                        pe.wait_ge(sem("sig"), 2 * n - 1 + j) if j < 2 else pe.wait_ge(sem("branch"), 2 * n - 3 + j)
                    if j < 2:
                        moving = u_real
                    else:
                        moving = lambda k, part, j=j: o_r[:, 8 * (j - 2) + k, part, :]
                    ready = (lambda k: pe.wait_ge(sem("o_lo"), 8 * (j - 2) + k + 1)) if first else None
                    product(pe, bank(j), c, moving, ready=ready).then_inc(sem("w_used"), 1)
            loop(pe, KT, body)

        def act_mix(act):
            act.wait_ge(sem("gated"), STEPS)
            for t in range(16):
                act.copy(o_r[:, t, HI, :], big[:, t, :]).then_inc(sem("o_hi"), 1)

            def body(n, first, last):
                for j in range(2):
                    act.wait_ge(sem("w_used"), MIX + j + 1 + 4 * n)
                    if not first:
                        act.wait_ge(sem("branch"), 2 * n - 1 + j)
                    act.activation(sig[:, j, :], bank(j), ACT.Sigmoid).then_inc(sem("sig"), 1)
                    if not first:
                        w_hi(act, MIX + j + 2, n, 4, "full")
                if last:
                    for k in range(KT - 1):
                        act.wait_ge(sem("mixed"), k + 1)
                        act.copy(u[:, k, HI, META:LEN], h[:, k, :]).then_inc(sem("mr_hi"), 1)
                act.wait_ge(sem("w_used"), MIX + 3 + 4 * n)
                w_hi(act, MIX + 4, n, 4, "full")
                act.wait_ge(sem("w_used"), MIX + 4 + 4 * n)
                w_hi(act, MIX + 5, n, 4, "full")
                if last:
                    act.wait_ge(sem("mixed"), KT)
                    act.copy(u[:, KT - 1, HI, META:LEN], h[:, KT - 1, :]).then_inc(sem("mr_hi"), 1)
            loop(act, KT, body)

        def mixed_lo(dve, ks):
            for k in ks:
                dve.wait_ge(sem("mr_hi"), k + 1)
                dve.tensor_tensor(u[:, k, LO, META:LEN], h[:, k, :], u[:, k, HI, META:LEN], ALU.subtract) \
                    .then_inc(sem("mr_lo"), 1)

        def dve_mix(dve):
            for t in range(16):
                dve.wait_ge(sem("o_hi"), t + 1)
                dve.tensor_tensor(o_r[:, t, LO, :], big[:, t, :], o_r[:, t, HI, :], ALU.subtract) \
                    .then_inc(sem("o_lo"), 1)

            def body(n, first, last):
                for j in range(2):
                    dve.wait_ge(sem("sig"), 2 * n + j + 1)
                    if not first:
                        w_lo(dve, MIX + j + 2, n, 4, "full")
                for j in range(2):
                    if last:
                        mixed_lo(dve, range(4 * j, min(4 * j + 4, KT - 1)))
                    dve.wait_ge(sem("w_used"), MIX + j + 3 + 4 * n)
                    if not first:
                        dve.wait_ge(sem("mixed"), n)
                    dve.tensor_tensor(sig[:, 2 + j, :], bank(2 + j), sig[:, j, :], ALU.mult).then_inc(sem("branch"), 1)
                    w_lo(dve, MIX + 4 + j, n, 4, "full")
                dve.wait_ge(sem("branch"), 2 * n + 2)
                dst = h[:, idx(n), :]
                s2, s3 = (sig[:, 2 + j, :] if isinstance(n, int) else sig[:, 2 + j:3 + j, :] for j in range(2))
                dve.tensor_tensor(dst, s2, s3, ALU.add).then_inc(sem("mixed"), 1)
            loop(dve, KT, body)

        NORMS = ("out", "e", "eo", "down0", "oo", "down1")

        def tiles_before(tag):
            return KT * NORMS.index(tag)

        def hs_before(tag):
            return KT * (NORMS.index(tag) - 1)

        def norms_done(tag):
            return NORMS.index(tag) + 1

        def res_units(name):
            return 3 if name in (("down", 0), ("down", 1)) else 1

        def pe_residual(pe, name, moving, ready, tag, banks_read, order=range(KT)):
            c0, per = FIRST[name], res_units(name)
            for reader, count in banks_read:
                pe.wait_ge(sem(reader), count)

            def body(i, first, last):
                for j in range(2):
                    if not first:
                        pe.wait_ge(sem("h_tile"), hs_before(tag) + 2 * i + j - 1)
                    if per == 1:
                        w_ready(pe, c0 + j, i, 2)
                        product(pe, bank(j), c0 + j, moving, order, ready=ready if first and j == 0 else None) \
                            .then_inc(sem("w_used"), 1)
                    else:
                        k0 = 0
                        for m, ks in enumerate(DOWN):
                            c = c0 + 3 * j + m
                            w_ready(pe, c, i, 6)
                            product(pe, bank(j), c, moving, range(k0, k0 + ks), start=m == 0, stop=m == 2, n0=k0,
                                    ready=ready if first and j == 0 else None) \
                                .then_inc(sem("w_used"), 1)
                            k0 += ks
            loop(pe, KT // 2, body)

        def load_residual(sp, name, dram):
            c0 = FIRST[name]

            def body(i, first, last):
                for j in range(2):
                    if res_units(name) == 1:
                        w_load(sp, c0 + j, panel(dram, (2 * i + j) * P), i, 2)
                    else:
                        k0 = 0
                        for m, ks in enumerate(DOWN):
                            w_load(sp, c0 + 3 * j + m, panel(dram, (2 * i + j) * P, ks, k0), i, 6)
                            k0 += ks
            loop(sp, KT // 2, body)

        def act_residual(act, name, gain, tag):
            c0, per = FIRST[name], res_units(name)

            def body(i, first, last):
                for j in range(2):
                    for m in range(per):
                        c = c0 + per * j + m
                        act.wait_ge(sem("w_used"), num(c, i, 2 * per) + 1)
                        if c + 2 - c0 >= 2 * per and last:
                            w_hi(act, c + 2 + i * 2 * per)
                        else:
                            w_hi(act, c + 2, i, 2 * per, KINDS[c + 2])
                    n = 2 * i + j
                    act.wait_ge(sem("h_tile"), hs_before(tag) + n + 1)
                    if not first:
                        act.wait_ge(sem("acc_done"), tiles_before(tag) + n - 1)
                    if gain:
                        hn = h[:, idx(n), :]
                        dst = u[:, n, HI, META:LEN] if isinstance(n, int) else u[:, bass.ds(n, 1), HI, META:LEN]
                        act.activation(dst, hn, ACT.Copy, scale=vcol(*gain_at(gain, n))).then_inc(sem("hs_hi"), 1)
                    sqj = sq[:, j, :] if isinstance(n, int) else sq[:, j:j + 1, :]
                    act.activation(sqj, h[:, idx(n), :], ACT.Square).then_inc(sem("squared"), 1)
            loop(act, KT // 2, body)

        def gain_at(gain, n):
            return (gain[0], gain[1] + n)

        def dve_residual(dve, name, gain, tag):
            c0, per = FIRST[name], res_units(name)

            def body(i, first, last):
                for j in range(2):
                    for m in range(per):
                        c = c0 + per * j + m
                        if c + 2 - c0 >= 2 * per and last:
                            w_lo(dve, c + 2 + i * 2 * per)
                        else:
                            w_lo(dve, c + 2, i, 2 * per, KINDS[c + 2])
                    n = 2 * i + j
                    dve.wait_ge(sem("w_used"), num(c0 + per * j + per - 1, i, 2 * per) + 1)
                    hn = h[:, idx(n), :]
                    b = bank(j) if isinstance(n, int) else bank(j).rearrange("p (a n) -> p a n", a=1)
                    dve.tensor_tensor(hn, b, hn, ALU.add).then_inc(sem("h_tile"), 1)
                    if gain:
                        dve.wait_ge(sem("hs_hi"), hs_before(tag) + n + 1)
                        dst, hi = (u[:, idx(n), part, META:LEN] for part in (LO, HI))
                        dve.scalar_tensor_tensor(out=dst, in0=hn, scalar=vcol(*gain_at(gain, n)), in1=hi,
                                                 op0=ALU.mult, op1=ALU.subtract).then_inc(sem("hs"), 1)
            loop(dve, KT // 2, body)

        def pool_squares(pool, tag):
            for n in range(KT):
                pool.wait_ge(sem("squared"), tiles_before(tag) + n + 1)
                if n == 0:
                    ins = pool.tensor_copy(acc[:, 0, :], sq[:, 0, :])
                else:
                    pool.wait_ge(sem("acc_done"), tiles_before(tag) + n)
                    ins = pool.tensor_tensor(acc[:, 0, :], acc[:, 0, :], sq[:, n % 2, :], ALU.add)
                ins.then_inc(sem("acc_done"), 1)

        def pe_stats(pe, tag, bc=True, tok=False):
            pe.wait_ge(sem("acc_done"), tiles_before(tag) + KT)
            if bc:
                ins = pe.matmul(bank(7), ones[:], acc[:, 0, :], start=True, stop=True)
            if tok:
                for t in range(NQ):
                    ins = pe.matmul(bank(6, t, t + 1), acc[:, 0, t * P:(t + 1) * P], ones[:, 0:1],
                                    start=True, stop=True)
            ins.then_inc(sem("summed"), 1)

        def act_stats(act, tag, bc=True, tok=False):
            act.wait_ge(sem("summed"), norms_done(tag))
            if tok:
                act.activation(sstok, bank(6, 0, NQ), ACT.Sqrt, scale=1.0 / D, bias=EPS).then_inc(sem("rms_tok"), 1)
            if bc:
                act.activation(rbc[:, 0, :], bank(7), ACT.Sqrt, scale=1.0 / D, bias=EPS).then_inc(sem("rms"), 1)

        def dve_stats(dve, tag, bc=True, tok=False):
            if tok:
                dve.wait_ge(sem("rms_tok"), 1 if tag == "down0" else 2)
                dve.reciprocal(rtok, sstok).then_inc(sem("rtok"), 1)
            if bc:
                dve.wait_ge(sem("rms"), norms_done(tag))
                dve.reciprocal(rbc[:, 0, :], rbc[:, 0, :]).then_inc(sem("rbc"), 1)
                dve.wait_ge(sem("rbc"), norms_done(tag))

        OUT = FIRST["out"]

        def load_out(sp):
            for n in range(KT):
                w_load(sp, OUT + n, panel(a["w_out"][0], n * P))
                if n % 2 == 1:
                    t = n // 2
                    if t == 0:
                        sp.wait_ge(sem("mixed"), KT)
                    if t >= 2:
                        sp.wait_ge(sem("x_again"), 2 * t - 2)
                    sp.dma_start(xin[:, t % 2, :], a["x"][0, t * P:(t + 1) * P, :]).then_inc(sem(f"x2_in{t % 2}"), 16)

        def pe_out(pe):
            for n in range(KT):
                w_ready(pe, OUT + n)
                if n >= 4:
                    pe.wait_ge(sem("m2"), n - 3)
                product(pe, bank(n % 4), OUT + n, u_real,
                        ready=(lambda k: pe.wait_ge(sem("mr_lo"), k + 1)) if n == 0 else None) \
                    .then_inc(sem("w_used"), 1)
                t, half = divmod(n, 2)
                if half == 0:
                    pe.wait_ge(sem(f"x2_in{t % 2}"), 16 * (t // 2 + 1))
                if n >= 2:
                    pe.wait_ge(sem("h_x"), n - 1)
                for k in range(4):
                    ins = pe.transpose(bank(4 + half, k * P, (k + 1) * P),
                                       xin[:, t % 2, (4 * half + k) * P:(4 * half + k + 1) * P], ident)
                ins.then_inc(sem("x_again"), 1)
            pe.wait_ge(sem("acc_done"), KT)
            for t in range(NQ):
                ins = pe.matmul(bank(6, t, t + 1), acc[:, 0, t * P:(t + 1) * P], ones[:, 0:1], start=True, stop=True)
            ins.then_inc(sem("summed"), 1)
            pe.wait_ge(sem("out_diag"), 1)
            pe.matmul(bank(7), ones[:], sq[:, 0, :], start=True, stop=True).then_inc(sem("out_rbc"), 1)

        def act_out(act):
            for n in range(KT):
                act.wait_ge(sem("m2"), n + 1)
                if n < KT - 1:
                    w_hi(act, OUT + n + 2)
                if n >= 2:
                    act.wait_ge(sem("acc_done"), n - 1)
                act.activation(sq[:, n % 2, :], m2[:, n, :], ACT.Square).then_inc(sem("squared"), 1)
                if n == KT - 1:
                    w_hi(act, OUT + n + 2)
                act.wait_ge(sem("x_again"), n + 1)
                t, half = divmod(n, 2)
                act.copy(h[:, 4 * half:4 * half + 4, t * P:(t + 1) * P],
                         bank(4 + half).rearrange("p (k n) -> p k n", k=4)).then_inc(sem("h_x"), 1)
            act.wait_ge(sem("summed"), 1)
            act.activation(sstok, bank(6, 0, NQ), ACT.Sqrt, scale=1.0 / D, bias=EPS).then_inc(sem("rms"), 1)
            for n in range(KT):
                act.wait_ge(sem("h_tile"), n + 1)
                act.activation(u[:, n, HI, META:LEN], h[:, n, :], ACT.Copy, scale=vcol("mix_g", n)) \
                    .then_inc(sem("hs_hi"), 1)
                if n >= 2:
                    act.wait_ge(sem("acc_done"), KT + n - 1)
                act.activation(sq[:, n % 2, :], h[:, n, :], ACT.Square).then_inc(sem("squared"), 1)

        def dve_out(dve):
            mixed_lo(dve, (KT - 1,))
            for n in range(KT):
                dve.wait_ge(sem("w_used"), OUT + n + 1)
                dve.tensor_copy(m2[:, n, :], bank(n % 4)).then_inc(sem("m2"), 1)
                w_lo(dve, OUT + n + 2)
            dve.wait_ge(sem("rms"), 1)
            dve.reciprocal(rtok, sstok).then_inc(sem("rbc"), 1)
            dve.wait_ge(sem("rbc"), 1)
            dve.tensor_tensor(sq[:, 0, :].rearrange("p (t n) -> p t n", t=NQ),
                              ident.rearrange("p (a n) -> p a n", a=1).to_broadcast([P, NQ, P]),
                              rtok.rearrange("p (t a) -> p t a", a=1).to_broadcast([P, NQ, P]), ALU.mult) \
                .then_inc(sem("out_diag"), 1)
            dve.wait_ge(sem("out_rbc"), 1)
            dve.wait_ge(sem("h_x"), KT)

            def h_low(n):
                dve.wait_ge(sem("hs_hi"), n + 1)
                dve.scalar_tensor_tensor(out=u[:, n, LO, META:LEN], in0=h[:, n, :], scalar=vcol("mix_g", n),
                                         in1=u[:, n, HI, META:LEN], op0=ALU.mult, op1=ALU.subtract) \
                    .then_inc(sem("hs"), 1)

            for n in range(KT):
                if n >= 2:
                    dve.wait_ge(sem("h_tile"), n - 1)
                dve.tensor_tensor(res_t[:, n % 2, :], m2[:, n, :], bank(7), ALU.mult).then_inc(sem("res"), 1)
                dve.wait_ge(sem("res"), n + 1)
                dve.scalar_tensor_tensor(out=h[:, n, :], in0=res_t[:, n % 2, :], scalar=vcol("post_g", n),
                                         in1=h[:, n, :], op0=ALU.mult, op1=ALU.add).then_inc(sem("h_tile"), 1)
                if n:
                    h_low(n - 1)
            h_low(KT - 1)

        EZ, EC, POOL = FIRST["even_z"], FIRST["even_c"], FIRST["pool"]
        CH = 4 * P

        def conv_unit(g):
            return EC + 3 * g + (1 if g else 0)

        def load_even(sp):
            w = a["w_in_even_2"][0]
            for g in range(GROUPS):
                w_load(sp, EZ + g, panel(w, 3 * CH + g * P))
            wp = a["w_pool_2"][0]
            for g in range(GROUPS):
                for j, col in enumerate((CH, 2 * CH, 0)):
                    w_load(sp, conv_unit(g) + j, panel(w, col + g * P))
                if g == 0:
                    w_load(sp, POOL, [
                        (lambda r, lo=lo: r[:, lo * P:(lo + 2) * P].rearrange("p (g n) -> p g n", g=2),
                         wp[lo:lo + 2].rearrange("g p n -> p g n")) for lo in (0, 2)])

        def pe_even(pe):
            pe.wait_ge(sem("m2"), KT)
            w_ready(pe, EZ)
            w_ready(pe, EZ + 1)
            for k in range(KT):
                h_ready(pe, "e")(k)
                for g in range(2):
                    ins = product(pe, bank(g), EZ + g, u_real, (k,), start=k == 0, stop=k == KT - 1)
                    if k == KT - 1:
                        ins.then_inc(sem("w_used"), 1)
            pe_stats(pe, "e")
            for g in (2, 3):
                w_ready(pe, EZ + g)
                product(pe, bank(g), EZ + g, u_real).then_inc(sem("w_used"), 1)
            for g in range(GROUPS):
                for j in range(3):
                    w_ready(pe, conv_unit(g) + j)
                    if g == 0 and j == 2:
                        pe.wait_ge(sem("h_tile"), KT)
                    elif g:
                        pe.wait_ge(sem("e_read"), 3 * (g - 1) + j + 1)
                    product(pe, bank(4 + j), conv_unit(g) + j, u_real).then_inc(sem("w_used"), 1)
                if g == 0:
                    w_ready(pe, POOL)
                    for q in range(GROUPS):
                        pe.wait_ge(sem("pooled"), q + 1)
                        for n, (ws, ms) in enumerate(PASSES):
                            ins = pe.matmul(bank(q), w_tile(POOL, ws, q), pool_r[:, q, ms, :], start=n == 0,
                                            stop=n == 2)
                        ins.then_inc(sem("pool_mm" if q < GROUPS - 1 else "w_used"), 1)

        def act_even(act):
            units = iter(range(EZ + 2, EZ + 4 * GROUPS + 3))
            w_hi(act, next(units))
            w_hi(act, next(units))
            act_stats(act, "e")
            for g in range(GROUPS):
                if g:
                    w_hi(act, next(units))
                act.wait_ge(sem("e_p"), g + 1)
                act.copy(pool_r[:, g, HI, :], zpad[:, pooled_slot(g), 8:8 + SEQ]).then_inc(sem("e_phi"), 1)
            for g in range(GROUPS):
                c = conv_unit(g)
                w_hi(act, next(units))
                act.wait_ge(sem("e_read"), 3 * g + 2)
                act.activation(ecv[:, 0, :], cpad[:, 0, 0:SEQ], ACT.Copy, scale=vcol("conv_a", g)) \
                    .then_inc(sem("e_t0"), 1)
                w_hi(act, next(units))
                if g == 0:
                    for q in range(GROUPS):
                        if q < GROUPS - 1:
                            act.wait_ge(sem("pool_mm"), q + 1)
                        else:
                            act.wait_ge(sem("w_used"), POOL + 1)
                        act.activation(mix_r[:, GROUPS + q, HI, :], bank(q), ACT.Copy, scale=vcol("pool_scale", q)) \
                            .then_inc(sem("e_mhi"), 1)
                if g < GROUPS - 1:
                    w_hi(act, next(units))
                act.wait_ge(sem("e_y"), g + 1)
                act.copy(mix_r[:, g, HI, :], ecv[:, 0, :]).then_inc(sem("e_yhi"), 1)
                if g == 0:
                    w_hi(act, next(units))

        def pooled_slot(g):
            return 2 - g % 2

        def dve_even(dve):
            chain = [0]

            def link(ins):
                chain[0] += 1
                ins.then_inc(sem("e_chain"), 1)
                dve.wait_ge(sem("e_chain"), chain[0])

            dve.memset(cpad[:, 0, 0:2], 0.0)
            link(dve.memset(zpad[:, :, 0:8], 0.0))
            units = iter(range(EZ + 2, EZ + 4 * GROUPS + 3))
            w_lo(dve, next(units))
            w_lo(dve, next(units))
            dve_stats(dve, "e")
            r, r2 = rbc[:, 0, :], sq[:, 0, :]
            link(dve.tensor_tensor(r2, r, r, ALU.mult))
            z = zpad[:, 0, 8:8 + SEQ]
            for g in range(GROUPS):
                w = 2 ** (g + 1)
                if g:
                    w_lo(dve, next(units))
                dve.wait_ge(sem("w_used"), EZ + g + 1)
                link(dve.tensor_tensor(z, bank(g), r, ALU.mult))
                src = 0
                for e in range(g + 1):
                    dst, d = 1 + e % 2, 2 ** e
                    link(dve.tensor_tensor(zpad[:, dst, 8:8 + SEQ], zpad[:, src, 8:8 + SEQ],
                                           zpad[:, src, 8 - d:8 - d + SEQ], ALU.add))
                    src = dst
                dst = 3 - src
                total, pooled = zpad[:, src, 8:8 + SEQ], zpad[:, dst, 8:8 + SEQ]
                head = w - 1
                link(dve.tensor_tensor(total[:, 0:head], total[:, 0:head], inv_count[:, 0:head], ALU.mult))
                dve.tensor_tensor(pooled[:, 0:head], total[:, 0:head], z[:, 0:head], ALU.subtract)
                dve.scalar_tensor_tensor(out=pooled[:, head:SEQ], in0=total[:, head:SEQ], scalar=1.0 / w,
                                         in1=z[:, head:SEQ], op0=ALU.mult, op1=ALU.subtract).then_inc(sem("e_p"), 1)
                dve.wait_ge(sem("e_phi"), g + 1)
                dve.tensor_tensor(pool_r[:, g, LO, :], pooled, pool_r[:, g, HI, :], ALU.subtract) \
                    .then_inc(sem("pooled"), 1)
            for g in range(GROUPS):
                c = conv_unit(g)
                cv = cpad[:, 0, 2:2 + SEQ]
                w_lo(dve, next(units))
                dve.wait_ge(sem("w_used"), c + 1)
                if g:
                    dve.wait_ge(sem("e_t0"), g)
                dve.tensor_tensor(cv, bank(4), r2, ALU.mult).then_inc(sem("e_read"), 1)
                dve.wait_ge(sem("e_read"), 3 * g + 1)
                dve.wait_ge(sem("w_used"), c + 2)
                dve.tensor_tensor(cv, bank(5), cv, ALU.mult).then_inc(sem("e_read"), 1)
                w_lo(dve, next(units))
                dve.wait_ge(sem("e_t0"), g + 1)
                for tap in (1, 2):
                    link(dve.scalar_tensor_tensor(out=ecv[:, 0, :], in0=cpad[:, 0, tap:tap + SEQ],
                                                  scalar=vcol("conv_a", 4 * tap + g), in1=ecv[:, 0, :],
                                                  op0=ALU.mult, op1=ALU.add))
                if g == 0:
                    for q in range(GROUPS):
                        dve.wait_ge(sem("e_mhi"), q + 1)
                        dve.scalar_tensor_tensor(out=mix_r[:, GROUPS + q, LO, :], in0=bank(q),
                                                 scalar=vcol("pool_scale", q), in1=mix_r[:, GROUPS + q, HI, :],
                                                 op0=ALU.mult, op1=ALU.subtract).then_inc(sem("e_mix"), 1)
                if g < GROUPS - 1:
                    w_lo(dve, next(units))
                dve.wait_ge(sem("w_used"), c + 3)
                dve.tensor_tensor(ecv[:, 0, :], bank(6), ecv[:, 0, :], ALU.mult).then_inc(sem("e_read"), 1)
                dve.wait_ge(sem("e_read"), 3 * g + 3)
                dve.tensor_tensor(ecv[:, 0, :], ecv[:, 0, :], r, ALU.mult).then_inc(sem("e_y"), 1)
                dve.wait_ge(sem("e_yhi"), g + 1)
                dve.tensor_tensor(mix_r[:, g, LO, :], ecv[:, 0, :], mix_r[:, g, HI, :], ALU.subtract) \
                    .then_inc(sem("e_ylo"), 1)
                if g == 0:
                    w_lo(dve, next(units))

        def even_mix_ready(pe, k):
            pe.wait_ge(sem("e_ylo"), k + 1) if k < GROUPS else pe.wait_ge(sem("e_mix"), k - GROUPS + 1)

        def load_ffn(sp, layer):
            c0 = FIRST[("ffn", layer)]

            def body(i, first, last):
                for j in range(4):
                    w = a["w_ffn_gate_2" if j % 2 == 0 else "w_ffn_up_2"][layer]
                    w_load(sp, c0 + j, panel(w, (2 * i + j // 2) * P), i, 4)
            loop(sp, FT // 2, body)

        def pe_ffn(pe, layer, tag):
            c0 = FIRST[("ffn", layer)]
            def body(i, first, last):
                for j in range(4):
                    w_ready(pe, c0 + j, i, 4)
                    if first and j < 2:
                        pe.wait_ge(sem("h_tile"), hs_before(tag) + KT - 1 + j)
                    if not first:
                        f = 2 * i + j // 2
                        pe.wait_ge(sem("ffn_g_read" if j % 2 == 0 else "ffn_a_done"), FT * layer + f - 1)
                    product(pe, bank(j), c0 + j, u_real, ready=h_ready(pe, tag) if first and j == 0 else None) \
                        .then_inc(sem("w_used"), 1)
                    if first and j == 0:
                        pe_stats(pe, tag)
            loop(pe, FT // 2, body)

        def act_ffn(act, layer, tag):
            c0 = FIRST[("ffn", layer)]
            act_stats(act, tag)
            act.wait_ge(sem("ffn_gz"), layer + 1)

            def body(i, first, last):
                for j in range(2):
                    f = 2 * i + j
                    c = c0 + 2 * j
                    act.wait_ge(sem("w_used"), num(c, i, 4) + 1)
                    w_hi(act, c + 2 + i * 4) if last and j else w_hi(act, c + 2, i, 4, "full")
                    act.wait_ge(sem("ffn_g_read"), FT * layer + f + 1)
                    if not first:
                        act.wait_ge(sem("ffn_a_done"), FT * layer + f - 1)
                    act.activation(cnv[:, j, :], gpad[:, j, 0:SEQ], ACT.Copy, scale=ffn_vec(layer, 0, f)) \
                        .then_inc(sem("ffn_tap"), 1)
                    act.wait_ge(sem("ffn_conv"), 2 * FT * layer + 2 * f + 2)
                    act.activation(cnv[:, j, :], cnv[:, j, :], ACT.Silu, bias=ffn_vec(layer, 3, f)) \
                        .then_inc(sem("ffn_silu"), 1)
                    act.wait_ge(sem("w_used"), num(c + 1, i, 4) + 1)
                    w_hi(act, c + 3 + i * 4) if last and j else w_hi(act, c + 3, i, 4, "full")
                    act.wait_ge(sem("ffn_a_done"), FT * layer + f + 1)
                    dst = a_r[:, idx(f), HI, :]
                    act.copy(dst, hid[:, 0, :] if isinstance(f, int) else hid[:, 0:1, :]).then_inc(sem("ffn_a_hi"), 1)
            loop(act, FT // 2, body)

        def pool_ffn(pool, layer, tag):
            pool.wait_ge(sem("rbc"), norms_done(tag))

            def body(i, first, last):
                for j in range(2):
                    pool.wait_ge(sem("ffn_silu"), FT * layer + 2 * i + j + 1)
                    pool.tensor_tensor(cnv[:, j, :], cnv[:, j, :], rbc[:, 0, :], ALU.mult) \
                        .then_inc(sem("ffn_scaled"), 1)
            loop(pool, FT // 2, body)

        def dve_ffn(dve, layer, tag):
            c0 = FIRST[("ffn", layer)]
            dve_stats(dve, tag)
            dve.memset(gpad[:, :, 0:2], 0.0).then_inc(sem("ffn_gz"), 1)

            def body(i, first, last):
                for j in range(2):
                    f = 2 * i + j
                    c = c0 + 2 * j
                    dve.wait_ge(sem("w_used"), num(c, i, 4) + 1)
                    if not first:
                        dve.wait_ge(sem("ffn_conv"), 2 * FT * layer + 2 * f - 2)
                    dve.tensor_tensor(gpad[:, j, 2:2 + SEQ], bank(2 * j), rbc[:, 0, :], ALU.mult) \
                        .then_inc(sem("ffn_g_read"), 1)
                    w_lo(dve, c + 2 + i * 4) if last and j else w_lo(dve, c + 2, i, 4, "full")
                    dve.wait_ge(sem("ffn_tap"), FT * layer + f + 1)
                    for tap in (1, 2):
                        dve.scalar_tensor_tensor(out=cnv[:, j, :], in0=gpad[:, j, tap:tap + SEQ],
                                                 scalar=ffn_vec(layer, tap, f), in1=cnv[:, j, :],
                                                 op0=ALU.mult, op1=ALU.add).then_inc(sem("ffn_conv"), 1)
                        if tap == 1:
                            dve.wait_ge(sem("ffn_conv"), 2 * FT * layer + 2 * f + 1)
                    w_lo(dve, c + 3 + i * 4) if last and j else w_lo(dve, c + 3, i, 4, "full")
                    dve.wait_ge(sem("ffn_scaled"), FT * layer + f + 1)
                    dve.wait_ge(sem("w_used"), num(c + 1, i, 4) + 1)
                    if not (first and j == 0):
                        dve.wait_ge(sem("ffn_a_lo"), FT * layer + f)
                    dve.tensor_tensor(hid[:, 0, :], bank(2 * j + 1), cnv[:, j, :], ALU.mult) \
                        .then_inc(sem("ffn_a_done"), 1)
                    dve.wait_ge(sem("ffn_a_hi"), FT * layer + f + 1)
                    hi, lo = (a_r[:, idx(f), part, :] for part in (HI, LO))
                    hv = hid[:, 0, :] if isinstance(f, int) else hid[:, 0:1, :]
                    dve.tensor_tensor(lo, hv, hi, ALU.subtract).then_inc(sem("ffn_a_lo"), 1)
            loop(dve, FT // 2, body)

        OV, OU = FIRST["odd_v"], FIRST["odd_u"]

        def load_odd(sp):
            w = a["w_in_odd_2"][0]
            for m in range(KT):
                half, kp = divmod(m, KT // 2)
                w_load(sp, OV + m, [
                    (lambda r, j=j: r[:, j * SEQ:(j + 1) * SEQ],
                     w[(2 * kp + j) * P:(2 * kp + j + 1) * P, D + half * SEQ:D + (half + 1) * SEQ])
                    for j in range(2)])
                if m == 1:
                    sp.wait_ge(sem("h_tile"), hs_before("down0") + KT)
                    sp.dma_start(bbc[:, 0, :], a["b_spatial_2"].rearrange("a h t -> a (h t)").to_broadcast([P, D])) \
                        .then_inc(sem("b_in"), 16)
                    sp.dma_start(m2[:, 0:2, :].rearrange("p a (b s) -> p (a b) s", s=P),
                                 a["w_spatial_2"][0].rearrange("h t s -> t h s")).then_inc(sem("ws_in"), 16)
            for n in range(KT):
                w_load(sp, OU + n, panel(w, n * P))

        def pe_odd(pe):
            for m in range(KT):
                half, kp = divmod(m, KT // 2)
                w_ready(pe, OV + m)
                if half == 0:
                    pe.wait_ge(sem("hs"), hs_before("down0") + 2 * kp + 2)
                if m == KT // 2:
                    pe.wait_ge(sem("rms"), norms_done("down0"))
                    pe.wait_ge(sem("rms_tok"), 1)
                    pe.wait_ge(sem("wst"), 2)
                for t in (0, 2, 3, 1):
                    if m == 0:
                        pe.wait_ge(sem("h_tile"), hs_before("down0") + KT - 1 + (t == 1))
                    for j in range(2):
                        k = 2 * kp + j
                        for n, (us, ws) in enumerate(PASSES):
                            ins = pe.matmul(bank(4 * half + t), u[:, k, us, META + t * P:META + (t + 1) * P],
                                            wsp[:, (OV + m) % 2, ws, j * SEQ:(j + 1) * SEQ],
                                            start=k == 0 and n == 0, stop=k == KT - 1 and n == 2,
                                            skip_group_check=True)
                ins.then_inc(sem("w_used"), 1)
                if m == 0:
                    pe_stats(pe, "down0", bc=True, tok=True)
                    pe.wait_ge(sem("ws_in"), 16)
                    wn = m2[:, 0:2, :].rearrange("p a (b s) -> p (a b) s", s=P)
                    for hd in range(C_HEADS):
                        ins = pe.transpose(bank(4 + hd // 4, (hd % 4) * P, (hd % 4 + 1) * P), wn[:, hd, :], ident)
                    ins.then_inc(sem("ws_t"), 1)

            def u_product(n):
                w_ready(pe, OU + n)
                pe.wait_ge(sem("ov_read"), n + 1) if n < 4 else pe.wait_ge(sem("ou_read"), n - 3)
                product(pe, bank(n % 4), OU + n, u_real).then_inc(sem("w_used"), 1)

            def spatial(hd):
                if hd == 0:
                    pe.wait_ge(sem("vs_lo"), 2 * NQ)
                if hd >= 4:
                    pe.wait_ge(sem("gate"), hd - 3)
                for t in range(NQ):
                    if hd == 0:
                        pe.wait_ge(sem("ws_lo"), t + 1)
                    for m, (vs, ws) in enumerate(PASSES):
                        ins = pe.matmul(bank(4 + hd % 4, t * P, (t + 1) * P), vs_r[:, t, vs, hd * P:(hd + 1) * P],
                                        ws_r[t][:, ws, hd * P:(hd + 1) * P], start=m == 0, stop=m == 2)
                ins.then_inc(sem("sgu"), 1)

            for n in range(KT):
                u_product(n)
            for hd in range(C_HEADS):
                spatial(hd)

        V_CHUNKS = {4: (0,), 5: (1,), 6: (2,), 7: (3,), 8: (4, 5), 9: (6, 7)}

        def act_odd(act):
            act_stats(act, "down0", bc=True, tok=True)
            for m in range(2 * KT):
                act.wait_ge(sem("w_used"), OV + m + 1)
                w_hi(act, OV + m + 2)
                for n in V_CHUNKS.get(m, ()):
                    half, t = divmod(n, NQ)
                    v = odt[:, n % 2, :]
                    if n == 0:
                        act.wait_ge(sem("rtok"), 1)
                    if n >= 2:
                        act.wait_ge(sem("vs_lo"), n - 1)
                    act.activation(v, bank(4 * half + t), ACT.Gelu, scale=rtok[:, t:t + 1]).then_inc(sem("ov_read"), 1)
                    act.wait_ge(sem("ov_read"), n + 1)
                    act.copy(vs_r[:, t, HI, half * SEQ:(half + 1) * SEQ], v).then_inc(sem("vs_hi"), 1)
                    if n:
                        act.wait_ge(sem("sqv"), n)
                    act.activation(sq[:, 0, :], v, ACT.Square, accum_out=ssv_part[:, n:n + 1]).then_inc(sem("sqv"), 1)
                if m == 10:
                    act.wait_ge(sem("ssv"), 1)
                    act.activation(ssv, ssv, ACT.Sqrt, scale=1.0 / D, bias=EPS).then_inc(sem("sdv"), 1)
                if 11 <= m < 15:
                    t = m - 11
                    if t == 0:
                        act.wait_ge(sem("rsv"), 1)
                        act.wait_ge(sem("wst"), 2)
                    act.activation(ws_r[t][:, HI, :], wst[:, 0, :], ACT.Copy, scale=rsv[:, t:t + 1]) \
                        .then_inc(sem("ws_hi"), 1)
                if m >= KT:
                    n = m - KT
                    act.wait_ge(sem("ou_read"), n + 1)
                    act.activation(m2[:, n, :], m2[:, n, :], ACT.Gelu).then_inc(sem("ou"), 1)
            for hd in range(C_HEADS):
                act.wait_ge(sem("gate_y"), hd + 1)
                if hd == C_HEADS - 2:
                    act.wait_ge(sem("sgu"), C_HEADS)
                act.copy(mix_r[:, hd, HI, :], odt[:, hd % 2, :]).then_inc(sem("gate_hi"), 1)

        def dve_odd(dve):
            w_lo(dve, OV + 2)
            dve_stats(dve, "down0", bc=True, tok=True)
            dve.wait_ge(sem("ws_t"), 1)
            dve.wait_ge(sem("b_in"), 16)
            for half in range(2):
                dve.tensor_tensor(wst[:, 0, half * 512:(half + 1) * 512].rearrange("p (h n) -> p h n", h=4),
                                  bank(4 + half).rearrange("p (h n) -> p h n", h=4),
                                  triu.rearrange("p (a n) -> p a n", a=1).to_broadcast([P, 4, P]), ALU.mult) \
                    .then_inc(sem("wst"), 1)
            for m in range(1, 2 * KT):
                w_lo(dve, OV + m + 2)
                for n in V_CHUNKS.get(m, ()):
                    half, t = divmod(n, NQ)
                    hi, lo = (vs_r[:, t, part, half * SEQ:(half + 1) * SEQ] for part in (HI, LO))
                    dve.wait_ge(sem("vs_hi"), n + 1)
                    dve.tensor_tensor(lo, odt[:, n % 2, :], hi, ALU.subtract).then_inc(sem("vs_lo"), 1)
                if m == 10:
                    dve.wait_ge(sem("sqv"), 2 * NQ)
                    dve.tensor_tensor(ssv, ssv_part[:, 0:4], ssv_part[:, 4:8], ALU.add).then_inc(sem("ssv"), 1)
                    dve.wait_ge(sem("sdv"), 1)
                    dve.reciprocal(rsv, ssv).then_inc(sem("rsv"), 1)
                    dve.wait_ge(sem("rsv"), 1)
                if 11 <= m < 15:
                    t = m - 11
                    dve.wait_ge(sem("ws_hi"), t + 1)
                    dve.scalar_tensor_tensor(out=ws_r[t][:, LO, :], in0=wst[:, 0, :], scalar=rsv[:, t:t + 1],
                                             in1=ws_r[t][:, HI, :], op0=ALU.mult, op1=ALU.subtract) \
                        .then_inc(sem("ws_lo"), 1)
                if m >= KT:
                    n = m - KT
                    dve.wait_ge(sem("w_used"), OU + n + 1)
                    dve.tensor_tensor(m2[:, n, :], bank(n % 4), rbc[:, 0, :], ALU.mult).then_inc(sem("ou_read"), 1)
            for hd in range(C_HEADS):
                y = odt[:, hd % 2, :]
                dve.wait_ge(sem("sgu"), hd + 1)
                if hd >= 2:
                    dve.wait_ge(sem("gate_lo"), hd - 1)
                dve.scalar_tensor_tensor(out=y.rearrange("p (t n) -> p t n", t=NQ),
                                         in0=bank(4 + hd % 4).rearrange("p (t n) -> p t n", t=NQ),
                                         scalar=vcol("sgu_g", hd),
                                         in1=bbc[:, :, hd * P:(hd + 1) * P].to_broadcast([P, NQ, P]),
                                         op0=ALU.mult, op1=ALU.add).then_inc(sem("gate"), 1)
                dve.wait_ge(sem("gate"), hd + 1)
                dve.wait_ge(sem("ou"), hd + 1)
                dve.tensor_tensor(y, y, m2[:, hd, :], ALU.mult).then_inc(sem("gate_y"), 1)
                if hd:
                    dve_gate_lo(dve, hd - 1)
            dve_gate_lo(dve, C_HEADS - 1)

        def dve_gate_lo(dve, hd):
            dve.wait_ge(sem("gate_hi"), hd + 1)
            dve.tensor_tensor(mix_r[:, hd, LO, :], odt[:, hd % 2, :], mix_r[:, hd, HI, :], ALU.subtract) \
                .then_inc(sem("gate_lo"), 1)

        def h_ready(pe, tag):
            return lambda k: pe.wait_ge(sem("hs"), hs_before(tag) + k + 1)

        def load_final(sp):
            sp.wait_ge(sem("ffn_a_lo"), 2 * FT)
            sp.dma_start(gfin[:, 0, :], a["final_norm_2"].rearrange("(a n) -> a n", a=1).to_broadcast([P, D])) \
                .then_inc(sem("gf_in"), 16)
            for t in range(NQ):
                sp.wait_ge(sem("fin"), 2 * t + 2)
                sp.dma_start(out[t * P:(t + 1) * P, :], xin[:, t % 2, :]).then_inc(sem(f"stored{t % 2}"), 16)
            for s in range(2):
                sp.wait_ge(sem(f"stored{s}"), 32)

        def pe_final(pe):
            pe.wait_ge(sem("h_tile"), hs_before("down1") + KT)
            for t in range(NQ):
                for half in range(2):
                    n = 2 * t + half
                    if n >= 4:
                        pe.wait_ge(sem("fin_s"), n - 3)
                    for k in range(4):
                        ins = pe.transpose(bank(2 + n % 4, k * P, (k + 1) * P), h[:, 4 * half + k, t * P:(t + 1) * P],
                                           ident)
                    ins.then_inc(sem("fin_t"), 1)
                if t == 0:
                    pe_stats(pe, "down1", bc=False, tok=True)

        def act_final(act):
            act_stats(act, "down1", bc=False, tok=True)
            act.wait_ge(sem("rtok"), 2)
            for t in range(NQ):
                for half in range(2):
                    n = 2 * t + half
                    act.wait_ge(sem("fin_t"), n + 1)
                    if t >= 2:
                        act.wait_ge(sem(f"stored{t % 2}"), 16)
                    act.activation(xin[:, t % 2, half * 512:(half + 1) * 512], bank(2 + n % 4), ACT.Copy,
                                   scale=rtok[:, t:t + 1]).then_inc(sem("fin_s"), 1)

        def dve_final(dve):
            dve_stats(dve, "down1", bc=False, tok=True)
            dve.wait_ge(sem("gf_in"), 16)
            for n in range(2 * NQ):
                t, half = divmod(n, 2)
                dve.wait_ge(sem("fin_s"), n + 1)
                o = xin[:, t % 2, half * 512:(half + 1) * 512]
                dve.tensor_tensor(o, o, gfin[:, 0, half * 512:(half + 1) * 512], ALU.mult).then_inc(sem("fin"), 1)

        def a_tiles(k, part):
            return a_r[:, k, part, :]

        def mix_tiles(k, part):
            return mix_r[:, k, part, :]

        block = ctx.enter_context(nc.Block())

        @block.sync
        def _(sp):
            dma_prologue(sp)
            load_prologue(sp)
            load_attention(sp)
            load_mix(sp)
            load_out(sp)
            load_even(sp)
            load_residual(sp, "even_out", a["w_out_even_2"][0])
            load_ffn(sp, 0)
            load_residual(sp, ("down", 0), a["w_ffn_down_2"][0])
            load_odd(sp)
            load_residual(sp, "odd_out", a["w_out_odd_2"][0])
            load_ffn(sp, 1)
            load_residual(sp, ("down", 1), a["w_ffn_down_2"][1])
            load_final(sp)

        @block.gpsimd
        def _(pool):
            pool_prologue(pool)
            pool_attention(pool)
            pool_squares(pool, "out")
            pool_squares(pool, "e")
            pool_squares(pool, "eo")
            pool_ffn(pool, 0, "eo")
            pool_squares(pool, "down0")
            pool_squares(pool, "oo")
            pool_ffn(pool, 1, "oo")
            pool_squares(pool, "down1")

        @block.scalar
        def _(act):
            act_prologue(act)
            steps(act, lambda *x: act_step(act, *x))
            act_mix(act)
            act_out(act)
            act_even(act)
            act_residual(act, "even_out", ("ffn_g", 0), "eo")
            act_ffn(act, 0, "eo")
            act_residual(act, ("down", 0), ("mix_g", KT), "down0")
            act_odd(act)
            act_residual(act, "odd_out", ("ffn_g", KT), "oo")
            act_ffn(act, 1, "oo")
            act_residual(act, ("down", 1), None, "down1")
            act_final(act)

        @block.vector
        def _(dve):
            dve_prologue(dve)
            steps(dve, lambda *x: dve_step(dve, *x))
            dve_mix(dve)
            dve_out(dve)
            dve_even(dve)
            dve_residual(dve, "even_out", ("ffn_g", 0), "eo")
            dve_ffn(dve, 0, "eo")
            dve_residual(dve, ("down", 0), ("mix_g", KT), "down0")
            dve_odd(dve)
            dve_residual(dve, "odd_out", ("ffn_g", KT), "oo")
            dve_ffn(dve, 1, "oo")
            dve_residual(dve, ("down", 1), None, "down1")
            dve_final(dve)

        @block.tensor
        def _(pe):
            pe_prologue(pe)
            steps(pe, lambda *x: pe_step(pe, *x[:7]))
            pe_mix(pe)
            pe_out(pe)
            pe_even(pe)
            pe_residual(pe, "even_out", mix_tiles, lambda k: even_mix_ready(pe, k), "eo",
                        (("e_mix", GROUPS),), (4, 5, 6, 7, 0, 1, 2, 3))
            pe_ffn(pe, 0, "eo")
            pe_residual(pe, ("down", 0), a_tiles, lambda k: pe.wait_ge(sem("ffn_a_lo"), k + 1), "down0",
                        (("ffn_g_read", FT - 1), ("ffn_a_done", FT - 1)))
            pe_odd(pe)
            pe_residual(pe, "odd_out", mix_tiles, lambda k: pe.wait_ge(sem("gate_lo"), k + 1), "oo",
                        (("ou_read", KT),))
            pe_ffn(pe, 1, "oo")
            pe_residual(pe, ("down", 1), a_tiles, lambda k: pe.wait_ge(sem("ffn_a_lo"), FT + k + 1), "down1",
                        (("ffn_g_read", 2 * FT - 1), ("ffn_a_done", 2 * FT - 1)))
            pe_final(pe)


def rope_tables():
    half = ROPE // 2
    freq = (np.float32(ROPE_THETA) ** (-np.arange(half, dtype=np.float32) / np.float32(half))).astype(np.float32)
    ang = np.arange(LEN, dtype=np.float32)[None, :] * freq[:, None]
    cos, sin = np.cos(ang).astype(np.float32), np.sin(ang).astype(np.float32)
    return np.concatenate([cos, cos, -sin, sin], axis=0)


def constant_tables():
    i = np.arange(P)
    ident = np.eye(P, dtype=np.float32)
    mask = np.where(i[None, :] > i[:, None], np.float32(MASKED), np.float32(0.0)).astype(np.float32)
    triu = (i[:, None] <= i[None, :]).astype(np.float32)
    counts = np.broadcast_to((np.float32(1.0) / (np.arange(16, dtype=np.float32) + 1)), (P, 16))
    return np.ascontiguousarray(np.concatenate([ident, mask, triu, counts], axis=1))


_INS = ["x", "meta_tokens", "pre_norm_g", "w_in", "fox_forget_b", "mla_q_norm_g", "mla_kv_norm_g", "w_uq",
        "w_ukv", "w_br_mla", "w_br_fox", "w_out", "post_norm_g", "norm_mix_2", "norm_ffn_2", "final_norm_2",
        "w_in_even_2", "conv_a_2", "w_pool_2", "pool_scale_2", "w_out_even_2", "w_in_odd_2", "sgu_norm_2",
        "w_spatial_2", "b_spatial_2", "w_out_odd_2", "w_ffn_gate_2", "w_ffn_up_2", "conv_ffn_2",
        "b_conv_ffn_2", "w_ffn_down_2"]


def kernel(**inputs):
    import concourse.bacc as _bacc
    from concourse.bass_utils import run_bass_kernel_spmd as _run

    nc = _bacc.Bacc("TRN2", target_bir_lowering=False, num_devices=1)
    arrays, aps = {}, {}

    def declare(name, array):
        arrays[f"in_{name}_dram"] = array
        return nc.dram_tensor(f"in_{name}_dram", array.shape, mybir.dt.from_np(array.dtype),
                              kind="ExternalInput").ap()

    for name in _INS:
        aps[name] = declare(name, np.ascontiguousarray(inputs[name]))
    rope = declare("rope_tables", rope_tables())
    consts = declare("constants", constant_tables())
    out = nc.dram_tensor("out_dram", (1, SEQ, D), F32, kind="ExternalOutput").ap()
    hybrid_blocks_kernel(nc, aps, rope, consts, out[0])
    r = _run(nc, [arrays], core_ids=[0])
    return r.results[0]["out_dram"]
```
